# Optimizing a Trainium2 kernel written in Bass

```python
import math
import jax
import jax.numpy as jnp
from jax import lax
import numpy as np
import jax, jax.numpy as jnp

D_MODEL = 1024
BATCH = 1
SEQ = 256
DEPTH = 2

GRID_W = 64
CTX_LEN = 256
N_MIXERS = 4
QBLOCK = 128
ROPE_BASE = 10000.0
LN_EPS = 1e-5
RMS_EPS = 1e-6
NEG_INF = -1e30
DEEPNORM_ALPHA = (2.0 * DEPTH) ** 0.25
DEEPNORM_BETA = (8.0 * DEPTH) ** -0.25

MLA_HEADS = 16
MLA_NOPE_DIM = 64
MLA_ROPE_DIM = 32
MLA_V_DIM = 64
MLA_Q_LORA = 384
MLA_KV_LORA = 256

NA_HEADS = 16
NA_HEAD_DIM = 64
NA_ROWS = 8
NA_COLS = 16
NA_QCOLS = 16
NA_KCOLS = 32

DIFF_HEADS = 8
DIFF_HEAD_DIM = 64

SWA_HEADS = 16
SWA_KV_HEADS = 4
SWA_HEAD_DIM = 64
SWA_WINDOW = 128

FFN_HIDDEN = 2816
FFN_CONV = 3


def layer_norm(x, g, b):
    xf = x.astype(jnp.float32)
    mu = jnp.mean(xf, -1, keepdims=True)
    var = jnp.mean(jnp.square(xf - mu), -1, keepdims=True)
    return ((xf - mu) * lax.rsqrt(var + LN_EPS)).astype(x.dtype) * g + b

def rms_norm(x, g):
    xf = x.astype(jnp.float32)
    return (xf * lax.rsqrt(jnp.mean(jnp.square(xf), -1, keepdims=True) + RMS_EPS)).astype(x.dtype) * g

def softmax_f32(s):
    return jax.nn.softmax(s.astype(jnp.float32), axis=-1)

def modulate(t, shift, scale):
    return t * (1.0 + scale) + shift

def axial_rope(n_tokens, rot_dim):
    t = jnp.arange(n_tokens)
    row = (t // GRID_W).astype(jnp.float32)
    col = (t % GRID_W).astype(jnp.float32)
    n_freq = rot_dim // 4
    inv_freq = ROPE_BASE ** (-jnp.arange(n_freq, dtype=jnp.float32) / n_freq)
    ang = jnp.concatenate([row[:, None] * inv_freq, col[:, None] * inv_freq], -1)
    return jnp.cos(ang), jnp.sin(ang)

def apply_rope(x, cos, sin):
    half = x.shape[-1] // 2
    shp = (cos.shape[0],) + (1,) * (x.ndim - 3) + (half,)
    c = cos.reshape(shp).astype(x.dtype)
    s = sin.reshape(shp).astype(x.dtype)
    x1, x2 = x[..., :half], x[..., half:]
    return jnp.concatenate([x1 * c - x2 * s, x2 * c + x1 * s], -1)

def ctx_attention(q, k, v):
    s = jnp.einsum('bqhd,bkhd->bhqk', q, k).astype(jnp.float32) * q.shape[-1] ** -0.5
    p = softmax_f32(s).astype(v.dtype)
    return jnp.einsum('bhqk,bkhd->bqhd', p, v)

def dense_attention(q_lat, q_ctx, k_lat, v_lat, k_ctx, v_ctx):
    B, S, H, dk = q_lat.shape
    dv = v_lat.shape[-1]
    n_ctx = k_ctx.shape[1]
    scale = dk ** -0.5
    nb = S // QBLOCK

    def to_blocks(t):
        return t.reshape(B, nb, QBLOCK, H, dk).swapaxes(0, 1)

    def one_block(qs):
        ql, qc = qs
        s = jnp.concatenate([jnp.einsum('bqhd,bkhd->bhqk', qc, k_ctx),
                             jnp.einsum('bqhd,bkhd->bhqk', ql, k_lat)], -1)
        p = softmax_f32(s.astype(jnp.float32) * scale).astype(v_lat.dtype)
        return (jnp.einsum('bhqk,bkhd->bqhd', p[..., :n_ctx], v_ctx)
                + jnp.einsum('bhqk,bkhd->bqhd', p[..., n_ctx:], v_lat))

    out = lax.map(one_block, (to_blocks(q_lat), to_blocks(q_ctx)))
    return out.swapaxes(0, 1).reshape(B, S, H, dv)

def mla_mixer(h, hc, w_in, q_norm, kv_norm, w_qb, w_kvb, w_o, need_ctx):
    H, DN, DR, DV, QL = MLA_HEADS, MLA_NOPE_DIM, MLA_ROPE_DIM, MLA_V_DIM, MLA_Q_LORA

    def project_q(t):
        cq = rms_norm(t @ w_in[:, :QL], q_norm)
        return (cq @ w_qb).reshape(t.shape[0], t.shape[1], H, DN + DR)

    def project_kv(t):
        a = t @ w_in[:, QL:]
        ckv = rms_norm(a[..., :MLA_KV_LORA], kv_norm)
        kv = (ckv @ w_kvb).reshape(t.shape[0], t.shape[1], H, DN + DV)
        return kv[..., :DN], kv[..., DN:], a[..., MLA_KV_LORA:]

    def full_key(k_nope, k_pe):
        return jnp.concatenate([k_nope, jnp.broadcast_to(k_pe[:, :, None, :], k_nope.shape[:3] + (DR,))], -1)

    B, S, _ = h.shape
    cos, sin = axial_rope(S, DR)
    q = project_q(h)
    k_nope, v, k_pe = project_kv(h)
    q_rot = jnp.concatenate([q[..., :DN], apply_rope(q[..., DN:], cos, sin)], -1)
    k = full_key(k_nope, apply_rope(k_pe, cos, sin))
    kc_nope, vc, kc_pe = project_kv(hc)
    kc = full_key(kc_nope, kc_pe)
    o = dense_attention(q_rot, q, k, v, kc, vc)
    y = o.reshape(B, S, H * DV) @ w_o
    yc = None
    if need_ctx:
        oc = ctx_attention(project_q(hc), kc, vc)
        yc = oc.reshape(oc.shape[0], oc.shape[1], H * DV) @ w_o
    return y, yc

def neighbourhood_attention(q, k, v, kc, vc, rpb):
    B, S, H, d = q.shape
    n_rows = S // GRID_W
    kr = min(NA_ROWS, n_rows)
    n_ctx = kc.shape[1]
    scale = d ** -0.5
    n_cb = GRID_W // NA_QCOLS
    q_cols = np.arange(GRID_W).reshape(n_cb, NA_QCOLS)
    win_start = np.clip(q_cols - NA_COLS // 2, 0, GRID_W - NA_COLS)
    band_start = np.clip(np.arange(n_cb) * NA_QCOLS - NA_COLS // 2, 0, GRID_W - NA_KCOLS)
    band_cols = band_start[:, None] + np.arange(NA_KCOLS)
    col_valid = ((band_cols[:, None, :] >= win_start[..., None])
                 & (band_cols[:, None, :] < win_start[..., None] + NA_COLS))
    col_idx = np.clip(band_cols[:, None, :] - q_cols[..., None] + NA_COLS - 1, 0, 2 * NA_COLS - 2)
    qg = q.reshape(B, n_rows, GRID_W, H, d)
    kg = k.reshape(B, n_rows, GRID_W, H, d)
    vg = v.reshape(B, n_rows, GRID_W, H, d)

    def row_block(r):
        r0 = jnp.clip(r - kr // 2, 0, n_rows - kr)
        kb = lax.dynamic_slice_in_dim(kg, r0, kr, axis=1)[:, :, band_cols]
        vb = lax.dynamic_slice_in_dim(vg, r0, kr, axis=1)[:, :, band_cols]
        qr = lax.dynamic_index_in_dim(qg, r, axis=1, keepdims=False).reshape(B, n_cb, NA_QCOLS, H, d)
        s = jnp.einsum('bjqhd,bmjnhd->bhjqmn', qr, kb).astype(jnp.float32) * scale
        row_idx = r0 + jnp.arange(kr) - r + NA_ROWS - 1
        bias = rpb[:, row_idx][:, :, col_idx].transpose(0, 2, 3, 1, 4)
        s = jnp.where(col_valid[:, :, None, :], s + bias.astype(jnp.float32), NEG_INF)
        s_ctx = jnp.einsum('bjqhd,bkhd->bhjqk', qr, kc).astype(jnp.float32) * scale
        p = softmax_f32(jnp.concatenate(
            [s_ctx, s.reshape(B, H, n_cb, NA_QCOLS, kr * NA_KCOLS)], -1)).astype(v.dtype)
        p_lat = p[..., n_ctx:].reshape(B, H, n_cb, NA_QCOLS, kr, NA_KCOLS)
        o = (jnp.einsum('bhjqk,bkhd->bjqhd', p[..., :n_ctx], vc)
             + jnp.einsum('bhjqmn,bmjnhd->bjqhd', p_lat, vb))
        return o.reshape(B, GRID_W, H, d)

    out = lax.map(row_block, jnp.arange(n_rows))
    return out.swapaxes(0, 1).reshape(B, S, H, d)

def na_mixer(h, hc, w_qkv, rpb, w_o, need_ctx):
    H, d = NA_HEADS, NA_HEAD_DIM
    nq = H * d

    def project_q(t):
        return (t @ w_qkv[:, :nq]).reshape(t.shape[0], t.shape[1], H, d)

    def project_kv(t):
        a = (t @ w_qkv[:, nq:]).reshape(t.shape[0], t.shape[1], 2, H, d)
        return a[:, :, 0], a[:, :, 1]

    B, S, _ = h.shape
    q = project_q(h)
    k, v = project_kv(h)
    kc, vc = project_kv(hc)
    y = neighbourhood_attention(q, k, v, kc, vc, rpb).reshape(B, S, H * d) @ w_o
    yc = None
    if need_ctx:
        oc = ctx_attention(project_q(hc), kc, vc)
        yc = oc.reshape(oc.shape[0], oc.shape[1], H * d) @ w_o
    return y, yc

def diff_mixer(h, hc, w_qkv, lam, subln, w_o, layer_idx, need_ctx):
    H, d = DIFF_HEADS, DIFF_HEAD_DIM
    nq = 2 * H * d

    def project_q(t):
        return (t @ w_qkv[:, :nq]).reshape(t.shape[0], t.shape[1], H, 2, d)

    def project_kv(t):
        a = t @ w_qkv[:, nq:]
        return (a[..., :nq].reshape(t.shape[0], t.shape[1], H, 2, d),
                a[..., nq:].reshape(t.shape[0], t.shape[1], H, 2 * d))

    lambda_init = 0.8 - 0.6 * math.exp(-0.3 * layer_idx)
    lf = lam.astype(jnp.float32)
    lam_full = jnp.exp(jnp.sum(lf[0] * lf[1])) - jnp.exp(jnp.sum(lf[2] * lf[3])) + lambda_init

    def combine(o1, o2):
        o = o1 - lam_full.astype(o1.dtype) * o2
        o = rms_norm(o, subln) * (1.0 - lambda_init)
        return o.reshape(o.shape[0], o.shape[1], H * 2 * d) @ w_o

    B, S, _ = h.shape
    cos, sin = axial_rope(S, d)
    q = project_q(h)
    k, v = project_kv(h)
    q_rot, k_rot = apply_rope(q, cos, sin), apply_rope(k, cos, sin)
    kc, vc = project_kv(hc)
    o1 = dense_attention(q_rot[:, :, :, 0], q[:, :, :, 0], k_rot[:, :, :, 0], v, kc[:, :, :, 0], vc)
    o2 = dense_attention(q_rot[:, :, :, 1], q[:, :, :, 1], k_rot[:, :, :, 1], v, kc[:, :, :, 1], vc)
    y = combine(o1, o2)
    yc = None
    if need_ctx:
        qc = project_q(hc)
        yc = combine(ctx_attention(qc[:, :, :, 0], kc[:, :, :, 0], vc),
                     ctx_attention(qc[:, :, :, 1], kc[:, :, :, 1], vc))
    return y, yc

def windowed_sink_attention(q_lat, q_ctx, k_lat, v_lat, k_ctx, v_ctx, sinks):
    B, S, G, R, d = q_lat.shape
    n_ctx = k_ctx.shape[1]
    scale = d ** -0.5
    nb = S // QBLOCK
    band = QBLOCK + 2 * SWA_WINDOW
    pad = ((0, 0), (SWA_WINDOW, SWA_WINDOW), (0, 0), (0, 0))
    kp = jnp.pad(k_lat, pad)
    vp = jnp.pad(v_lat, pad)
    sink_logit = sinks.astype(jnp.float32).reshape(G, R)[None, :, :, None, None]

    def one_block(n):
        start = n * QBLOCK
        ql = lax.dynamic_slice_in_dim(q_lat, start, QBLOCK, axis=1)
        qc = lax.dynamic_slice_in_dim(q_ctx, start, QBLOCK, axis=1)
        kb = lax.dynamic_slice_in_dim(kp, start, band, axis=1)
        vb = lax.dynamic_slice_in_dim(vp, start, band, axis=1)
        qpos = start + jnp.arange(QBLOCK)
        kpos = start - SWA_WINDOW + jnp.arange(band)
        valid = ((jnp.abs(qpos[:, None] - kpos[None, :]) <= SWA_WINDOW)
                 & (kpos[None, :] >= 0) & (kpos[None, :] < S))
        s_lat = jnp.where(valid, jnp.einsum('bqgrd,bkgd->bgrqk', ql, kb).astype(jnp.float32) * scale, NEG_INF)
        s_ctx = jnp.einsum('bqgrd,bkgd->bgrqk', qc, k_ctx).astype(jnp.float32) * scale
        sink = jnp.broadcast_to(sink_logit, s_ctx.shape[:-1] + (1,))
        p = softmax_f32(jnp.concatenate([sink, s_ctx, s_lat], -1))[..., 1:].astype(v_lat.dtype)
        return (jnp.einsum('bgrqk,bkgd->bqgrd', p[..., :n_ctx], v_ctx)
                + jnp.einsum('bgrqk,bkgd->bqgrd', p[..., n_ctx:], vb))

    out = lax.map(one_block, jnp.arange(nb))
    return out.swapaxes(0, 1).reshape(B, S, G * R * d)

def ctx_sink_attention(q, k, v, sinks):
    B, L, G, R, d = q.shape
    s = jnp.einsum('bqgrd,bkgd->bgrqk', q, k).astype(jnp.float32) * d ** -0.5
    sink = jnp.broadcast_to(sinks.astype(jnp.float32).reshape(G, R)[None, :, :, None, None], s.shape[:-1] + (1,))
    p = softmax_f32(jnp.concatenate([sink, s], -1))[..., 1:].astype(v.dtype)
    return jnp.einsum('bgrqk,bkgd->bqgrd', p, v).reshape(B, L, G * R * d)

def swa_mixer(h, hc, w_qkv, sinks, w_o, need_ctx):
    H, G, d = SWA_HEADS, SWA_KV_HEADS, SWA_HEAD_DIM
    R = H // G
    nq = H * d

    def project_q(t):
        return (t @ w_qkv[:, :nq]).reshape(t.shape[0], t.shape[1], G, R, d)

    def project_kv(t):
        a = t @ w_qkv[:, nq:]
        return (a[..., :G * d].reshape(t.shape[0], t.shape[1], G, d),
                a[..., G * d:].reshape(t.shape[0], t.shape[1], G, d))

    B, S, _ = h.shape
    cos, sin = axial_rope(S, d)
    q = project_q(h)
    k, v = project_kv(h)
    kc, vc = project_kv(hc)
    o = windowed_sink_attention(apply_rope(q, cos, sin), q, apply_rope(k, cos, sin), v, kc, vc, sinks)
    y = o @ w_o
    yc = None
    if need_ctx:
        yc = ctx_sink_attention(project_q(hc), kc, vc, sinks) @ w_o
    return y, yc

def conv_ffn(h, w_in, conv_w, conv_b, w_out):
    u = h @ w_in
    u = lax.conv_general_dilated(
        u, conv_w[:, None, :].astype(u.dtype), window_strides=(1,),
        padding=[(FFN_CONV // 2, FFN_CONV // 2)],
        dimension_numbers=('NWC', 'WIO', 'NWC'),
        feature_group_count=u.shape[-1]) + conv_b
    a, g = jnp.split(u, 2, axis=-1)
    return (jax.nn.silu(g) * a) @ w_out

def first_inputs(seed: int = 0) -> dict:
    key = jax.random.key(seed)
    ks = iter(jax.random.split(key, 40))

    def nrm(shape, scale):
        return jax.random.normal(next(ks), shape, jnp.float32) * scale

    D, F = D_MODEL, FFN_HIDDEN
    beta = DEEPNORM_BETA
    n_a, n_b, n_c, n_d = [len(range(m, DEPTH, N_MIXERS)) for m in range(N_MIXERS)]
    mla_in = MLA_Q_LORA + MLA_KV_LORA + MLA_ROPE_DIM
    return {
        'x': nrm((BATCH, SEQ, D), 1.0),
        'c': nrm((BATCH, D), 1.0),
        'ctx': nrm((BATCH, CTX_LEN, D), 1.0),
        'c_ctx': nrm((D,), 1.0),
        'ada_w': nrm((DEPTH, D, 6 * D), 0.5 * D ** -0.5),
        'ada_b': nrm((DEPTH, 6 * D), 0.01),
        'ln1_g': 1.0 + nrm((DEPTH, D), 0.02),
        'ln1_b': nrm((DEPTH, D), 0.02),
        'ln2_g': 1.0 + nrm((DEPTH, D), 0.02),
        'ln2_b': nrm((DEPTH, D), 0.02),
        'ffn_w_in': nrm((DEPTH, D, 2 * F), D ** -0.5),
        'ffn_conv_w': nrm((DEPTH, FFN_CONV, 2 * F), FFN_CONV ** -0.5),
        'ffn_conv_b': nrm((DEPTH, 2 * F), 0.01),
        'ffn_w_out': nrm((DEPTH, F, D), beta * F ** -0.5),
        'mla_w_in': nrm((n_a, D, mla_in), D ** -0.5),
        'mla_q_norm': 1.0 + nrm((n_a, MLA_Q_LORA), 0.02),
        'mla_kv_norm': 1.0 + nrm((n_a, MLA_KV_LORA), 0.02),
        'mla_w_qb': nrm((n_a, MLA_Q_LORA, MLA_HEADS * (MLA_NOPE_DIM + MLA_ROPE_DIM)), MLA_Q_LORA ** -0.5),
        'mla_w_kvb': nrm((n_a, MLA_KV_LORA, MLA_HEADS * (MLA_NOPE_DIM + MLA_V_DIM)), MLA_KV_LORA ** -0.5),
        'mla_w_o': nrm((n_a, MLA_HEADS * MLA_V_DIM, D), beta * (MLA_HEADS * MLA_V_DIM) ** -0.5),
        'na_w_qkv': nrm((n_b, D, 3 * NA_HEADS * NA_HEAD_DIM), D ** -0.5),
        'na_rpb': nrm((n_b, NA_HEADS, 2 * NA_ROWS - 1, 2 * NA_COLS - 1), 0.1),
        'na_w_o': nrm((n_b, NA_HEADS * NA_HEAD_DIM, D), beta * (NA_HEADS * NA_HEAD_DIM) ** -0.5),
        'diff_w_qkv': nrm((n_c, D, 6 * DIFF_HEADS * DIFF_HEAD_DIM), D ** -0.5),
        'diff_lambda': nrm((n_c, 4, DIFF_HEAD_DIM), 0.1),
        'diff_subln': 1.0 + nrm((n_c, 2 * DIFF_HEAD_DIM), 0.02),
        'diff_w_o': nrm((n_c, DIFF_HEADS * 2 * DIFF_HEAD_DIM, D), beta * (DIFF_HEADS * 2 * DIFF_HEAD_DIM) ** -0.5),
        'swa_w_qkv': nrm((n_d, D, (SWA_HEADS + 2 * SWA_KV_HEADS) * SWA_HEAD_DIM), D ** -0.5),
        'swa_sinks': nrm((n_d, SWA_HEADS), 0.5),
        'swa_w_o': nrm((n_d, SWA_HEADS * SWA_HEAD_DIM, D), beta * (SWA_HEADS * SWA_HEAD_DIM) ** -0.5),
    }

def first_block(x, c, ctx, c_ctx, ada_w, ada_b, ln1_g, ln1_b, ln2_g, ln2_b,
              ffn_w_in, ffn_conv_w, ffn_conv_b, ffn_w_out,
              mla_w_in, mla_q_norm, mla_kv_norm, mla_w_qb, mla_w_kvb, mla_w_o,
              na_w_qkv, na_rpb, na_w_o,
              diff_w_qkv, diff_lambda, diff_subln, diff_w_o,
              swa_w_qkv, swa_sinks, swa_w_o):
    silu_c = jax.nn.silu(c)
    silu_cc = jax.nn.silu(c_ctx)
    h_lat, h_ctx = x, ctx
    for i in range(DEPTH):
        last = i == DEPTH - 1
        need_ctx = not last
        m = (silu_c @ ada_w[i] + ada_b[i])[:, None, :]
        sh1, sc1, g1, sh2, sc2, g2 = jnp.split(m, 6, axis=-1)
        mc = silu_cc @ ada_w[i] + ada_b[i]
        csh1, csc1, cg1, csh2, csc2, cg2 = jnp.split(mc, 6, axis=-1)
        a_lat = modulate(h_lat, sh1, sc1)
        a_ctx = modulate(h_ctx, csh1, csc1)
        kind, slot = i % N_MIXERS, i // N_MIXERS
        if kind == 0:
            y, yc = mla_mixer(a_lat, a_ctx, mla_w_in[slot], mla_q_norm[slot], mla_kv_norm[slot],
                              mla_w_qb[slot], mla_w_kvb[slot], mla_w_o[slot], need_ctx)
        elif kind == 1:
            y, yc = na_mixer(a_lat, a_ctx, na_w_qkv[slot], na_rpb[slot], na_w_o[slot], need_ctx)
        elif kind == 2:
            y, yc = diff_mixer(a_lat, a_ctx, diff_w_qkv[slot], diff_lambda[slot], diff_subln[slot],
                               diff_w_o[slot], i, need_ctx)
        else:
            y, yc = swa_mixer(a_lat, a_ctx, swa_w_qkv[slot], swa_sinks[slot], swa_w_o[slot], need_ctx)
        h_lat = layer_norm(DEEPNORM_ALPHA * h_lat + g1 * y, ln1_g[i], ln1_b[i])
        f = conv_ffn(modulate(h_lat, sh2, sc2), ffn_w_in[i], ffn_conv_w[i], ffn_conv_b[i], ffn_w_out[i])
        h_lat = layer_norm(DEEPNORM_ALPHA * h_lat + g2 * f, ln2_g[i], ln2_b[i])
        if need_ctx:
            h_ctx = layer_norm(DEEPNORM_ALPHA * h_ctx + cg1 * yc, ln1_g[i], ln1_b[i])
            fc = conv_ffn(modulate(h_ctx, csh2, csc2), ffn_w_in[i], ffn_conv_w[i], ffn_conv_b[i], ffn_w_out[i])
            h_ctx = layer_norm(DEEPNORM_ALPHA * h_ctx + cg2 * fc, ln2_g[i], ln2_b[i])
    return h_lat


DEPTH_2 = 1

NSA_HEADS = 8
NSA_KV_GROUPS = 2
NSA_HEAD_DIM = 64
NSA_HEADS_PER_GROUP = NSA_HEADS // NSA_KV_GROUPS
NSA_WIDTH = NSA_HEADS * NSA_HEAD_DIM
NSA_KV_WIDTH = NSA_KV_GROUPS * NSA_HEAD_DIM
CMP_LEN = 32
CMP_STRIDE = 16
SLC_LEN = 64
SLC_TOPN = 16
WINDOW = 512
Q_BLOCK = 128
ROPE_THETA = 500000.0
ROPE_DIM = NSA_HEAD_DIM // 4
HG_HEADS = 4
HG_KEY_DIM = 128
HG_VAL_DIM = 128
HG_WIDTH = HG_HEADS * HG_VAL_DIM
HG_CHUNK = 64
N_GROUPS = 4
EXPERTS_PER_GROUP = 8
N_EXPERTS = N_GROUPS * EXPERTS_PER_GROUP
TOP_K_IN_GROUP = 2
D_FF_EXPERT = 512
NEG_INF_2 = -1e30
FORCE_SCORE = 1e4

IN_SPLITS = [NSA_WIDTH, 6 * NSA_KV_WIDTH, 3 * NSA_HEADS,
             HG_HEADS * HG_KEY_DIM, HG_HEADS * HG_KEY_DIM, HG_WIDTH, HG_WIDTH, 2 * D_MODEL]
IN_COLS = sum(IN_SPLITS)


def rmsnorm(x, g):
    x32 = x.astype(jnp.float32)
    y = x32 * lax.rsqrt(jnp.mean(x32 * x32, axis=-1, keepdims=True) + RMS_EPS)
    return (y * g.astype(jnp.float32)).astype(x.dtype)

def partial_rope(t, pos):
    half = ROPE_DIM // 2
    inv_freq = ROPE_THETA ** (-jnp.arange(half, dtype=jnp.float32) / half)
    ang = pos.astype(jnp.float32)[:, None] * inv_freq[None, :]
    cos = jnp.cos(ang)[:, None, :]
    sin = jnp.sin(ang)[:, None, :]
    t1 = t[..., :half]
    t2 = t[..., half:ROPE_DIM]
    return jnp.concatenate([t1 * cos - t2 * sin, t2 * cos + t1 * sin, t[..., ROPE_DIM:]], axis=-1)

def masked_softmax(s, mask):
    s = jnp.where(mask, s, NEG_INF_2)
    return jax.nn.softmax(s, axis=-1) * mask

def nsa_mixer(q, k_cmp_in, v_cmp_in, k_slc, v_slc, k_win, v_win, gate_logits, w_cmp_k, w_cmp_v, cmp_pos):
    f32 = jnp.float32
    b, s = q.shape[0], q.shape[1]
    G, R, dk = NSA_KV_GROUPS, NSA_HEADS_PER_GROUP, NSA_HEAD_DIM
    pos = jnp.arange(s)
    scale = dk ** -0.5
    q = partial_rope(q.astype(f32), pos).reshape(b, s, G, R, dk)
    k_slc = partial_rope(k_slc.astype(f32), pos)
    k_win = partial_rope(k_win.astype(f32), pos)
    v_slc = v_slc.astype(f32)
    v_win = v_win.astype(f32)
    gates = jax.nn.sigmoid(gate_logits.astype(f32)).reshape(b, s, G, R, 3)

    n_cmp = (s - CMP_LEN) // CMP_STRIDE + 1
    cmp_start = jnp.arange(n_cmp) * CMP_STRIDE
    cmp_end = cmp_start + CMP_LEN - 1
    cmp_idx = cmp_start[:, None] + jnp.arange(CMP_LEN)[None, :]

    def compress(t, w):
        blk = t.astype(f32)[:, cmp_idx] + cmp_pos.astype(f32)[None, None, :, None, :]
        blk = blk.transpose(0, 1, 3, 2, 4).reshape(b, n_cmp, G, CMP_LEN * dk)
        return jnp.einsum('bngc,cd->bngd', blk, w.astype(f32))

    k_cmp = partial_rope(compress(k_cmp_in, w_cmp_k), cmp_start)
    v_cmp = compress(v_cmp_in, w_cmp_v)

    n_sel = s // SLC_LEN
    top_n = min(SLC_TOPN, n_sel)
    sel_start = jnp.arange(n_sel) * SLC_LEN
    blk_ids = jnp.arange(n_sel)
    overlap = ((cmp_start[:, None] < sel_start[None, :] + SLC_LEN) &
               (cmp_end[:, None] >= sel_start[None, :])).astype(f32)
    k_sel_blocks = k_slc.reshape(b, n_sel, SLC_LEN, G, dk).transpose(0, 3, 1, 2, 4)
    v_sel_blocks = v_slc.reshape(b, n_sel, SLC_LEN, G, dk).transpose(0, 3, 1, 2, 4)
    gather_blocks = jax.vmap(jax.vmap(lambda blocks, ids: blocks[ids]))
    slc_offsets = jnp.arange(SLC_LEN)

    k_win_pad = jnp.pad(k_win, ((0, 0), (WINDOW, 0), (0, 0), (0, 0)))
    v_win_pad = jnp.pad(v_win, ((0, 0), (WINDOW, 0), (0, 0), (0, 0)))
    win_offsets = jnp.arange(WINDOW + Q_BLOCK) - WINDOW
    q_offsets = jnp.arange(Q_BLOCK)

    def query_block(c):
        t0 = c * Q_BLOCK
        tpos = t0 + q_offsets
        qb = lax.dynamic_slice_in_dim(q, t0, Q_BLOCK, axis=1)
        gb = lax.dynamic_slice_in_dim(gates, t0, Q_BLOCK, axis=1)
        cmask = cmp_end[None, :] <= tpos[:, None]
        p_cmp = masked_softmax(jnp.einsum('bqgrd,bngd->bgrqn', qb, k_cmp) * scale, cmask)
        o_cmp = jnp.einsum('bgrqn,bngd->bqgrd', p_cmp, v_cmp)
        imp = jnp.einsum('bgrqn,nj->bgqj', p_cmp, overlap)
        force = (blk_ids[None, :] == (tpos // SLC_LEN)[:, None]) | (blk_ids[None, :] == 0)
        valid = sel_start[None, :] <= tpos[:, None]
        score = jnp.where(force, FORCE_SCORE, jnp.where(valid, imp, -1.0))
        _, sel_idx = lax.top_k(score, top_n)
        k_sel = gather_blocks(k_sel_blocks, sel_idx).reshape(b, G, Q_BLOCK, top_n * SLC_LEN, dk)
        v_sel = gather_blocks(v_sel_blocks, sel_idx).reshape(b, G, Q_BLOCK, top_n * SLC_LEN, dk)
        sel_pos = (sel_idx[..., None] * SLC_LEN + slc_offsets).reshape(b, G, Q_BLOCK, top_n * SLC_LEN)
        smask = (sel_pos <= tpos[None, None, :, None])[:, :, None]
        p_slc = masked_softmax(jnp.einsum('bqgrd,bgqmd->bgrqm', qb, k_sel) * scale, smask)
        o_slc = jnp.einsum('bgrqm,bgqmd->bqgrd', p_slc, v_sel)
        kw = lax.dynamic_slice_in_dim(k_win_pad, t0, WINDOW + Q_BLOCK, axis=1)
        vw = lax.dynamic_slice_in_dim(v_win_pad, t0, WINDOW + Q_BLOCK, axis=1)
        kpos = t0 + win_offsets
        rel = tpos[:, None] - kpos[None, :]
        wmask = (rel >= 0) & (rel < WINDOW) & (kpos[None, :] >= 0)
        p_win = masked_softmax(jnp.einsum('bqgrd,bmgd->bgrqm', qb, kw) * scale, wmask)
        o_win = jnp.einsum('bgrqm,bmgd->bqgrd', p_win, vw)
        return gb[..., 0:1] * o_cmp + gb[..., 1:2] * o_slc + gb[..., 2:3] * o_win

    out = lax.map(query_block, jnp.arange(s // Q_BLOCK))
    return out.transpose(1, 0, 2, 3, 4, 5).reshape(b, s, NSA_WIDTH)

def hgrn2_mixer(q, f_logit, i_in, lb):
    f32 = jnp.float32
    b, s = q.shape[0], q.shape[1]
    q = q.astype(f32).reshape(b, s, HG_HEADS, HG_KEY_DIM)
    f = lb + (1.0 - lb) * jax.nn.sigmoid(f_logit.astype(f32).reshape(b, s, HG_HEADS, HG_KEY_DIM))
    log_f = jnp.log(f)
    k = 1.0 - f
    v = i_in.astype(f32).reshape(b, s, HG_HEADS, HG_VAL_DIM)
    n_ch = s // HG_CHUNK

    def to_chunks(t):
        return t.reshape(b, n_ch, HG_CHUNK, HG_HEADS, t.shape[-1]).transpose(1, 0, 3, 2, 4)

    causal = jnp.tril(jnp.ones((HG_CHUNK, HG_CHUNK), dtype=bool))

    def chunk_step(state, inp):
        qc, kc, vc, gc = inp
        bcum = jnp.cumsum(gc, axis=2)
        o_inter = jnp.einsum('bhtk,bhkv->bhtv', qc * jnp.exp(bcum), state)
        rel = jnp.where(causal[:, :, None], bcum[:, :, :, None, :] - bcum[:, :, None, :, :], -jnp.inf)
        attn = jnp.einsum('bhtk,bhsk,bhtsk->bhts', qc, kc, jnp.exp(rel))
        o_intra = jnp.einsum('bhts,bhsv->bhtv', attn, vc)
        b_last = bcum[:, :, -1:, :]
        new_state = (jnp.exp(b_last[:, :, 0, :])[..., None] * state +
                     jnp.einsum('bhsk,bhsv->bhkv', kc * jnp.exp(b_last - bcum), vc))
        return new_state, o_inter + o_intra

    state0 = jnp.zeros((b, HG_HEADS, HG_KEY_DIM, HG_VAL_DIM), f32)
    _, o = lax.scan(chunk_step, state0, (to_chunks(q), to_chunks(k), to_chunks(v), to_chunks(log_f)))
    return o.transpose(1, 0, 3, 2, 4).reshape(b, s, HG_HEADS, HG_VAL_DIM)

def hier_moe(h, w_grp, b_grp, w_rtr, b_rtr, w_gate, w_up, w_down):
    f32 = jnp.float32
    b, s, d = h.shape
    t = h.reshape(b * s, d)
    grp_logits = (t @ w_grp).astype(f32) + b_grp.astype(f32)
    grp_sel = jnp.argmax(grp_logits, axis=-1)
    grp_prob = jnp.take_along_axis(jax.nn.softmax(grp_logits, axis=-1), grp_sel[:, None], axis=1)
    exp_logits = ((t @ w_rtr).astype(f32) + b_rtr.astype(f32)).reshape(-1, N_GROUPS, EXPERTS_PER_GROUP)
    in_grp = jnp.take_along_axis(exp_logits, grp_sel[:, None, None], axis=1)[:, 0]
    top_logits, top_idx = lax.top_k(in_grp, TOP_K_IN_GROUP)
    top_w = jax.nn.softmax(top_logits, axis=-1) * grp_prob
    expert_ids = grp_sel[:, None] * EXPERTS_PER_GROUP + top_idx
    combine = jnp.sum(jax.nn.one_hot(expert_ids, N_EXPERTS, dtype=f32) * top_w[..., None], axis=1)
    out = jnp.zeros((b * s, d), f32)
    for e in range(N_EXPERTS):
        hid = jax.nn.silu(t @ w_gate[e]) * (t @ w_up[e])
        out = out + combine[:, e:e + 1] * (hid @ w_down[e]).astype(f32)
    return out.reshape(b, s, d).astype(h.dtype)

def second_inputs(seed: int = 0) -> dict:
    key = jax.random.key(seed)
    ks = jax.random.split(key, 24)
    f32 = jnp.float32
    nrm = lambda k, shape, scale: jax.random.normal(k, shape, f32) * scale
    return {
        'x': nrm(ks[0], (BATCH, SEQ, D_MODEL), 1.0),
        'attn_norm': 1.0 + nrm(ks[1], (DEPTH_2, D_MODEL), 0.01),
        'w_in': nrm(ks[2], (DEPTH_2, D_MODEL, IN_COLS), D_MODEL ** -0.5),
        'w_cmp_k': nrm(ks[3], (DEPTH_2, CMP_LEN * NSA_HEAD_DIM, NSA_HEAD_DIM), (CMP_LEN * NSA_HEAD_DIM) ** -0.5),
        'w_cmp_v': nrm(ks[4], (DEPTH_2, CMP_LEN * NSA_HEAD_DIM, NSA_HEAD_DIM), (CMP_LEN * NSA_HEAD_DIM) ** -0.5),
        'cmp_pos': nrm(ks[5], (DEPTH_2, CMP_LEN, NSA_HEAD_DIM), 0.02),
        'hg_lb_logits': nrm(ks[6], (DEPTH_2 + 1, HG_HEADS * HG_KEY_DIM), 0.5),
        'hg_norm': 1.0 + nrm(ks[7], (DEPTH_2, HG_VAL_DIM), 0.01),
        'w_br_nsa': nrm(ks[8], (DEPTH_2, NSA_WIDTH, D_MODEL), NSA_WIDTH ** -0.5),
        'w_br_hg': nrm(ks[9], (DEPTH_2, HG_WIDTH, D_MODEL), HG_WIDTH ** -0.5),
        'w_out': nrm(ks[10], (DEPTH_2, D_MODEL, D_MODEL), D_MODEL ** -0.5),
        'ffn_norm': 1.0 + nrm(ks[11], (DEPTH_2, D_MODEL), 0.01),
        'w_grp': nrm(ks[12], (DEPTH_2, D_MODEL, N_GROUPS), D_MODEL ** -0.5),
        'b_grp': nrm(ks[13], (DEPTH_2, N_GROUPS), 0.01),
        'w_rtr': nrm(ks[14], (DEPTH_2, D_MODEL, N_EXPERTS), D_MODEL ** -0.5),
        'b_rtr': nrm(ks[15], (DEPTH_2, N_EXPERTS), 0.01),
        'w_gate': nrm(ks[16], (DEPTH_2, N_EXPERTS, D_MODEL, D_FF_EXPERT), D_MODEL ** -0.5),
        'w_up': nrm(ks[17], (DEPTH_2, N_EXPERTS, D_MODEL, D_FF_EXPERT), D_MODEL ** -0.5),
        'w_down': nrm(ks[18], (DEPTH_2, N_EXPERTS, D_FF_EXPERT, D_MODEL), D_FF_EXPERT ** -0.5),
        'final_norm': 1.0 + nrm(ks[19], (D_MODEL,), 0.01),
    }

def second_block(x, attn_norm, w_in, w_cmp_k, w_cmp_v, cmp_pos, hg_lb_logits, hg_norm, w_br_nsa, w_br_hg,
              w_out, ffn_norm, w_grp, b_grp, w_rtr, b_rtr, w_gate, w_up, w_down, final_norm):
    b, s, _ = x.shape
    lower_bounds = jnp.cumsum(jax.nn.softmax(hg_lb_logits.astype(jnp.float32), axis=0), axis=0)
    split_points = np.cumsum(IN_SPLITS)[:-1].tolist()
    for layer in range(DEPTH_2):
        h = rmsnorm(x, attn_norm[layer])
        proj = h @ w_in[layer]
        nsa_q, nsa_kv, nsa_gate, hg_q, hg_f, hg_i, hg_g, merge_logits = jnp.split(proj, split_points, axis=-1)
        kv = nsa_kv.reshape(b, s, 6, NSA_KV_GROUPS, NSA_HEAD_DIM)
        o_nsa = nsa_mixer(nsa_q.reshape(b, s, NSA_HEADS, NSA_HEAD_DIM),
                          kv[:, :, 0], kv[:, :, 1], kv[:, :, 2], kv[:, :, 3], kv[:, :, 4], kv[:, :, 5],
                          nsa_gate.reshape(b, s, NSA_HEADS, 3),
                          w_cmp_k[layer], w_cmp_v[layer], cmp_pos[layer])
        lb = lower_bounds[layer].reshape(HG_HEADS, HG_KEY_DIM)
        o_hg = hgrn2_mixer(hg_q, hg_f, hg_i, lb)
        o_hg = rmsnorm(o_hg, hg_norm[layer]) * jax.nn.silu(
            hg_g.astype(jnp.float32).reshape(b, s, HG_HEADS, HG_VAL_DIM))
        o_hg = o_hg.reshape(b, s, HG_WIDTH).astype(x.dtype)
        gate_nsa, gate_hg = jnp.split(jax.nn.sigmoid(merge_logits), 2, axis=-1)
        mixed = (gate_nsa * (o_nsa.astype(x.dtype) @ w_br_nsa[layer]) +
                 gate_hg * (o_hg @ w_br_hg[layer]))
        x = x + mixed @ w_out[layer]
        x = x + hier_moe(rmsnorm(x, ffn_norm[layer]), w_grp[layer], b_grp[layer], w_rtr[layer], b_rtr[layer],
                         w_gate[layer], w_up[layer], w_down[layer])
    return rmsnorm(x, final_norm)


def setup_inputs(seed=0):
    out = dict(first_inputs(seed))
    for name, value in second_inputs(seed + 1).items():
        if name != "x":
            out[name + "_2"] = value
    return out


def reference(
    x, c, ctx, c_ctx, ada_w, ada_b, ln1_g, ln1_b, ln2_g, ln2_b, ffn_w_in, ffn_conv_w,
    ffn_conv_b, ffn_w_out, mla_w_in, mla_q_norm, mla_kv_norm, mla_w_qb, mla_w_kvb, mla_w_o,
    na_w_qkv, na_rpb, na_w_o, diff_w_qkv, diff_lambda, diff_subln, diff_w_o, swa_w_qkv,
    swa_sinks, swa_w_o, attn_norm_2, w_in_2, w_cmp_k_2, w_cmp_v_2, cmp_pos_2, hg_lb_logits_2,
    hg_norm_2, w_br_nsa_2, w_br_hg_2, w_out_2, ffn_norm_2, w_grp_2, b_grp_2, w_rtr_2, b_rtr_2,
    w_gate_2, w_up_2, w_down_2, final_norm_2,
):
    x = first_block(
        x, c, ctx, c_ctx, ada_w, ada_b, ln1_g, ln1_b, ln2_g, ln2_b, ffn_w_in, ffn_conv_w,
        ffn_conv_b, ffn_w_out, mla_w_in, mla_q_norm, mla_kv_norm, mla_w_qb, mla_w_kvb, mla_w_o,
        na_w_qkv, na_rpb, na_w_o, diff_w_qkv, diff_lambda, diff_subln, diff_w_o, swa_w_qkv,
        swa_sinks, swa_w_o,
    )
    return second_block(
        x, attn_norm_2, w_in_2, w_cmp_k_2, w_cmp_v_2, cmp_pos_2, hg_lb_logits_2, hg_norm_2,
        w_br_nsa_2, w_br_hg_2, w_out_2, ffn_norm_2, w_grp_2, b_grp_2, w_rtr_2, b_rtr_2,
        w_gate_2, w_up_2, w_down_2, final_norm_2,
    )


_drawn_inputs = setup_inputs


def setup_inputs(seed=0):
    import zlib

    import numpy as np

    out = dict(_drawn_inputs(seed))
    spreads = {}
    factors = {'ada_b': 3.008,
     'ffn_conv_b': 8.0,
     'mla_q_norm': 8.0,
     'mla_kv_norm': 8.0,
     'na_rpb': 8.0,
     'attn_norm_2': 3.861,
     'hg_norm_2': 4.019,
     'ffn_norm_2': 2.801,
     'b_grp_2': 7.201,
     'b_rtr_2': 4.775,
     'final_norm_2': 26.945,
     'cmp_pos_2': 8.0}
    for name, (base, spread) in spreads.items():
        noise = np.random.default_rng([zlib.crc32(name.encode()), seed]).standard_normal(out[name].shape)
        drawn = base * np.exp(spread * noise) if base else spread * noise
        out[name] = jnp.asarray(drawn.astype(out[name].dtype))
    for name, factor in factors.items():
        out[name] = (out[name] * factor).astype(out[name].dtype)
    return out
```

```python
import math
from contextlib import ExitStack

import numpy as np
import concourse.bass as bass
from concourse import mybir

F32 = mybir.dt.float32
ACT = mybir.ActivationFunctionType
ALU = mybir.AluOpType
AX = mybir.AxisListType

P = 128
D = 1024
KT = D // P
CTX = 256
LAT = 256
T = CTX + LAT
DEPTH = 2
ALPHA = (2.0 * DEPTH) ** 0.25
LN_EPS, RMS_EPS = 1e-5, 1e-6
NEG = -1e30
HUGE = 3.0e38
GRID_W = 64

MLA_H, DN, DR, DV = 16, 64, 32, 64
QK = DN + DR
QL, KVL = 384, 256
QLT, KVT = QL // P, KVL // P
NA_PAIRS = 8
FFN = 2816
FT = FFN // P
NSA_PAIRS = 4
NCMP = 15
HG = 4
EXPERTS, GROUPS, PER_GROUP = 32, 4, 8
FE = 512
FET = FE // P

SLOT = 6144
RING = 2

VECS = [("cvec", KT * 2), ("ada_b", DEPTH * 48),
        ("ln1_g", DEPTH * KT), ("ln1_b", DEPTH * KT), ("ln2_g", DEPTH * KT), ("ln2_b", DEPTH * KT),
        ("conv_w", DEPTH * 3 * 2 * FT), ("conv_b", DEPTH * 2 * FT),
        ("q_norm", QLT), ("kv_norm", KVT), ("attn_norm", KT), ("ffn_norm", KT),
        ("hg_lb", 2 * HG), ("hg_norm", 1), ("cmp_pos", 32),
        ("w_gate24", KT * 24), ("w_route", KT * 36), ("b_route", 36), ("final_norm", D)]
VOFF, _at = {}, 0
for _n, _w in VECS:
    VOFF[_n] = (_at, _w)
    _at += _w
NVEC = _at

LEVELS = [64, 32, 16, 8, 4, 2, 1]
CONSTS = [("ident", P), ("ones", P), ("mean", P), ("rot_mla", QK), ("cos_mla", LAT), ("sin_mla", LAT),
          ("rot_nsa", P), ("cos_nsa", LAT), ("sin_nsa", LAT), ("na_mask", LAT),
          ("nsa_mask", 416), ("cmp_keep", 32), ("level_mask", (len(LEVELS) + 1) * P), ("scan_keep", LAT),
          ("first4", GROUPS), ("first8", PER_GROUP)]
COFF, _at = {}, 0
for _n, _w in CONSTS:
    COFF[_n] = (_at, _w)
    _at += _w
NCONST = _at

T_Q, T_CK, T_CV, T_SK, T_SV, T_WK, T_WV, T_HQ, T_HF, T_HI, T_HGATE, T_MN, T_MH = \
    0, 4, 5, 6, 7, 8, 9, 10, 14, 18, 22, 26, 34
NPROJ = 42

STREAM = [("ada", 16, 6144), ("mla_in", 1, 5 * D + 8 * QK), ("mla_head", 16, 544), ("mla_o", 2, 4096),
          ("ffn_in0", 11, 4096), ("ffn_out0", 4, 5632),
          ("na_pair", NA_PAIRS, 3072), ("na_o", 2, 4096),
          ("ffn_in1", 11, 4096), ("ffn_out1", 4, 5632),
          ("proj", 7, 6144), ("cmp", 2, 4096), ("branch", 2, 4096), ("w_out", 2, 4096),
          ("moe", 2 * EXPERTS, 6144)]
FIRST, _at = {}, 0
for _n, _c, _w in STREAM:
    FIRST[_n] = _at
    _at += _c
CHUNKS = {n: c for n, c, _ in STREAM}


def each(k):
    return lambda c: c * k + k


CHUNK_USED = {
    "ada": ("ada_used", each(1)), "mla_in": ("mla_in_used", each(1)),
    "mla_head": ("mla_proj_done", each(1)), "mla_o": ("mla_o_y_ready", each(4)),
    "ffn_in0": ("ffn0_up_done", each(2)), "ffn_out0": ("ffn_out0_y_ready", each(2)),
    "na_pair": ("na_proj_done", each(1)), "na_o": ("na_o_y_ready", each(4)),
    "ffn_in1": ("ffn1_up_done", each(2)), "ffn_out1": ("ffn_out1_y_ready", each(2)),
    "proj": ("proj_tile_done", each(6)), "cmp": ("cmp_used", each(1)),
    "branch": ("branch_done", lambda c: KT), "w_out": ("w_out_y_ready", each(4)),
    "moe": (None, None),
}


class Kernel:

    def __init__(self, nc, W, vec, const, xT, na_bias, out):
        self.nc, self.W, self.vec_d, self.const_d, self.xT, self.nab_d, self.out = \
            nc, W, vec, const, xT, na_bias, out
        self.phases = {"pe": 0, "act": 0, "dve": 0}
        self.links = {"act": 0, "dve": 0}
        self.norms = {"pe": 0, "act": 0, "dve": 0}
        self.norm_counts = {w: (0, 0, 0) for w in self.norms}
        self.flips = {"pe": 0, "dve": 0}
        self.outs = {"pe": 0, "dve": 0}

    def sem(self, name):
        if name not in self.sems:
            self.sems[name] = self.ctx.enter_context(self.nc.semaphore(name))
        return self.sems[name]

    def vec(self, name, i=0, n=None):
        off, w = VOFF[name]
        return self.V[:, off + i:off + (w if n is None else i + n)]

    def con(self, name, i=0, n=None):
        off, w = COFF[name]
        return self.C[:, off + i:off + (w if n is None else i + n)]

    def phase_end(self, eng, who):
        self.phases[who] += 1
        eng.drain().then_inc(self.phase_done, 1)
        eng.wait_ge(self.phase_done, 3 * self.phases[who])

    def link(self, eng, who, ins):
        self.links[who] += 1
        s = self.chain[who]
        ins.then_inc(s, 1)
        eng.wait_ge(s, self.links[who])

    def chunks(self, pe, name, body, count=None, start=0):
        g0 = FIRST[name] + start
        n = (CHUNKS[name] if count is None else count)
        turns = n // 2
        if turns >= 2:
            with pe.Fori(0, turns) as it:
                for s in range(2):
                    g = g0 + s
                    pe.wait_ge(self.w_loaded[g % 2], it * 16 + 16 * (g // 2 + 1))
                    body(it * 2 + s + start, self.ring[g % 2])
            done = 2 * turns
        else:
            done = 0
        for j in range(done, n):
            g = g0 + j
            pe.wait_ge(self.w_loaded[g % 2], 16 * (g // 2 + 1))
            body(j + start, self.ring[g % 2])

    def counted(self, eng, n, body):
        with eng.Fori(0, n // 2) as it:
            for s in range(2):
                body(it * 2 + s)
        if n % 2:
            body(n - 1)

    def build(self):
        nc = self.nc
        with ExitStack() as ctx:
            self.ctx, self.sems = ctx, {}

            def sb(name, shape):
                return ctx.enter_context(nc.sbuf_tensor(name, shape, F32))
            self.ring = [sb(f"ring{i}", [P, SLOT]) for i in range(RING)]
            self.H = sb("residual", [P, KT, T])
            self.A = sb("layer_input", [P, KT, T])
            self.X = sb("scratch", [P, KT * T])
            self.B = sb("big", [P, FT * T])
            self.N = sb("bias", [P, 16 * 2 * LAT])
            self.V = sb("vectors", [P, NVEC])
            self.C = sb("constants", [P, NCONST])
            self.ADA = sb("ada", [P, DEPTH, 48, 2])
            self.S = sb("stats", [P, 256])
            self.R = sb("rstd", [P, T])
            self.bank = [ctx.enter_context(nc.psum_tensor(f"bank{i}", [P, 512], F32)) for i in range(8)]
            self.w_loaded = [self.sem(f"w_loaded{i}") for i in range(RING)]
            self.phase_done = self.sem("phase_done")
            self.chain = {"dve": self.sem("dve_link"), "act": self.sem("act_link")}
            self.const_in, self.bias_in = self.sem("const_in"), self.sem("bias_in")
            block = ctx.enter_context(nc.Block())

            @block.tensor
            def _(pe):
                self.run("pe", pe)

            @block.scalar
            def _(act):
                act.dma_start(self.V[:, :], self.vec_d).then_inc(self.const_in, 16)
                act.dma_start(self.C[:, :], self.const_d).then_inc(self.const_in, 16)
                act.dma_start(self.H[:, :, :], self.xT).then_inc(self.const_in, 16)
                nb = self.N[:, :].rearrange("p (t h k) -> p t h k", t=2, h=16)
                for row in range(4):
                    part = slice(64 * (row % 2), 64 * (row % 2) + 64)
                    act.dma_start(nb[part, row // 2, :, :], self.nab_d[row]).then_inc(self.bias_in, 16)
                self.run("act", act)

            @block.vector
            def _(dve):
                self.run("dve", dve)

            @block.sync
            def _(sp):
                self.sync_program(sp)

    def stages(self):
        return [self.ada, self.modulate_first, self.mla_in, self.mla_heads, self.mla_out,
                lambda w, e: self.ffn(w, e, 0), self.na_heads, self.na_out,
                lambda w, e: self.ffn(w, e, 1),
                self.proj, self.compress, self.nsa_heads, self.hgrn, self.branches,
                self.router, self.moe, self.final]

    def run(self, who, eng):
        st = self.stages()
        for stage in st:
            stage(who, eng)

    def sync_program(self, sp):
        for name, n, width in STREAM:
            w, g0 = self.W[name], FIRST[name]

            def load(j, s, g):
                sp.dma_start(self.ring[s][:, 0:width], w[j]).then_inc(self.w_loaded[s], 16)
            first = 0
            if g0 == 0:
                for j in range(RING):
                    load(j, j, j)
                first = RING
            while first < min(n, RING):
                g = g0 + first - RING
                before = max((m for m in FIRST if FIRST[m] <= g), key=FIRST.get)
                sem, upto = CHUNK_USED[before]
                sp.wait_ge(self.sem(sem), upto(g - FIRST[before]))
                load(first, (g0 + first) % 2, g0 + first)
                first += 1
            sem, upto = CHUNK_USED[name]
            turns = (n - first) // 2
            if turns >= 2:
                with sp.Fori(0, turns) as it:
                    for s in range(2):
                        g = g0 + first + s
                        if name == "moe":
                            sem = ("moe_up_done", "moe_down_done")[s]
                            sp.wait_ge(self.sem(sem), it * 4 + (2, 4)[s])
                        else:
                            sp.wait_ge(self.sem(sem), upto(it * 2 + (first + s - RING)))
                        load(it * 2 + first + s, g % 2, g)
                first += 2 * turns
            for j in range(first, n):
                sp.wait_ge(self.sem(sem), upto(j - RING))
                load(j, (g0 + j) % 2, g0 + j)
        sp.wait_ge(self.sem("result_ready"), 1)
        sp.dma_start(self.out.rearrange("a (t p) d -> p (a t) d", p=P),
                     self.result()).then_inc(self.sem("result_out"), 16)
        sp.wait_ge(self.sem("result_out"), 16)

    def mm(self, pe, out, lhs, rhs):
        for k, (a, b) in enumerate(zip(lhs, rhs)):
            last = pe.matmul(out, a, b, start=(k == 0), stop=(k == len(lhs) - 1))
        return last

    def norm(self, who, eng, c0, write, src=None, tiles=KT, centre=True, dim=D, eps=LN_EPS, sq=None):
        w = T - c0
        src = src or (lambda k: self.H[:, k, c0:T])
        xc = self.X[:, :].rearrange("p (k t) -> p k t", k=KT)
        sq = sq or (lambda k: self.A[:, k, c0:T])
        n = self.norms[who]
        self.norms[who] += 1
        mean_ready, centred, squared, var_ready, dev_ready = \
            [self.sem(x) for x in ("mean_ready", "centred", "squared", "var_ready", "dev_ready")]
        base, cbase, means = self.norm_counts[who]
        self.norm_counts[who] = (base + tiles, cbase + tiles * centre, means + centre)
        val = (lambda k: xc[:, k, 0:w]) if centre else src
        mu, var = self.bank[0][:, 0:w], self.bank[1][:, 0:w]
        if who == "pe":
            if centre:
                self.mm(eng, mu, [self.con("mean")] * tiles, [src(k) for k in range(tiles)])\
                    .then_inc(mean_ready, 1)
            for k in range(tiles):
                eng.wait_ge(squared, base + k + 1)
                last = eng.matmul(var, self.con("mean" if dim == D else "ones"), sq(k),
                                  start=(k == 0), stop=(k == tiles - 1))
            last.then_inc(var_ready, 1)
        if who == "act":
            for k in range(tiles):
                if centre:
                    eng.wait_ge(centred, cbase + k + 1)
                eng.activation(sq(k), val(k), ACT.Square).then_inc(squared, 1)
            eng.wait_ge(dev_ready, 2 * n + 1)
            eng.activation(self.R[:, 0:w], self.R[:, 0:w], ACT.Sqrt).then_inc(dev_ready, 1)
        if who == "dve":
            if centre:
                eng.wait_ge(mean_ready, means + 1)
                for k in range(tiles):
                    eng.tensor_tensor(val(k), src(k), mu, ALU.subtract).then_inc(centred, 1)
            eng.wait_ge(var_ready, n + 1)
            eng.tensor_scalar(self.R[:, 0:w], var, 1.0 if dim == D else 1.0 / dim, eps,
                              ALU.mult, ALU.add).then_inc(dev_ready, 1)
            eng.wait_ge(dev_ready, 2 * n + 2)
            self.link(eng, who, eng.reciprocal(self.R[:, 0:w], self.R[:, 0:w]))
            for k in range(tiles):
                write(k, val(k), self.R[:, 0:w])
        self.phase_end(eng, who)

    def layer_norm(self, who, eng, c0, gain, bias, layer):
        def write(k, x, r):
            self.link(eng, who, eng.tensor_tensor(x, x, r, ALU.mult))
            self.link(eng, who, eng.tensor_scalar(self.H[:, k, c0:T], x, self.vec(gain, layer * KT + k, 1),
                                                  self.vec(bias, layer * KT + k, 1), ALU.mult, ALU.add))
        self.norm(who, eng, c0, write)

    def modulate(self, who, eng, layer, shift, scale, segs):
        if who == "act":
            for k in range(KT):
                for seg in segs:
                    c = slice(CTX * seg, CTX * seg + 256)
                    eng.activation(self.A[:, k, c], self.H[:, k, c], ACT.Identity,
                                   bias=self.ADA[:, layer, shift * KT + k, seg:seg + 1],
                                   scale=self.ADA[:, layer, scale * KT + k, seg:seg + 1])
        self.phase_end(eng, who)

    def project_residual(self, who, eng, name, rhs, nk, per_chunk, gate, layer, segs):
        c0 = CTX * segs[0]
        w = T - c0
        y_ready, y_used = self.sem(name + "_y_ready"), self.sem(name + "_y_used")
        tiles = KT
        if who == "pe":
            def body(j, slot):
                for s in range(per_chunk):
                    oc = j * per_chunk + s
                    first_two = isinstance(oc, int) and oc < 2
                    if not first_two:
                        eng.wait_ge(y_used, oc - 1)
                    o = s % 2
                    m = self.mm(eng, self.bank[o][:, 0:w],
                                [slot[:, (s * nk + k) * P:(s * nk + k + 1) * P] for k in range(nk)],
                                [rhs(k) for k in range(nk)])
                    m.then_inc(y_ready, 1)
            for j in range(CHUNKS[name]):
                g = FIRST[name] + j
                eng.wait_ge(self.w_loaded[g % 2], 16 * (g // 2 + 1))
                body(j, self.ring[g % 2])
        if who == "dve":
            tmp = self.X[:, 0:w]
            for oc in range(tiles):
                eng.wait_ge(y_ready, oc + 1)
                y = self.bank[oc % 2][:, 0:w]
                if gate is None:
                    eng.tensor_tensor(self.H[:, oc, c0:T], self.H[:, oc, c0:T], y, ALU.add)\
                        .then_inc(y_used, 1)
                    continue
                for seg in segs:
                    part = slice(CTX * seg - c0, CTX * seg - c0 + 256)
                    last = eng.tensor_scalar(tmp[:, part], y[:, part],
                                             self.ADA[:, layer, gate * KT + oc, seg:seg + 1], None, ALU.mult)
                self.link(eng, who, last)
                last = eng.scalar_tensor_tensor(out=self.H[:, oc, c0:T], in0=self.H[:, oc, c0:T],
                                                scalar=ALPHA, in1=tmp, op0=ALU.mult, op1=ALU.add)
                last.then_inc(y_used, 1)
                eng.wait_ge(y_used, oc + 1)
        self.phase_end(eng, who)

    def flip(self, who, eng, src, dst, tiles, rows, name):
        n0 = self.flips.get(who, 0)
        self.flips[who] = n0 + tiles
        turned, copied = self.sem("turned"), self.sem("turned_copied")
        if who == "pe":
            for k in range(tiles):
                if n0 + k >= 2:
                    eng.wait_ge(copied, n0 + k - 1)
                for t in range(rows):
                    last = eng.transpose(self.bank[(n0 + k) % 2][:, t * P:(t + 1) * P], src(t, k),
                                         self.con("ident"))
                last.then_inc(turned, 1)
        if who == "dve":
            for k in range(tiles):
                eng.wait_ge(turned, n0 + k + 1)
                eng.tensor_copy(dst(k), self.bank[(n0 + k) % 2][:, 0:rows * P]).then_inc(copied, 1)
        self.phase_end(eng, who)

    def ada(self, who, eng):
        silu_ready = self.sem("silu_ready")
        cs = self.S[:, 0:2 * KT]
        if who == "act":
            eng.wait_ge(self.const_in, 48)
            eng.activation(cs, self.vec("cvec"), ACT.Silu).then_inc(silu_ready, 1)
        if who == "pe":
            eng.wait_ge(silu_ready, 1)

            def body(j, slot):
                for t in range(6):
                    last = self.mm(eng, self.bank[0][:, bass.ds(j * 12 + 2 * t, 2)],
                                   [slot[:, (t * KT + k) * P:(t * KT + k + 1) * P] for k in range(KT)],
                                   [cs[:, 2 * k:2 * k + 2] for k in range(KT)])
                last.then_inc(self.sem("ada_used"), 1)
            self.chunks(eng, "ada", body)
        self.phase_end(eng, who)
        if who == "dve":
            flat = self.ADA[:, :, :, :].rearrange("p l m s -> p (l m) s")
            b = self.vec("ada_b").unsqueeze(2).to_broadcast([P, DEPTH * 48, 2])
            self.link(eng, who, eng.tensor_tensor(
                flat, self.bank[0][:, 0:DEPTH * 96].rearrange("p (m s) -> p m s", s=2), b, ALU.add))
            for m in (1, 4):
                sc = self.ADA[:, :, m * KT:(m + 1) * KT, :]
                self.link(eng, who, eng.tensor_scalar(sc, sc, 1.0, None, ALU.add))
        self.phase_end(eng, who)

    def modulate_first(self, who, eng):
        self.modulate(who, eng, 0, 0, 1, (0, 1))

    def mla_views(self):
        b = self.B
        v = {}
        at = 0
        for name, n in (("cq", QLT * T), ("ckv", KVT * T), ("kpe", T), ("kpr", LAT),
                        ("q0", T), ("q1", T), ("qr0", LAT), ("qr1", LAT), ("qt0", LAT), ("qt1", LAT),
                        ("kt0", T), ("kt1", T), ("v0", 4 * DV), ("v1", 4 * DV)):
            v[name] = b[:, at:at + n]
            at += n
        assert at <= FT * T
        v["p"] = self.X[:, 0:1536]
        v["pt"] = self.X[:, 1536:3072]
        v["o"] = self.A[:, :, :].rearrange("p k t -> p (k t)").rearrange("p (t d) -> p t d", t=4)
        return v

    def mla_in(self, who, eng):
        v = self.mla_views()
        cq = v["cq"].rearrange("p (k t) -> p k t", k=QLT)
        ckv = v["ckv"].rearrange("p (k t) -> p k t", k=KVT)
        if who == "pe":
            g = FIRST["mla_in"]
            eng.wait_ge(self.w_loaded[g % 2], 16 * (g // 2 + 1))
            slot = self.ring[g % 2]
            for m in range(6):
                wd = P if m < 5 else QK
                last = self.mm(eng, self.bank[m][0:wd, :],
                               [slot[:, m * D + k * wd:m * D + (k + 1) * wd] for k in range(KT)],
                               [self.A[:, k, :] for k in range(KT)])
            last.then_inc(self.sem("mla_in_used"), 1)
        self.phase_end(eng, who)
        if who == "dve":
            for m in range(3):
                eng.tensor_copy(cq[:, m, :], self.bank[m][:, :])
            for m in range(2):
                eng.tensor_copy(ckv[:, m, :], self.bank[3 + m][:, :])
        if who == "act":
            eng.copy(v["kpe"][0:QK, :], self.bank[5][0:QK, :])
        self.phase_end(eng, who)

        def scaled(dst, gain):
            def write(k, x, r):
                self.link(eng, who, eng.tensor_tensor(x, x, r, ALU.mult))
                self.link(eng, who, eng.tensor_scalar(dst[:, k, :], x, self.vec(gain, k, 1), None, ALU.mult))
            return write
        sq = lambda k: self.A[:, k, :]
        self.norm(who, eng, 0, scaled(cq, "q_norm"), src=lambda k: cq[:, k, :], tiles=QLT, centre=False,
                  dim=QL, eps=RMS_EPS, sq=sq)
        self.norm(who, eng, 0, scaled(ckv, "kv_norm"), src=lambda k: ckv[:, k, :], tiles=KVT, centre=False,
                  dim=KVL, eps=RMS_EPS, sq=sq)
        if who == "pe":
            eng.matmul(self.bank[2][0:QK, 0:LAT], self.con("rot_mla")[0:QK, :], v["kpe"][0:QK, CTX:T],
                       start=True, stop=True)
        self.phase_end(eng, who)
        if who == "dve":
            r = slice(DN, QK)
            self.link(eng, who, eng.tensor_tensor(v["kpr"][r, :], self.bank[2][r, 0:LAT],
                                                  self.con("sin_mla")[r, :], ALU.mult))
            self.link(eng, who, eng.tensor_tensor(v["kt0"][r, CTX:T], v["kpe"][r, CTX:T],
                                                  self.con("cos_mla")[r, :], ALU.mult))
            self.link(eng, who, eng.tensor_tensor(v["kt0"][r, CTX:T], v["kt0"][r, CTX:T],
                                                  v["kpr"][r, :], ALU.add))
            eng.tensor_copy(v["kt1"][r, CTX:T], v["kt0"][r, CTX:T])
            eng.tensor_copy(v["kt0"][r, 0:CTX], v["kpe"][r, 0:CTX])
            eng.tensor_copy(v["kt1"][r, 0:CTX], v["kpe"][r, 0:CTX])
        self.phase_end(eng, who)

    def mla_heads(self, who, eng):
        v = self.mla_views()
        names = ("proj_done", "q_copied", "kv_copied", "rot_done", "rotated", "scored", "max_ready",
                 "exp_done", "turned", "pt_act", "pt_dve", "o_done", "o_used")
        s = {n: self.sem("mla_" + n) for n in names}
        link = self.sem("mla_link")
        scale = QK ** -0.5
        cq = v["cq"].rearrange("p (k t) -> p k t", k=QLT)
        ckv = v["ckv"].rearrange("p (k t) -> p k t", k=KVT)
        p, pt = v["p"], v["pt"].rearrange("p (b q) -> p b q", q=P)
        ptiles = [p[:, 0:256], p[:, 256:512], p[:, 512:1024], p[:, 1024:1536]]
        mx, nb, rs, rc = [[self.S[:, 64 + 16 * e + 4 * n:64 + 16 * e + 4 * n + 4] for e in range(2)]
                          for n in range(4)]
        bank = self.bank
        g0 = FIRST["mla_head"]

        def pe_project(h, e):
            slot = self.ring[(g0 + e) % 2]
            eng.wait_ge(self.w_loaded[(g0 + e) % 2], (h - e) * 8 + 16 * ((g0 + e) // 2 + 1))
            if isinstance(h, int) and h == 0:
                pass
            else:
                eng.wait_ge(s["rotated"], h)
                eng.wait_ge(s["kv_copied"], 2 * h)
            self.mm(eng, bank[0][0:QK, :], [slot[:, k * QK:(k + 1) * QK] for k in range(QLT)],
                    [cq[:, k, :] for k in range(QLT)])
            o = QLT * QK
            self.mm(eng, bank[1][0:DN, :], [slot[:, o + k * DN:o + (k + 1) * DN] for k in range(KVT)],
                    [ckv[:, k, :] for k in range(KVT)])
            o += KVT * DN
            for t in range(4):
                last = self.mm(eng, bank[2][:, t * DV:(t + 1) * DV],
                               [ckv[:, k, t * P:(t + 1) * P] for k in range(KVT)],
                               [slot[:, o + k * DV:o + (k + 1) * DV] for k in range(KVT)])
            last.then_inc(s["proj_done"], 1)

        def pe_scores(h, e):
            eng.wait_ge(s["q_copied"], h + 1)
            eng.wait_ge(s["kv_copied"], 2 * h + 2)
            eng.matmul(bank[2][0:QK, 256:512], self.con("rot_mla")[0:QK, :], v[f"q{e}"][0:QK, CTX:T],
                       start=True, stop=True).then_inc(s["rot_done"], 1)
            eng.wait_ge(s["o_used"], h + 1)
            q, qr, k = v[f"q{e}"], v[f"qr{e}"], v[f"kt{e}"]
            for t in range(2):
                last = eng.matmul(bank[3][:, t * 256:(t + 1) * 256], q[0:QK, t * P:(t + 1) * P],
                                  k[0:QK, 0:CTX], start=True, stop=True)
            last.then_inc(s["scored"], 1)
            eng.wait_ge(s["rotated"], h + 1)
            for t in range(2):
                eng.matmul(bank[4 + t][:, 0:CTX], q[0:QK, CTX + t * P:CTX + (t + 1) * P], k[0:QK, 0:CTX],
                           start=True, stop=True)
                eng.matmul(bank[4 + t][:, CTX:T], qr[0:QK, t * P:(t + 1) * P], k[0:QK, CTX:T],
                           start=True, stop=True).then_inc(s["scored"], 1)

        def pe_tail(h, e):
            for n, (b, tile0, blocks) in enumerate(((6, 0, 4), (7, 2, 4), (3, 3, 4))):
                eng.wait_ge(s["exp_done"], 4 * h + (2, 3, 4)[n])
                for j in range(blocks):
                    src = ptiles[j // 2][:, (j % 2) * P:(j % 2 + 1) * P] if n == 0 \
                        else ptiles[tile0][:, j * P:(j + 1) * P]
                    last = eng.transpose(bank[b][:, j * P:(j + 1) * P], src, self.con("ident"))
                last.then_inc(s["turned"], 1)
            vv = v[f"v{e}"].rearrange("p (t d) -> p t d", t=4)
            eng.wait_ge(s["pt_act"], 2 * h + 2)
            eng.wait_ge(s["pt_dve"], h + 1)
            for t in range(4):
                bl = ((0, 1), (2, 3), (4, 5, 6, 7), (8, 9, 10, 11))[t]
                last = self.mm(eng, bank[4][:, t * DV:(t + 1) * DV], [pt[:, b, :] for b in bl],
                               [vv[:, i, :] for i in range(len(bl))])
            last.then_inc(s["o_done"], 1)

        def dve_project(h, e):
            eng.wait_ge(s["proj_done"], h + 1)
            eng.tensor_copy(v[f"q{e}"][0:QK, :], bank[0][0:QK, :]).then_inc(s["q_copied"], 1)
            eng.wait_ge(s["q_copied"], h + 1)
            eng.tensor_tensor(v[f"qt{e}"][0:QK, :], v[f"q{e}"][0:QK, CTX:T], self.con("cos_mla")[0:QK, :],
                              ALU.mult).then_inc(link, 1)

        def dve_max(h, e):
            eng.wait_ge(s["rot_done"], h + 1)
            eng.tensor_tensor(v[f"qr{e}"][0:QK, :], bank[2][0:QK, 256:512], self.con("sin_mla")[0:QK, :],
                              ALU.mult).then_inc(link, 1)
            eng.wait_ge(link, self.mla_links(h, 0))
            eng.tensor_tensor(v[f"qr{e}"][0:QK, :], v[f"qr{e}"][0:QK, :], v[f"qt{e}"][0:QK, :],
                              ALU.add).then_inc(s["rotated"], 1)
            eng.wait_ge(s["scored"], 3 * h + 1)
            eng.tensor_reduce(mx[e][:, 0:2], bank[3][:, :].rearrange("p (t k) -> p t k", t=2), AX.X, ALU.max)
            for t in range(2):
                eng.wait_ge(s["scored"], 3 * h + 2 + t)
                last = eng.tensor_reduce(mx[e][:, 2 + t:3 + t], bank[4 + t][:, :], AX.X, ALU.max)
            last.then_inc(link, 1)
            eng.wait_ge(link, self.mla_links(h, 1))
            eng.tensor_scalar(nb[e], mx[e], -scale, None, ALU.mult).then_inc(s["max_ready"], 1)

        def dve_tail(h, e):
            eng.wait_ge(s["exp_done"], 4 * h + 4)
            eng.reciprocal(rc[e], rs[e]).then_inc(link, 1)
            eng.wait_ge(s["turned"], 3 * h + 2)
            eng.tensor_copy(v["pt"][:, 512:1024], bank[7][:, :]).then_inc(s["pt_dve"], 1)
            eng.wait_ge(s["o_done"], h + 1)
            eng.wait_ge(link, self.mla_links(h, 2))
            eng.tensor_tensor(v["o"][:, :, bass.ds(h * DV, DV)],
                              bank[4][:, 0:256].rearrange("p (t d) -> p t d", t=4),
                              rc[e].unsqueeze(2).to_broadcast([P, 4, DV]), ALU.mult).then_inc(s["o_used"], 1)

        def act_project(h, e):
            eng.wait_ge(s["proj_done"], h + 1)
            eng.copy(v[f"kt{e}"][0:DN, :], bank[1][0:DN, :]).then_inc(s["kv_copied"], 1)
            eng.copy(v[f"v{e}"], bank[2][:, 0:256]).then_inc(s["kv_copied"], 1)

        def act_exp(h, e):
            eng.wait_ge(s["max_ready"], h + 1)
            src = [bank[3][:, 0:256], bank[3][:, 256:512], bank[4][:, :], bank[5][:, :]]
            for t in range(4):
                eng.activation(ptiles[t], src[t], ACT.Exp, bias=nb[e][:, t:t + 1], scale=scale,
                               accum_out=rs[e][:, t:t + 1]).then_inc(s["exp_done"], 1)

        def act_tail(h, e):
            eng.wait_ge(s["turned"], 3 * h + 1)
            eng.copy(v["pt"][:, 0:512], bank[6][:, :]).then_inc(s["pt_act"], 1)
            eng.wait_ge(s["turned"], 3 * h + 3)
            eng.copy(v["pt"][:, 1024:1536], bank[3][:, :]).then_inc(s["pt_act"], 1)

        steps = {"pe": (pe_project, pe_scores, pe_tail), "dve": (dve_project, dve_max, dve_tail),
                 "act": (act_project, act_exp, act_tail)}[who]
        if who == "dve":
            eng.nop().then_inc(s["o_used"], 1)
        self.pipelined(eng, MLA_H, *steps)
        self.phase_end(eng, who)

    @staticmethod
    def mla_links(h, which):
        return h * 4 + (2, 3, 4 if isinstance(h, int) and h == MLA_H - 1 else 5)[which]

    def pipelined(self, eng, n, project, middle, tail):
        project(0, 0)
        with eng.Fori(0, n // 2 - 1) as it:
            for e in range(2):
                u = it * 2 + e
                middle(u, e)
                project(u + 1, 1 - e)
                tail(u, e)
        for u in (n - 2, n - 1):
            middle(u, u % 2)
            if u + 1 < n:
                project(u + 1, (u + 1) % 2)
            tail(u, u % 2)

    def mla_out(self, who, eng):
        v = self.mla_views()
        o = v["o"]
        oT = self.B[:, 0:KT * T].rearrange("p (k t) -> p k t", k=KT)
        self.flip(who, eng, lambda t, k: o[:, t, k * P:(k + 1) * P], lambda k: oT[:, k, :], KT, 4, "mla")
        self.project_residual(who, eng, "mla_o", lambda k: oT[:, k, :], KT, 4, 2, 0, (0, 1))
        self.layer_norm(who, eng, 0, "ln1_g", "ln1_b", 0)

    def ffn(self, who, eng, layer):
        segs = (0, 1) if layer == 0 else (1,)
        c0 = CTX * segs[0]
        w = T - c0
        ns = len(segs)
        self.modulate(who, eng, layer, 3, 4, segs)
        name = f"ffn{layer}_"
        up_done, up_used, gate_in, gate_out, hid_done = \
            [self.sem(name + x) for x in ("up_done", "up_used", "gate_in", "gate_out", "hid_done")]
        link = self.sem(name + "link")
        hid = self.B[:, :].rearrange("p (f t) -> p f t", f=FT)
        cw, cb = VOFF["conv_w"][0] + layer * 3 * 2 * FT, VOFF["conv_b"][0] + layer * 2 * FT
        u = [[self.X[:, (2 * e + x) * T:(2 * e + x) * T + w] for x in range(2)] for e in range(2)]
        sg = [self.X[:, (4 + e) * T:(4 + e) * T + w] for e in range(2)]

        if who == "pe":
            def body(j, slot):
                for e in range(2):
                    f = j * 2 + e
                    if not (isinstance(j, int) and j == 0):
                        eng.wait_ge(up_used, f - 1)
                    for x in range(2):
                        m = 2 * x + e
                        last = self.mm(eng, self.bank[2 * e + x][:, 0:w],
                                       [slot[:, (m * KT + k) * P:(m * KT + k + 1) * P] for k in range(KT)],
                                       [self.A[:, k, c0:T] for k in range(KT)])
                    last.then_inc(up_done, 1)
            g = FIRST[f"ffn_in{layer}"]
            eng.wait_ge(self.w_loaded[g % 2], 16 * (g // 2 + 1))
            body(0, self.ring[g % 2])
            self.chunks(eng, f"ffn_in{layer}", body, count=CHUNKS[f"ffn_in{layer}"] - 1, start=1)

        def seg(ap, lo, hi):
            return ap.rearrange("p (s t) -> p s t", s=ns)[:, :, lo:hi]

        def conv(f, e):
            eng.wait_ge(up_done, f + 1)
            for tap, (olo, ohi, ilo, ihi) in enumerate(((None,) * 4, (1, 256, 0, 255), (0, 255, 1, 256))):
                for x in range(2):
                    src, dst = self.bank[2 * e + x][:, 0:w], u[e][x]
                    col = f + x * FT
                    if tap == 0:
                        ins = eng.tensor_scalar(dst, src, self.V[:, bass.ds(cw + 2 * FT + col, 1)],
                                                self.V[:, bass.ds(cb + col, 1)], ALU.mult, ALU.add)
                    else:
                        t = 0 if tap == 1 else 2
                        ins = eng.scalar_tensor_tensor(
                            out=seg(dst, olo, ohi), in0=seg(src, ilo, ihi),
                            scalar=self.V[:, bass.ds(cw + t * 2 * FT + col, 1)],
                            in1=seg(dst, olo, ohi), op0=ALU.mult, op1=ALU.add)
                if tap < 2:
                    ins.then_inc(link, 1)
                    eng.wait_ge(link, f * 2 + tap + 1)
            ins.then_inc(up_used, 1)

        def mult(f, e):
            eng.wait_ge(gate_out, f + 1)
            eng.wait_ge(up_used, f + 1)
            eng.tensor_tensor(hid[:, bass.ds(f, 1), 0:w].rearrange("p a t -> p (a t)"), u[e][0], sg[e],
                              ALU.mult).then_inc(hid_done, 1)
            eng.wait_ge(hid_done, f + 1)

        if who == "dve":
            conv(0, 0)
            with eng.Fori(0, FT // 2 - 1) as it:
                conv(it * 2 + 1, 1)
                mult(it * 2, 0)
                conv(it * 2 + 2, 0)
                mult(it * 2 + 1, 1)
            conv(FT - 1, 1)
            mult(FT - 2, 0)
            mult(FT - 1, 1)
        if who == "act":
            with eng.Fori(0, FT // 2) as it:
                for e in range(2):
                    f = it * 2 + e
                    eng.wait_ge(up_used, f + 1)
                    eng.activation(sg[e], u[e][1], ACT.Silu).then_inc(gate_out, 1)
        self.phase_end(eng, who)
        nm = f"ffn_out{layer}"
        self.project_residual(who, eng, nm, lambda k: hid[:, k, 0:w], FT, 2, 5, layer, segs)
        self.layer_norm(who, eng, c0, "ln2_g", "ln2_b", layer)
        if layer == 0:
            self.modulate(who, eng, 1, 0, 1, (0, 1))

    def na_views(self):
        b, v, at = self.B, {}, 0
        for name, n in (("q0", 2 * LAT), ("q1", 2 * LAT), ("k0", T), ("k1", T), ("v0", 4 * P), ("v1", 4 * P),
                        ("p", 4 * T), ("pt", 4 * T), ("o", 2 * D)):
            v[name] = b[:, at:at + n]
            at += n
        assert at <= FT * T
        return v

    def na_heads(self, who, eng):
        v = self.na_views()
        names = ("proj_done", "q_copied", "k_copied", "v_copied", "scored", "biased", "max_ready", "exp_done",
                 "turned", "pt_copied", "o_done", "o_used")
        s = {n: self.sem("na_" + n) for n in names}
        link = self.sem("na_link")
        bank = self.bank
        scale = 64 ** -0.5
        g0 = FIRST["na_pair"]
        sc = self.X[:, 0:4 * T].rearrange("p (n k) -> p n k", n=4)
        p = v["p"].rearrange("p (n k) -> p n k", n=4)
        pt = v["pt"].rearrange("p (n b q) -> p n b q", n=4, q=P)
        qz = [v[f"q{e}"].rearrange("p (h t) -> p h t", h=2) for e in range(2)]
        o = v["o"].rearrange("p (t d) -> p t d", t=2)
        nb_all = self.N[:, :].rearrange("p (t h k) -> p t h k", t=2, h=16)
        mx, nb, rs, rc = [[self.S[:, 64 + 16 * e + 4 * n:64 + 16 * e + 4 * n + 4] for e in range(2)]
                          for n in range(4)]
        pt_bank = (7, 3, 4, 5)
        if who == "dve":
            eng.wait_ge(self.bias_in, 64)
            for t in range(2):
                eng.tensor_tensor(nb_all[:, t, :, :], nb_all[:, t, :, :],
                                  self.con("na_mask").unsqueeze(1).to_broadcast([P, 16, LAT]), ALU.add)
            for e in range(2):
                eng.memset(qz[e], 0.0)
        self.phase_end(eng, who)

        def pe_project(u, e):
            slot = self.ring[(g0 + e) % 2]
            eng.wait_ge(self.w_loaded[(g0 + e) % 2], (u - e) * 8 + 16 * ((g0 + e) // 2 + 1))
            if not (isinstance(u, int) and u == 0):
                eng.wait_ge(s["q_copied"], u)
                eng.wait_ge(s["k_copied"], u)
                eng.wait_ge(s["v_copied"], u)
            self.mm(eng, bank[0][:, 0:LAT], [slot[:, k * P:(k + 1) * P] for k in range(KT)],
                    [self.A[:, k, CTX:T] for k in range(KT)])
            self.mm(eng, bank[1][:, :], [slot[:, D + k * P:D + (k + 1) * P] for k in range(KT)],
                    [self.A[:, k, :] for k in range(KT)])
            for t in range(4):
                last = self.mm(eng, bank[2][:, t * P:(t + 1) * P],
                               [self.A[:, k, t * P:(t + 1) * P] for k in range(KT)],
                               [slot[:, 2 * D + k * P:2 * D + (k + 1) * P] for k in range(KT)])
            last.then_inc(s["proj_done"], 1)

        def pe_scores(u, e):
            eng.wait_ge(s["q_copied"], u + 1)
            eng.wait_ge(s["k_copied"], u + 1)
            eng.wait_ge(s["o_used"], u + 1)
            for n in range(4):
                h, t = n // 2, n % 2
                eng.matmul(bank[3 + n][:, :], qz[e][:, h, t * P:(t + 1) * P], v[f"k{e}"],
                           start=True, stop=True).then_inc(s["scored"], 1)

        def pe_tail(u, e):
            for n in range(4):
                eng.wait_ge(s["exp_done"], 4 * u + n + 1)
                for b in range(4):
                    last = eng.transpose(bank[pt_bank[n]][:, b * P:(b + 1) * P], p[:, n, b * P:(b + 1) * P],
                                         self.con("ident"))
                last.then_inc(s["turned"], 1)
            eng.wait_ge(s["v_copied"], u + 1)
            vv = v[f"v{e}"].rearrange("p (t d) -> p t d", t=4)
            for n in range(4):
                eng.wait_ge(s["pt_copied"], 4 * u + n + 1)
                h = n // 2
                last = self.mm(eng, bank[6][:, n * 64:(n + 1) * 64], [pt[:, n, b, :] for b in range(4)],
                               [vv[:, b, h * 64:(h + 1) * 64] for b in range(4)])
            last.then_inc(s["o_done"], 1)

        def dve_project(u, e):
            eng.wait_ge(s["proj_done"], u + 1)
            eng.tensor_copy(qz[e][0:64, 0, :], bank[0][0:64, 0:LAT])
            eng.tensor_copy(qz[e][64:128, 1, :], bank[0][64:128, 0:LAT]).then_inc(s["q_copied"], 1)

        def dve_max(u, e):
            for n in range(4):
                h, t = n // 2, n % 2
                eng.wait_ge(s["scored"], 4 * u + n + 1)
                eng.tensor_scalar(sc[:, n, 0:CTX], bank[3 + n][:, 0:CTX], scale, None, ALU.mult)
                bias = nb_all[:, t, bass.ds(u * 2 + h, 1), :].rearrange("p a k -> p (a k)")
                eng.scalar_tensor_tensor(out=sc[:, n, CTX:T], in0=bank[3 + n][:, CTX:T], scalar=scale,
                                         in1=bias, op0=ALU.mult, op1=ALU.add).then_inc(s["biased"], 1)
            eng.wait_ge(s["biased"], 4 * u + 4)
            eng.tensor_reduce(mx[e], sc, AX.X, ALU.max).then_inc(link, 1)
            eng.wait_ge(link, 2 * u + 1)
            eng.tensor_scalar(nb[e], mx[e], -1.0, None, ALU.mult).then_inc(s["max_ready"], 1)

        def dve_tail(u, e):
            eng.wait_ge(s["exp_done"], 4 * u + 4)
            eng.reciprocal(rc[e], rs[e]).then_inc(link, 1)
            for n in range(4):
                eng.wait_ge(s["turned"], 4 * u + n + 1)
                eng.tensor_copy(v["pt"][:, n * T:(n + 1) * T], bank[pt_bank[n]][:, :])\
                    .then_inc(s["pt_copied"], 1)
            eng.wait_ge(s["o_done"], u + 1)
            eng.wait_ge(link, 2 * u + 2)
            for h in range(2):
                ins = eng.tensor_tensor(o[:, :, bass.ds(u * P + h * 64, 64)],
                                        bank[6][:, h * P:(h + 1) * P].rearrange("p (t d) -> p t d", t=2),
                                        rc[e][:, 2 * h:2 * h + 2].unsqueeze(2).to_broadcast([P, 2, 64]),
                                        ALU.mult)
            ins.then_inc(s["o_used"], 1)

        def act_project(u, e):
            eng.wait_ge(s["proj_done"], u + 1)
            eng.copy(v[f"k{e}"], bank[1][:, :]).then_inc(s["k_copied"], 1)
            eng.copy(v[f"v{e}"], bank[2][:, :]).then_inc(s["v_copied"], 1)

        def act_exp(u, e):
            eng.wait_ge(s["max_ready"], u + 1)
            for n in range(4):
                eng.activation(p[:, n, :], sc[:, n, :], ACT.Exp, bias=nb[e][:, n:n + 1], scale=1.0,
                               accum_out=rs[e][:, n:n + 1]).then_inc(s["exp_done"], 1)

        def act_tail(u, e):
            pass

        steps = {"pe": (pe_project, pe_scores, pe_tail), "dve": (dve_project, dve_max, dve_tail),
                 "act": (act_project, act_exp, act_tail)}[who]
        if who == "dve":
            eng.nop().then_inc(s["o_used"], 1)
        self.pipelined(eng, NA_PAIRS, *steps)
        self.phase_end(eng, who)

    def na_out(self, who, eng):
        v = self.na_views()
        o = v["o"].rearrange("p (t d) -> p t d", t=2)
        oT = self.X[:, 512:512 + KT * LAT].rearrange("p (k t) -> p k t", k=KT)
        self.flip(who, eng, lambda t, k: o[:, t, k * P:(k + 1) * P], lambda k: oT[:, k, :], KT, 2, "na")
        self.project_residual(who, eng, "na_o", lambda k: oT[:, k, :], KT, 4, 2, 1, (1,))
        self.layer_norm(who, eng, CTX, "ln1_g", "ln1_b", 1)

    def rms_to_input(self, who, eng, gain):
        def write(k, x, r):
            a = self.A[:, k, CTX:T]
            self.link(eng, who, eng.tensor_tensor(a, x, r, ALU.mult))
            self.link(eng, who, eng.tensor_scalar(a, a, self.vec(gain, k, 1), None, ALU.mult))
        self.norm(who, eng, CTX, write, centre=False, eps=RMS_EPS)

    def tile2(self, t, n=1):
        return self.B[:, t * LAT:(t + n) * LAT]

    def proj(self, who, eng):
        self.rms_to_input(who, eng, "attn_norm")
        done, used = self.sem("proj_tile_done"), self.sem("proj_tile_used")
        if who == "pe":
            def body(j, slot):
                for t in range(6):
                    if not (isinstance(j, int) and j == 0):
                        eng.wait_ge(used, j * 6 + t - 5)
                    last = self.mm(eng, self.bank[t][:, 0:LAT],
                                   [slot[:, (t * KT + k) * P:(t * KT + k + 1) * P] for k in range(KT)],
                                   [self.A[:, k, CTX:T] for k in range(KT)])
                    last.then_inc(done, 1)
            g = FIRST["proj"]
            eng.wait_ge(self.w_loaded[g % 2], 16 * (g // 2 + 1))
            body(0, self.ring[g % 2])
            self.chunks(eng, "proj", body, count=CHUNKS["proj"] - 1, start=1)
            for t in range(2):
                self.mm(eng, self.bank[6][:, t * 24:(t + 1) * 24],
                        [self.A[:, k, CTX + t * P:CTX + (t + 1) * P] for k in range(KT)],
                        [self.vec("w_gate24", k * 24, 24) for k in range(KT)])
        if who == "dve":
            with eng.Fori(0, CHUNKS["proj"]) as j:
                for t in range(6):
                    eng.wait_ge(done, j * 6 + t + 1)
                    eng.tensor_copy(self.B[:, bass.ds(j * (6 * LAT) + t * LAT, LAT)], self.bank[t][:, 0:LAT])\
                        .then_inc(used, 1)
        self.phase_end(eng, who)
        if who == "act":
            eng.activation(self.S[:, 0:48], self.bank[6][:, 0:48], ACT.Sigmoid)
            eng.activation(self.tile2(T_HF, 4), self.tile2(T_HF, 4), ACT.Sigmoid)
            eng.activation(self.tile2(T_MN, 16), self.tile2(T_MN, 16), ACT.Sigmoid)
            eng.activation(self.tile2(T_HGATE, 4), self.tile2(T_HGATE, 4), ACT.Silu)
        self.phase_end(eng, who)

    def nsa_views(self):
        n, x, v, at = self.N, self.X, {}, 0
        for name, w in (("qr", 4 * LAT), ("sk", LAT), ("wk", LAT), ("kc", 16), ("vc", P), ("vtok", 12 * P),
                        ("qz0", 2 * LAT // 2), ("qz1", 2 * LAT // 2), ("o_hg", 4 * LAT),
                        ("s0", 800), ("s1", 800), ("p0", 800), ("p1", 800)):
            v[name] = n[:, at:at + w]
            at += w
        assert at <= 16 * 2 * LAT, at
        v["at"] = v["s0"].offset
        at = 0
        for name, w in (("pt", 16 * P), ("o", 2 * 512), ("t0", 384), ("t1", 384)):
            v[name] = x[:, at:at + w]
            at += w
        assert at <= KT * T
        return v

    def compress(self, who, eng):
        v = self.nsa_views()
        bank = self.bank
        blk = [self.A[:, :, :].rearrange("p k t -> p (k t)")[:, 512 * x:512 * x + NCMP * 32]
               .rearrange("p (n l) -> p n l", l=32) for x in range(2)]
        vct = self.S[:, 48:64]
        if who == "dve":
            for x, tile in enumerate((T_CK, T_CV)):
                rows = self.tile2(tile).rearrange("p (n b) -> p n b", b=16)
                for a in range(2):
                    pos = self.vec("cmp_pos", 16 * a, 16).unsqueeze(1).to_broadcast([P, NCMP, 16])
                    eng.tensor_tensor(blk[x][:, :, 16 * a:16 * a + 16], rows[:, a:a + NCMP, :], pos, ALU.add)
            eng.memset(v["kc"], 0.0)
            eng.memset(vct, 0.0)
        self.phase_end(eng, who)
        tiles = [T_Q, T_Q + 1, T_Q + 2, T_Q + 3, T_SK, T_WK]
        turn = [T_SV, T_WV, T_HI, T_HI + 1, T_HI + 2, T_HI + 3]
        vtok = v["vtok"].rearrange("p (t m d) -> p t m d", t=2, m=6)
        if who == "pe":
            for x in range(2):
                g = FIRST["cmp"] + x
                eng.wait_ge(self.w_loaded[g % 2], 16 * (g // 2 + 1))
                slot = self.ring[g % 2]
                self.mm(eng, bank[x][:, 0:NCMP], [slot[:, l * P:(l + 1) * P] for l in range(32)],
                        [blk[x][:, :, l] for l in range(32)]).then_inc(self.sem("cmp_used"), 1)
            for i, t in enumerate(tiles):
                eng.matmul(bank[2 + i // 2][:, (i % 2) * LAT:(i % 2 + 1) * LAT], self.con("rot_nsa"),
                           self.tile2(t), start=True, stop=True)
            for i, t in enumerate(turn):
                for tt in range(2):
                    b = 5 + i // 2
                    c = (i % 2) * LAT + tt * P
                    eng.transpose(bank[b][:, c:c + P], self.tile2(t)[:, tt * P:(tt + 1) * P], self.con("ident"))
        self.phase_end(eng, who)
        if who == "dve":
            eng.tensor_copy(v["kc"][:, 0:NCMP], bank[0][:, 0:NCMP])
            eng.tensor_copy(vct[:, 0:NCMP], bank[1][:, 0:NCMP])
            for i, t in enumerate(tiles):
                dst = v["qr"][:, i * LAT:(i + 1) * LAT] if i < 4 else v["sk" if i == 4 else "wk"]
                src = self.tile2(t)
                self.link(eng, who, eng.tensor_tensor(src, src, self.con("cos_nsa"), ALU.mult))
                self.link(eng, who, eng.tensor_tensor(dst, bank[2 + i // 2][:, (i % 2) * LAT:(i % 2 + 1) * LAT],
                                                      self.con("sin_nsa"), ALU.mult))
                self.link(eng, who, eng.tensor_tensor(dst, dst, src, ALU.add))
        if who == "act":
            for i in range(6):
                for tt in range(2):
                    c = (i % 2) * LAT + tt * P
                    eng.copy(vtok[:, tt, i, :], bank[5 + i // 2][:, c:c + P])
        self.phase_end(eng, who)
        if who == "pe":
            eng.matmul(bank[0][:, 0:16], self.con("rot_nsa"), v["kc"], start=True, stop=True)
            eng.transpose(bank[1][0:16, 0:P], vct, self.con("ident"))
        self.phase_end(eng, who)
        if who == "dve":
            at16 = [self.con(c).rearrange("p (n b) -> p n b", b=16)[:, :, 0] for c in ("cos_nsa", "sin_nsa")]
            tmp = self.S[:, 64:80]
            self.link(eng, who, eng.tensor_tensor(tmp, bank[0][:, 0:16], at16[1], ALU.mult))
            self.link(eng, who, eng.tensor_tensor(v["kc"], v["kc"], at16[0], ALU.mult))
            eng.tensor_tensor(v["kc"], v["kc"], tmp, ALU.add)
            eng.tensor_copy(v["vc"][0:16, :], bank[1][0:16, 0:P])
            eng.memset(v["qz0"], 0.0)
            eng.memset(v["qz1"], 0.0)
        self.phase_end(eng, who)

    def nsa_heads(self, who, eng):
        v = self.nsa_views()
        names = ("q_ready", "scored", "max_ready", "exp_done", "kept", "turned", "pt_copied", "o_done")
        s = {n: self.sem("nsa_" + n) for n in names}
        link = self.sem("nsa_link")
        bank = self.bank
        scale = 64 ** -0.5
        qz = [v["qz0"], v["qz1"]]
        sc, p = [v["s0"], v["s1"]], [v["p0"], v["p1"]]
        pt = v["pt"].rearrange("p (e b q) -> p e b q", e=2, q=P)
        o = v["o"].rearrange("p (t d) -> p t d", t=2)
        tmp = [v[f"t{e}"].rearrange("p (b t d) -> p b t d", b=3, t=2) for e in range(2)]
        vtok = v["vtok"].rearrange("p (t m d) -> p t m d", t=2, m=6)
        mx, nb, rs, fc = [[self.S[:, 64 + 32 * e + 6 * n:64 + 32 * e + 6 * n + 6] for e in range(2)]
                          for n in range(4)]
        segs = [(0, 128), (128, 384), (384, 400), (400, 416), (416, 544), (544, 800)]
        sb = [(3, 4), (5, 6)]
        tb = [(7, 0), (1, 2)]
        blocks = [(0, 128), (128, 256), (256, 384), (384, 400), (416, 544), (544, 672), (672, 800), (400, 416)]
        gates = self.S[:, 0:48].rearrange("p (t c) -> p t c", t=2)
        LINKS = 8
        with eng.Fori(0, NSA_PAIRS) as it:
            if who == "pe":
                eng.wait_ge(s["q_ready"], it + 1)
                for e in range(2):
                    a, b = (bank[i] for i in sb[e])
                    q = qz[e]
                    for k, bk in ((v["sk"], a), (v["wk"], b)):
                        eng.matmul(bk[:, 0:128], q[:, 0:P], k[:, 0:P], start=True, stop=True)
                        last = eng.matmul(bk[:, 128:384], q[:, P:LAT], k, start=True, stop=True)
                    for t in range(2):
                        last = eng.matmul(a[:, 384 + 16 * t:400 + 16 * t], q[:, t * P:(t + 1) * P], v["kc"],
                                          start=True, stop=True)
                    last.then_inc(s["scored"], 1)
                for e in range(2):
                    eng.wait_ge(s["kept"], it * 2 + e + 1)
                    for i, (lo, hi) in enumerate(blocks):
                        last = eng.transpose(bank[tb[e][i // 4]][0:hi - lo, (i % 4) * P:(i % 4 + 1) * P],
                                             p[e][:, lo:hi], self.con("ident"))
                    last.then_inc(s["turned"], 1)
                for e in range(2):
                    eng.wait_ge(s["pt_copied"], it * 4 + 2 * e + 2)
                    ob = bank[sb[e][0]]
                    g = slice(64 * e, 64 * e + 64)

                    def out(i):
                        return ob[:, i * 64:(i + 1) * 64]
                    for br, m, b0 in ((0, 0, 0), (2, 1, 4)):
                        eng.matmul(out(2 * br), pt[:, e, b0, :], vtok[:, 0, m, g], start=True, stop=True)
                        self.mm(eng, out(2 * br + 1), [pt[:, e, b0 + 1, :], pt[:, e, b0 + 2, :]],
                                [vtok[:, 0, m, g], vtok[:, 1, m, g]])
                    for t in range(2):
                        last = eng.matmul(out(2 + t), pt[0:16, e, (3, 7)[t], :], v["vc"][0:16, g],
                                          start=True, stop=True)
                    last.then_inc(s["o_done"], 1)
            if who == "dve":
                for e in range(2):
                    r = slice(64 * e, 64 * e + 64)
                    last = eng.tensor_copy(qz[e][r, :], v["qr"][r, bass.ds(it * LAT, LAT)])
                last.then_inc(s["q_ready"], 1)
                for e in range(2):
                    eng.wait_ge(s["scored"], it * 2 + e + 1)
                    eng.scalar_tensor_tensor(out=sc[e][:, 0:416], in0=bank[sb[e][0]][:, 0:416], scalar=scale,
                                             in1=self.con("nsa_mask"), op0=ALU.mult, op1=ALU.add)
                    eng.scalar_tensor_tensor(out=sc[e][:, 416:800], in0=bank[sb[e][1]][:, 0:384],
                                             scalar=scale, in1=self.con("nsa_mask", 0, 384), op0=ALU.mult,
                                             op1=ALU.add).then_inc(link, 1)
                    eng.wait_ge(link, it * LINKS + 2 * e + 1)
                    for i, (lo, hi) in enumerate(segs):
                        last = eng.tensor_reduce(mx[e][:, i:i + 1], sc[e][:, lo:hi], AX.X, ALU.max)
                    last.then_inc(link, 1)
                    eng.wait_ge(link, it * LINKS + 2 * e + 2)
                    eng.tensor_scalar(nb[e], mx[e], -1.0, None, ALU.mult).then_inc(s["max_ready"], 1)
                for e in range(2):
                    eng.wait_ge(s["exp_done"], it * 2 + e + 1)
                    eng.tensor_tensor(p[e][:, 384:416], p[e][:, 384:416], self.con("cmp_keep"), ALU.mult)\
                        .then_inc(s["kept"], 1)
                    eng.reciprocal(fc[e], rs[e]).then_inc(link, 1)
                    eng.wait_ge(link, it * LINKS + 2 * e + 5)
                    f = fc[e].rearrange("p (b t) -> p b t", t=2)
                    eng.tensor_tensor(f, f, gates[:, :, bass.ds(it * 6 + 3 * e, 3)].rearrange("p t b -> p b t"),
                                      ALU.mult).then_inc(link, 1)
                for e in range(2):
                    eng.wait_ge(s["turned"], it * 2 + e + 1)
                    for half in range(2):
                        eng.tensor_copy(pt[:, e, 4 * half:4 * half + 3, :],
                                        bank[tb[e][half]][:, 0:384].rearrange("p (b q) -> p b q", q=P))
                        eng.tensor_copy(pt[0:16, e, 4 * half + 3, :], bank[tb[e][half]][0:16, 384:512])\
                            .then_inc(s["pt_copied"], 1)
                for e in range(2):
                    eng.wait_ge(s["o_done"], it * 2 + e + 1)
                    eng.wait_ge(link, it * LINKS + 2 * e + 6)
                    eng.tensor_tensor(v[f"t{e}"].rearrange("p (i d) -> p i d", d=64),
                                      bank[sb[e][0]][:, 0:384].rearrange("p (i d) -> p i d", d=64),
                                      fc[e].unsqueeze(2).to_broadcast([P, 6, 64]), ALU.mult)\
                        .then_inc(self.sem("nsa_weighted"), 1)
                    eng.wait_ge(self.sem("nsa_weighted"), it * 4 + 2 * e + 1)
                    dst = o[:, :, bass.ds(it * 64 + 256 * e, 64)]
                    eng.tensor_tensor(tmp[e][:, 0, :, :], tmp[e][:, 0, :, :], tmp[e][:, 1, :, :], ALU.add)\
                        .then_inc(self.sem("nsa_weighted"), 1)
                    eng.wait_ge(self.sem("nsa_weighted"), it * 4 + 2 * e + 2)
                    eng.tensor_tensor(dst, tmp[e][:, 0, :, :], tmp[e][:, 2, :, :], ALU.add)
            if who == "act":
                for e in range(2):
                    eng.wait_ge(s["max_ready"], it * 2 + e + 1)
                    for i, (lo, hi) in enumerate(segs):
                        last = eng.activation(p[e][:, lo:hi], sc[e][:, lo:hi], ACT.Exp, bias=nb[e][:, i:i + 1],
                                              scale=1.0, accum_out=rs[e][:, i:i + 1])
                    last.then_inc(s["exp_done"], 1)
        self.phase_end(eng, who)

    def hgrn(self, who, eng):
        v = self.nsa_views()
        bank = self.bank
        af = self.A[:, :, :].rearrange("p k t -> p (k t)")
        logf, K, E, KL = [af[:, 1024 * i:1024 * (i + 1)] for i in range(4)]
        QL = self.X[:, 0:1024]
        b = self.X[:, 3072:4096]
        n0 = 16 * 2 * LAT - 3 * 1024
        diag = self.N[:, n0:n0 + 1024]
        tmp = self.N[:, n0 + 1024:n0 + 2048]
        off = self.N[:, n0 + 2048:n0 + 2560]
        q, f = self.tile2(T_HQ, 4), self.tile2(T_HF, 4)
        o = v["o_hg"]
        vtok = v["vtok"].rearrange("p (t m d) -> p t m d", t=2, m=6)
        lo = self.S[:, 64:96]
        if who == "dve":
            a0, a1 = self.vec("hg_lb", 0, HG), self.vec("hg_lb", HG, HG)
            self.link(eng, who, eng.tensor_tensor(lo[:, 8:12], a0, a1, ALU.max))
            eng.tensor_tensor(lo[:, 0:4], a0, lo[:, 8:12], ALU.subtract)
            eng.tensor_tensor(lo[:, 4:8], a1, lo[:, 8:12], ALU.subtract)
        self.phase_end(eng, who)
        if who == "act":
            eng.activation(lo[:, 0:8], lo[:, 0:8], ACT.Exp)
        self.phase_end(eng, who)
        if who == "dve":
            self.link(eng, who, eng.tensor_tensor(lo[:, 8:12], lo[:, 0:4], lo[:, 4:8], ALU.add))
            self.link(eng, who, eng.reciprocal(lo[:, 8:12], lo[:, 8:12]))
            self.link(eng, who, eng.tensor_tensor(lo[:, 0:4], lo[:, 0:4], lo[:, 8:12], ALU.mult))
            self.link(eng, who, eng.tensor_scalar(lo[:, 4:8], lo[:, 0:4], -1.0, 1.0, ALU.mult, ALU.add))
            for h in range(HG):
                fh = f[:, h * LAT:(h + 1) * LAT]
                last = eng.tensor_scalar(fh, fh, lo[:, 4 + h:5 + h], lo[:, h:h + 1], ALU.mult, ALU.add)
            self.link(eng, who, last)
            eng.tensor_scalar(K, f, -1.0, 1.0, ALU.mult, ALU.add)
        self.phase_end(eng, who)
        if who == "act":
            eng.activation(logf, f, ACT.Ln)
        self.phase_end(eng, who)
        if who == "dve":
            for h in range(HG):
                c = slice(h * LAT, (h + 1) * LAT)
                last = eng.tensor_tensor_scan(b[:, c], self.con("scan_keep"), logf[:, c], 0.0,
                                              ALU.mult, ALU.add)
            self.link(eng, who, last)

        def exponents(level):
            if level == 128:
                bb, ee = [x.rearrange("p (h c t) -> p h c t", h=HG, c=4) for x in (b, E)]
                end = lambda c: bb[:, :, c, 63:64].to_broadcast([P, HG, 64])
                eng.tensor_tensor(ee[:, :, 1, :], end(1), bb[:, :, 1, :], ALU.subtract)
                self.link(eng, who, eng.tensor_tensor(ee[:, :, 0, :], end(0), bb[:, :, 0, :], ALU.subtract))
                eng.tensor_tensor(ee[:, :, 0, :], ee[:, :, 0, :], end(1), ALU.add)
                eng.tensor_copy(ee[:, :, 2, :], bb[:, :, 2, :])
                return eng.tensor_tensor(ee[:, :, 3, :], bb[:, :, 3, :], end(2), ALU.add)
            m = level
            bb, ee = [x.rearrange("p (n s t) -> p n s t", s=2, t=m) for x in (b, E)]
            n = 1024 // (2 * m)
            ref = bb[:, :, 0, m - 1:m].to_broadcast([P, n, m])
            eng.tensor_tensor(ee[:, :, 0, :], ref, bb[:, :, 0, :], ALU.subtract)
            if m == 64:
                return eng.tensor_copy(ee[:, :, 1, :], bb[:, :, 1, :])
            return eng.tensor_tensor(ee[:, :, 1, :], bb[:, :, 1, :], ref, ALU.subtract)

        e_ready, x_ready, kq_ready, mm_done = \
            [self.sem("hg_" + x) for x in ("exponents", "decays", "decayed", "products")]
        levels = [128] + LEVELS
        nl = len(levels)
        if who == "dve":
            exponents(128).then_inc(e_ready, 1)
            for i in range(nl + 1):
                if i < nl:
                    eng.wait_ge(x_ready, i + 1)
                    eng.tensor_tensor(KL, K, E, ALU.mult)
                    eng.tensor_tensor(QL, q, E, ALU.mult).then_inc(kq_ready, 1)
                if i + 1 < nl:
                    eng.wait_ge(kq_ready, i + 1)
                    exponents(levels[i + 1]).then_inc(e_ready, 1)
                eng.wait_ge(mm_done, i + 1)
                if i == 0:
                    eng.tensor_copy(off, bank[0][:, :])
                    continue
                mask = self.con("level_mask", (i - 1) * P, P).unsqueeze(1).to_broadcast([P, 4, P])
                for half in range(2):
                    src = bank[2 * (i % 2) + half][:, :].rearrange("p (n t) -> p n t", n=4)
                    dst = (diag if i == 1 else tmp)[:, 512 * half:512 * half + 512]
                    last = eng.tensor_tensor(dst.rearrange("p (n t) -> p n t", n=4), src, mask, ALU.mult)
                self.link(eng, who, last)
                if i > 1:
                    self.link(eng, who, eng.tensor_tensor(diag, diag, tmp, ALU.add))
        if who == "act":
            for i in range(nl):
                eng.wait_ge(e_ready, i + 1)
                eng.activation(E, E, ACT.Exp).then_inc(x_ready, 1)
        if who == "pe":
            for i in range(nl + 1):
                if i < nl:
                    eng.wait_ge(kq_ready, i + 1)
                kk, qq = (KL, QL) if i < nl else (K, q)
                for h in range(HG):
                    if i == 0:
                        last = eng.matmul(bank[0][:, h * P:(h + 1) * P], kk[:, h * LAT:h * LAT + P],
                                          qq[:, h * LAT + P:(h + 1) * LAT], start=True, stop=True)
                        continue
                    for st in range(2):
                        c = slice(h * LAT + st * P, h * LAT + (st + 1) * P)
                        j = 2 * h + st
                        last = eng.matmul(bank[2 * (i % 2) + j // 4][:, (j % 4) * P:(j % 4 + 1) * P],
                                          kk[:, c], qq[:, c], start=True, stop=True)
                last.then_inc(mm_done, 1)
        self.phase_end(eng, who)
        if who == "pe":
            for h in range(HG):
                ob = bank[4 + h // 2][:, (h % 2) * LAT:(h % 2 + 1) * LAT]
                eng.matmul(ob[:, 0:P], vtok[:, 0, 2 + h, :], diag[:, 2 * h * P:(2 * h + 1) * P],
                           start=True, stop=True)
                self.mm(eng, ob[:, P:LAT], [vtok[:, 0, 2 + h, :], vtok[:, 1, 2 + h, :]],
                        [off[:, h * P:(h + 1) * P], diag[:, (2 * h + 1) * P:(2 * h + 2) * P]])
        self.phase_end(eng, who)
        if who == "act":
            for i in range(2):
                eng.activation(KL[:, 512 * i:512 * i + 512], bank[4 + i][:, :], ACT.Square)
        self.phase_end(eng, who)
        if who == "pe":
            for i in range(2):
                eng.matmul(bank[i][:, :], self.con("ones"), KL[:, 512 * i:512 * i + 512], start=True, stop=True)
        self.phase_end(eng, who)
        if who == "dve":
            for i in range(2):
                eng.tensor_scalar(QL[:, 512 * i:512 * i + 512], bank[i][:, :], 1.0 / P, RMS_EPS,
                                  ALU.mult, ALU.add)
        self.phase_end(eng, who)
        if who == "act":
            eng.activation(QL, QL, ACT.Sqrt)
        self.phase_end(eng, who)
        if who == "dve":
            self.link(eng, who, eng.reciprocal(QL, QL))
            for i in range(2):
                c = slice(512 * i, 512 * i + 512)
                last = eng.tensor_tensor(o[:, c], bank[4 + i][:, :], QL[:, c], ALU.mult)
            self.link(eng, who, last)
            self.link(eng, who, eng.scalar_tensor_tensor(out=o, in0=o, scalar=self.vec("hg_norm"),
                                                         in1=self.tile2(T_HGATE, 4), op0=ALU.mult, op1=ALU.mult))
        self.phase_end(eng, who)

    def branches(self, who, eng):
        v = self.nsa_views()
        o = v["o"].rearrange("p (t d) -> p t d", t=2)
        oT = v["qr"].rearrange("p (k t) -> p k t", k=4)
        oh = v["o_hg"].rearrange("p (k t) -> p k t", k=4)
        self.flip(who, eng, lambda t, k: o[:, t, k * P:(k + 1) * P], lambda k: oT[:, k, :], 4, 2, "nsa")
        done, used = self.sem("branch_done"), self.sem("branch_used")
        bank = self.bank
        mixed = self.B[:, 0:KT * LAT].rearrange("p (k t) -> p k t", k=KT)
        tmp = self.X[:, 0:LAT]
        if who == "pe":
            g = FIRST["branch"]
            for s in range(2):
                eng.wait_ge(self.w_loaded[(g + s) % 2], 16 * ((g + s) // 2 + 1))
            for oc in range(KT):
                if oc >= 2:
                    eng.wait_ge(used, oc - 1)
                for s, r in enumerate((oT, oh)):
                    slot = self.ring[(g + s) % 2]
                    last = self.mm(eng, bank[2 * (oc % 2) + s][:, 0:LAT],
                                   [slot[:, (oc * 4 + k) * P:(oc * 4 + k + 1) * P] for k in range(4)],
                                   [r[:, k, :] for k in range(4)])
                last.then_inc(done, 1)
        if who == "dve":
            for oc in range(KT):
                eng.wait_ge(done, oc + 1)
                self.link(eng, who, eng.tensor_tensor(tmp, bank[2 * (oc % 2)][:, 0:LAT], self.tile2(T_MN + oc),
                                                      ALU.mult))
                eng.tensor_tensor(mixed[:, oc, :], bank[2 * (oc % 2) + 1][:, 0:LAT], self.tile2(T_MH + oc),
                                  ALU.mult).then_inc(used, 1)
                eng.wait_ge(used, oc + 1)
                self.link(eng, who, eng.tensor_tensor(mixed[:, oc, :], mixed[:, oc, :], tmp, ALU.add))
        self.phase_end(eng, who)
        self.project_residual(who, eng, "w_out", lambda k: mixed[:, k, :], KT, 4, None, 0, (1,))

    def router(self, who, eng):
        self.rms_to_input(who, eng, "ffn_norm")
        if who == "pe":
            for t in range(2):
                self.mm(eng, self.bank[0][:, t * 36:(t + 1) * 36],
                        [self.A[:, k, CTX + t * P:CTX + (t + 1) * P] for k in range(KT)],
                        [self.vec("w_route", k * 36, 36) for k in range(KT)])
        self.phase_end(eng, who)
        x = self.X
        lg = x[:, 0:72].rearrange("p (t c) -> p t c", t=2)
        at = [72]

        def small(*shape):
            n = 2 * int(np.prod(shape)) if shape else 2
            r = x[:, at[0]:at[0] + n]
            at[0] += n
            return r.rearrange("p (t c) -> p t c", t=2)
        gm, ge, gs, gp = small(1), small(4), small(1), small(1)
        oneg, pref, pm = small(4), small(8), small(1)
        sel, ing = small(32), small(8)
        m1, o1, m2, o2, x2 = small(1), small(8), small(1), small(8), small(8)
        d, w1, w2 = small(1), small(1), small(1)
        comb = small(8)
        C = self.S[:, 0:64].rearrange("p (t g c) -> p t g c", t=2, g=GROUPS)

        def L(ins):
            self.link(eng, who, ins)

        def one_hot(dst, src, m, first, n):
            pr = pref[:, :, 0:n]
            L(eng.tensor_tensor(dst, src, m.to_broadcast([P, 2, n]), ALU.is_equal))
            L(eng.tensor_tensor(pr, dst, self.con(first).unsqueeze(1).to_broadcast([P, 2, n]), ALU.mult))
            L(eng.tensor_reduce(pm, pr, AX.X, ALU.max))
            L(eng.tensor_tensor(dst, pr, pm.to_broadcast([P, 2, n]), ALU.is_equal))
        if who == "dve":
            br = self.vec("b_route").unsqueeze(1).to_broadcast([P, 2, 36])
            L(eng.tensor_tensor(lg, self.bank[0][:, 0:72].rearrange("p (t c) -> p t c", t=2), br, ALU.add))
            gl, el = lg[:, :, 0:4], lg[:, :, 4:36].rearrange("p t (g c) -> p t g c", g=GROUPS)
            L(eng.tensor_reduce(gm, gl, AX.X, ALU.max))
            L(eng.tensor_tensor(ge, gl, gm.to_broadcast([P, 2, 4]), ALU.subtract))
            one_hot(oneg, gl, gm, "first4", 4)
            s4 = sel.rearrange("p t (g c) -> p t g c", g=GROUPS)
            for t in range(2):
                L(eng.tensor_tensor(s4[:, t, :, :], el[:, t, :, :],
                                    oneg[:, t, :].unsqueeze(2).to_broadcast([P, 4, 8]), ALU.mult))
                L(eng.tensor_reduce(ing[:, t, :], s4[:, t, :, :].rearrange("p g c -> p c g"), AX.X, ALU.add))
            L(eng.tensor_reduce(m1, ing, AX.X, ALU.max))
            one_hot(o1, ing, m1, "first8", 8)
            L(eng.scalar_tensor_tensor(out=x2, in0=o1, scalar=-HUGE, in1=ing, op0=ALU.mult, op1=ALU.add))
            L(eng.tensor_reduce(m2, x2, AX.X, ALU.max))
            one_hot(o2, x2, m2, "first8", 8)
            L(eng.tensor_tensor(d, m2, m1, ALU.subtract))
        self.phase_end(eng, who)
        if who == "act":
            eng.activation(ge, ge, ACT.Exp)
            eng.activation(d, d, ACT.Exp)
        self.phase_end(eng, who)
        if who == "dve":
            L(eng.tensor_reduce(gs, ge, AX.X, ALU.add))
            L(eng.reciprocal(gp, gs))
            L(eng.tensor_scalar(w1, d, 1.0, None, ALU.add))
            L(eng.reciprocal(w1, w1))
            L(eng.tensor_tensor(w1, w1, gp, ALU.mult))
            L(eng.tensor_tensor(w2, w1, d, ALU.mult))
            L(eng.tensor_tensor(o1, o1, w1.to_broadcast([P, 2, 8]), ALU.mult))
            L(eng.tensor_tensor(o2, o2, w2.to_broadcast([P, 2, 8]), ALU.mult))
            L(eng.tensor_tensor(comb, o1, o2, ALU.add))
            for t in range(2):
                L(eng.tensor_tensor(C[:, t, :, :], comb[:, t, :].unsqueeze(1).to_broadcast([P, 4, 8]),
                                    oneg[:, t, :].unsqueeze(2).to_broadcast([P, 4, 8]), ALU.mult))
            eng.memset(self.N[:, 0:2 * D], 0.0)
        self.phase_end(eng, who)

    def moe(self, who, eng):
        up_done, silu_done, hid_done, down_done, acc_used = \
            [self.sem("moe_" + x) for x in ("up_done", "silu_done", "hid_done", "down_done", "acc_used")]
        bank = self.bank
        acc = self.N[:, 0:2 * D].rearrange("p (t h d) -> p t h d", t=2, h=2)
        sg = self.X[:, 0:FET * LAT].rearrange("p (f t) -> p f t", f=FET)
        hid = self.X[:, 1024:1024 + FET * LAT].rearrange("p (f t) -> p f t", f=FET)
        C = self.S[:, 0:64].rearrange("p (t c) -> p t c", t=2)
        if who == "dve":
            eng.nop().then_inc(acc_used, 4)
        with eng.Fori(0, EXPERTS) as e:
            if who == "pe":
                g = FIRST["moe"]
                s0, s1 = self.ring[g % 2], self.ring[(g + 1) % 2]
                eng.wait_ge(self.w_loaded[g % 2], e * 16 + 16 * (g // 2 + 1))

                def gate_up(x, f, slot, tile):
                    return self.mm(eng, bank[f][:, x * LAT:(x + 1) * LAT],
                                   [slot[:, (tile * KT + k) * P:(tile * KT + k + 1) * P] for k in range(KT)],
                                   [self.A[:, k, CTX:T] for k in range(KT)])
                for f in range(4):
                    last = gate_up(0, f, s0, f)
                for f in range(2):
                    last = gate_up(1, f, s0, 4 + f)
                    last.then_inc(up_done, 1)
                eng.wait_ge(self.w_loaded[(g + 1) % 2], e * 16 + 16 * ((g + 1) // 2 + 1))
                for f in range(2, 4):
                    last = gate_up(1, f, s1, f - 2)
                    last.then_inc(up_done, 1)
                eng.wait_ge(acc_used, e * 4 + 4)
                for f in range(FET):
                    eng.wait_ge(hid_done, e * 4 + f + 1)
                    for t in range(2):
                        for h in range(2):
                            o = 2 * D + f * D + h * 512
                            last = eng.matmul(bank[4 + 2 * t + h][:, :], hid[:, f, t * P:(t + 1) * P],
                                              s1[:, o:o + 512], start=(f == 0), stop=(f == FET - 1))
                            if f == FET - 1:
                                last.then_inc(down_done, 1)
            if who == "act":
                for f in range(4):
                    eng.wait_ge(up_done, e * 4 + f + 1)
                    eng.activation(sg[:, f, :], bank[f][:, 0:LAT], ACT.Silu).then_inc(silu_done, 1)
            if who == "dve":
                for f in range(4):
                    eng.wait_ge(silu_done, e * 4 + f + 1)
                    eng.tensor_tensor(hid[:, f, :], sg[:, f, :], bank[f][:, LAT:2 * LAT], ALU.mult)\
                        .then_inc(hid_done, 1)
                for t in range(2):
                    c = C[:, t, bass.ds(e, 1)]
                    for h in range(2):
                        eng.wait_ge(down_done, e * 4 + 2 * t + h + 1)
                        eng.scalar_tensor_tensor(out=acc[:, t, h, :], in0=bank[4 + 2 * t + h][:, :], scalar=c,
                                                 in1=acc[:, t, h, :], op0=ALU.mult, op1=ALU.add)\
                            .then_inc(acc_used, 1)
        self.phase_end(eng, who)

    def result(self):
        return self.N[:, 0:2 * D].rearrange("p (t d) -> p t d", t=2)

    def final(self, who, eng):
        acc = self.result()
        bank = self.bank
        if who == "pe":
            for t in range(2):
                for k in range(KT):
                    eng.transpose(bank[t * 2 + k // 4][:, (k % 4) * P:(k % 4 + 1) * P],
                                  self.H[:, k, CTX + t * P:CTX + (t + 1) * P], self.con("ident"))
        self.phase_end(eng, who)
        ss = self.S[:, 128:130]
        if who == "dve":
            for t in range(2):
                for h in range(2):
                    c = acc[:, t, 512 * h:512 * h + 512]
                    eng.tensor_tensor(c, c, bank[t * 2 + h][:, :], ALU.add)
        self.phase_end(eng, who)
        if who == "act":
            for t in range(2):
                eng.activation(self.X[:, t * D:(t + 1) * D], acc[:, t, :], ACT.Square,
                               accum_out=ss[:, t:t + 1])
        self.phase_end(eng, who)
        if who == "dve":
            eng.tensor_scalar(ss, ss, 1.0 / D, RMS_EPS, ALU.mult, ALU.add)
        self.phase_end(eng, who)
        if who == "act":
            eng.activation(ss, ss, ACT.Sqrt)
        self.phase_end(eng, who)
        if who == "dve":
            self.link(eng, who, eng.reciprocal(ss, ss))
            for t in range(2):
                last = eng.scalar_tensor_tensor(out=acc[:, t, :], in0=acc[:, t, :], scalar=ss[:, t:t + 1],
                                                in1=self.vec("final_norm"), op0=ALU.mult, op1=ALU.mult)
                self.link(eng, who, last)
            eng.nop().then_inc(self.sem("result_ready"), 1)


def constants():
    c = {}
    i = np.arange(P)
    c["ident"] = np.eye(P)
    c["ones"] = np.ones((P, P))
    c["mean"] = np.full((P, P), 1.0 / D)

    def rotation(base, half, n):
        r = np.zeros((P, n))
        for j in range(half):
            for at in base:
                r[at + half + j, at + j] = -1.0
                r[at + j, at + half + j] = 1.0
        return r
    tok = np.arange(LAT)
    nf = DR // 4
    inv = (10000.0 ** (-np.arange(nf, dtype=np.float32) / np.float32(nf))).astype(np.float32)
    row, col = (tok // GRID_W).astype(np.float32), (tok % GRID_W).astype(np.float32)
    ang = np.concatenate([row[:, None] * inv, col[:, None] * inv], -1).T.astype(np.float32)
    cos, sin = np.ones((P, LAT)), np.zeros((P, LAT))
    for h in range(2):
        cos[DN + 16 * h:DN + 16 * h + 16] = np.cos(ang)
        sin[DN + 16 * h:DN + 16 * h + 16] = np.sin(ang)
    c["rot_mla"], c["cos_mla"], c["sin_mla"] = rotation([DN], DR // 2, QK), cos, sin
    inv = (500000.0 ** (-np.arange(8, dtype=np.float32) / np.float32(8))).astype(np.float32)
    ang = (tok.astype(np.float32)[:, None] * inv).T.astype(np.float32)
    cos, sin = np.ones((P, LAT)), np.zeros((P, LAT))
    for at in (0, 8, 64, 72):
        cos[at:at + 8], sin[at:at + 8] = np.cos(ang), np.sin(ang)
    c["rot_nsa"], c["cos_nsa"], c["sin_nsa"] = rotation([0, 64], 8, P), cos, sin
    qc, kc = i % GRID_W, np.arange(LAT) % GRID_W
    start = np.clip(qc - 8, 0, GRID_W - 16)
    ok = (kc[None, :] >= start[:, None]) & (kc[None, :] < start[:, None] + 16)
    c["na_mask"] = np.where(ok, 0.0, NEG)
    m = np.full((P, 416), NEG)
    tri = np.where(i[None, :] <= i[:, None], 0.0, NEG)
    m[:, 0:128] = tri
    m[:, 128:256] = 0.0
    m[:, 256:384] = tri
    keep = np.zeros((P, 32))
    for t in range(2):
        n = np.arange(16)
        ok = (16 * n + 31)[None, :] <= (i + P * t)[:, None]
        ok &= (n < NCMP)[None, :]
        m[:, 384 + 16 * t:400 + 16 * t] = np.where(ok, 0.0, NEG)
        keep[:, 16 * t:16 * t + 16] = ok
    c["nsa_mask"], c["cmp_keep"] = m, keep
    s, t = i[:, None], i[None, :]
    masks = [(s // (2 * v) == t // (2 * v)) & (s // v % 2 == 0) & (t // v % 2 == 1) for v in LEVELS]
    c["level_mask"] = np.concatenate(masks + [s == t], 1)
    c["scan_keep"] = np.broadcast_to((tok % 64 != 0), (P, LAT))
    c["first4"] = np.broadcast_to(4.0 - np.arange(4), (P, 4))
    c["first8"] = np.broadcast_to(8.0 - np.arange(8), (P, 8))
    out = np.zeros((P, NCONST), np.float32)
    for n, w in CONSTS:
        out[:, COFF[n][0]:COFF[n][0] + w] = c[n]
    return out


def tiled(w, tiles_per_chunk):
    k, n = w.shape
    w = w.reshape(k // P, P, n // P // tiles_per_chunk, tiles_per_chunk, P)
    return np.ascontiguousarray(w.transpose(2, 1, 3, 0, 4)).reshape(w.shape[2], P, -1)


def columns(v):
    return np.asarray(v).reshape(-1, P).T


def lay_out(a):
    W = {}
    W["ada"] = np.concatenate([tiled(a["ada_w"][i], 6) for i in range(DEPTH)])
    w = a["mla_w_in"][0]
    pe = np.zeros((D, QK), np.float32)
    pe[:, DN:] = w[:, QL + KVL:]
    W["mla_in"] = np.concatenate(
        [tiled(w[:, :QL + KVL], 5)[0], pe.reshape(KT, P, QK).transpose(1, 0, 2).reshape(P, -1)], 1)[None]
    q = a["mla_w_qb"][0].reshape(QLT, P, MLA_H, QK).transpose(2, 1, 0, 3).reshape(MLA_H, P, -1)
    kv = a["mla_w_kvb"][0].reshape(KVT, P, MLA_H, 2, DN).transpose(2, 1, 3, 0, 4).reshape(MLA_H, P, -1)
    W["mla_head"] = np.concatenate([q, kv], 2)
    W["mla_o"] = tiled(a["mla_w_o"][0], 4)
    for i in range(DEPTH):
        u = a["ffn_w_in"][i].reshape(KT, P, 2, FT // 2, 2, P)
        W[f"ffn_in{i}"] = u.transpose(3, 1, 2, 4, 0, 5).reshape(FT // 2, P, -1)
        W[f"ffn_out{i}"] = tiled(a["ffn_w_out"][i], 2)
    W["na_pair"] = a["na_w_qkv"][0].reshape(KT, P, 3, NA_PAIRS, P).transpose(3, 1, 2, 0, 4)\
        .reshape(NA_PAIRS, P, -1)
    W["na_o"] = tiled(a["na_w_o"][0], 4)
    w = a["w_in_2"][0]
    q = w[:, :512].reshape(D, 2, 4, 64).transpose(0, 2, 1, 3).reshape(D, 512)
    W["proj"] = tiled(np.concatenate([q, w[:, 512:1280], w[:, 1304:]], 1), 6)
    cmp = np.zeros((2, P, 32, P), np.float32)
    for x, n in enumerate(("w_cmp_k_2", "w_cmp_v_2")):
        c = a[n][0].reshape(32, 64, 64).transpose(1, 0, 2)
        cmp[x, 0:64, :, 0:64] = c
        cmp[x, 64:128, :, 64:128] = c
    W["cmp"] = cmp.reshape(2, P, -1)
    W["branch"] = np.concatenate([tiled(a["w_br_nsa_2"][0], 8), tiled(a["w_br_hg_2"][0], 8)])
    W["w_out"] = tiled(a["w_out_2"][0], 4)
    g, u = [a[n][0].reshape(EXPERTS, KT, P, FET, P).transpose(0, 2, 3, 1, 4).reshape(EXPERTS, P, -1)
            for n in ("w_gate_2", "w_up_2")]
    dn = a["w_down_2"][0].reshape(EXPERTS, FET, P, D).transpose(0, 2, 1, 3).reshape(EXPERTS, P, -1)
    W["moe"] = np.concatenate([g, u, dn], 2).reshape(EXPERTS, P, 2, SLOT).transpose(0, 2, 1, 3)\
        .reshape(2 * EXPERTS, P, SLOT)

    v = {}
    v["cvec"] = np.stack([columns(a["c_ctx"]), columns(a["c"][0])], 2).reshape(P, -1)
    for n in ("ada_b", "ln1_g", "ln1_b", "ln2_g", "ln2_b"):
        v[n] = columns(a[n])
    v["conv_w"], v["conv_b"] = columns(a["ffn_conv_w"]), columns(a["ffn_conv_b"])
    v["q_norm"], v["kv_norm"] = columns(a["mla_q_norm"]), columns(a["mla_kv_norm"])
    v["attn_norm"], v["ffn_norm"] = columns(a["attn_norm_2"]), columns(a["ffn_norm_2"])
    v["hg_lb"], v["hg_norm"] = columns(a["hg_lb_logits_2"]), columns(a["hg_norm_2"])
    v["cmp_pos"] = np.concatenate([a["cmp_pos_2"][0].T] * 2)
    w = a["w_in_2"][0][:, 1280:1304].reshape(KT, P, 2, 4, 3)[..., [1, 0, 2]]
    v["w_gate24"] = w.transpose(1, 0, 3, 2, 4).reshape(P, -1)
    w = np.concatenate([a["w_grp_2"][0], a["w_rtr_2"][0]], 1)
    v["w_route"] = w.reshape(KT, P, 36).transpose(1, 0, 2).reshape(P, -1)
    v["b_route"] = np.broadcast_to(np.concatenate([a["b_grp_2"][0], a["b_rtr_2"][0]]), (P, 36))
    v["final_norm"] = np.broadcast_to(a["final_norm_2"], (P, D))
    vec = np.zeros((P, NVEC), np.float32)
    for n, wd in VECS:
        vec[:, VOFF[n][0]:VOFF[n][0] + wd] = v[n]

    xT = np.concatenate([a["ctx"][0], a["x"][0]]).T.reshape(KT, P, T).transpose(1, 0, 2)
    r = a["na_rpb"][0]
    wide = np.zeros((16, 7, 2 * GRID_W - 1), np.float32)
    wide[:, :, 48:79] = r[:, 4:11, :]
    nab = np.empty((4, GRID_W, 16, 4, GRID_W), np.float32)
    for qr in range(4):
        for qc in range(GRID_W):
            nab[qr, qc] = wide[:, 3 - qr:7 - qr, 63 - qc:127 - qc]
    return W, vec, np.ascontiguousarray(xT), nab.reshape(4, GRID_W, 16, LAT)


def kernel(**inputs):
    import concourse.bacc as _bacc
    from concourse.bass_utils import run_bass_kernel_spmd as _run

    weights, vectors, x_t, na_bias = lay_out({k: np.asarray(v) for k, v in inputs.items()})
    nc = _bacc.Bacc("TRN2", target_bir_lowering=False, num_devices=1)
    arrays = {"in_vectors": vectors, "in_constants": constants(), "in_x_t": x_t, "in_na_bias": na_bias}
    arrays |= {"w_" + n: weights[n] for n, _, _ in STREAM}
    arrays = {n: np.ascontiguousarray(v) for n, v in arrays.items()}
    d = {n: nc.dram_tensor(n, v.shape, F32, kind="ExternalInput").ap() for n, v in arrays.items()}
    out = nc.dram_tensor("out", (1, LAT, D), F32, kind="ExternalOutput").ap()
    program = Kernel(nc, {n: d["w_" + n] for n, _, _ in STREAM}, d["in_vectors"], d["in_constants"],
                     d["in_x_t"], d["in_na_bias"], out)
    program.build()
    r = _run(nc, [arrays], core_ids=[0])
    return r.results[0]["out"]
```

```python
import math
from contextlib import ExitStack

import numpy as np
import concourse.bass as bass
from concourse import mybir

F32 = mybir.dt.float32
ACT = mybir.ActivationFunctionType
ALU = mybir.AluOpType
AX = mybir.AxisListType

P = 128
D = 1024
KT = D // P
CTX = 256
LAT = 256
T = CTX + LAT
DEPTH = 2
ALPHA = (2.0 * DEPTH) ** 0.25
LN_EPS, RMS_EPS = 1e-5, 1e-6
NEG = -1e30
HUGE = 3.0e38
GRID_W = 64

MLA_H, DN, DR, DV = 16, 64, 32, 64
QK = DN + DR
QL, KVL = 384, 256
QLT, KVT = QL // P, KVL // P
NA_PAIRS = 8
FFN = 2816
FT = FFN // P
NSA_PAIRS = 4
NCMP = 15
HG = 4
EXPERTS, GROUPS, PER_GROUP = 32, 4, 8
FE = 512
SLOTS = 64
FET = FE // P

SLOT = 6144
RING = 2

VECS = [("cvec", KT * 2), ("ada_b", DEPTH * 48),
        ("ln1_g", DEPTH * KT), ("ln1_b", DEPTH * KT), ("ln2_g", DEPTH * KT), ("ln2_b", DEPTH * KT),
        ("conv_w", DEPTH * 3 * 2 * FT), ("conv_b", DEPTH * 2 * FT),
        ("q_norm", QLT), ("kv_norm", KVT), ("attn_norm", KT), ("ffn_norm", KT),
        ("hg_lb", 2 * HG), ("hg_norm", 1), ("cmp_pos", 32),
        ("w_gate24", KT * 24), ("w_route", KT * 36), ("b_route", 36), ("final_norm", D)]
VOFF, _at = {}, 0
for _n, _w in VECS:
    VOFF[_n] = (_at, _w)
    _at += _w
NVEC = _at

LEVELS = [64, 32, 16, 8, 4, 2, 1]
CONSTS = [("ident", P), ("ones", P), ("mean", P), ("rot_mla", QK), ("cos_mla", LAT), ("sin_mla", LAT),
          ("rot_nsa", P), ("cos_nsa", LAT), ("sin_nsa", LAT), ("na_mask", LAT),
          ("nsa_mask", 416), ("cmp_keep", 32), ("level_mask", (len(LEVELS) + 1) * P), ("scan_keep", LAT),
          ("fold", 2), ("first4", GROUPS), ("first8", PER_GROUP), ("before", P), ("slot", SLOTS)]
COFF, _at = {}, 0
for _n, _w in CONSTS:
    COFF[_n] = (_at, _w)
    _at += _w
NCONST = _at

T_Q, T_CK, T_CV, T_SK, T_SV, T_WK, T_WV, T_HQ, T_HF, T_HI, T_HGATE, T_MN, T_MH = \
    0, 4, 5, 6, 7, 8, 9, 10, 14, 18, 22, 26, 34
NPROJ = 42

HEAD_W = QLT * QK + KVT * (DN + DV)
ADA_FIRST, ADA_TILES = 4 * 4, 5
STREAM = [("ada", 4, KT * 512), ("mla_in", 1, 5 * D + 8 * QK),
          ("mla_head", 16, HEAD_W + KT * ADA_TILES * P), ("mla_o", 2, 4096),
          ("ffn_in0", 11, 4096), ("ffn_out0", 4, 5632),
          ("na_pair", NA_PAIRS, 3072), ("na_o", 2, 4096),
          ("ffn_in1", 11, 4096), ("ffn_out1", 4, 5632),
          ("proj", 7, 6144), ("cmp", 2, 4096), ("branch", 2, 4096), ("w_out", 2, 4096),
          ("moe", EXPERTS, (2 * KT + 2 * FET) * FE)]
UPS = 2 * KT * FE
FIRST, _at = {}, 0
for _n, _c, _w in STREAM:
    FIRST[_n] = _at
    _at += _c
CHUNKS = {n: c for n, c, _ in STREAM}


def each(k):
    return lambda c: c * k + k


CHUNK_USED = {
    "ada": ("ada_used", each(1)), "mla_in": ("mla_in_used", each(1)),
    "mla_head": ("ada_rows", each(1)), "mla_o": ("mla_o_y_ready", each(4)),
    "ffn_in0": ("ffn0_up_done", each(2)), "ffn_out0": ("ffn_out0_y_ready", each(2)),
    "na_pair": ("na_proj_done", each(1)), "na_o": ("na_o_y_ready", each(4)),
    "ffn_in1": ("ffn1_up_done", each(2)), "ffn_out1": ("ffn_out1_y_ready", each(2)),
    "proj": ("proj_tile_done", each(6)), "cmp": ("cmp_used", each(1)),
    "branch": ("branch_done", lambda c: KT), "w_out": ("w_out_y_ready", each(4)),
}


class Kernel:

    def __init__(self, nc, W, vec, const, xT, na_bias, out):
        self.nc, self.W, self.vec_d, self.const_d, self.xT, self.nab_d, self.out = \
            nc, W, vec, const, xT, na_bias, out
        self.phases = {"pe": 0, "act": 0, "dve": 0}
        self.links = {"act": 0, "dve": 0}
        self.norms = {"pe": 0, "act": 0, "dve": 0}
        self.norm_counts = {w: (0, 0, 0) for w in self.norms}
        self.flips = {"pe": 0, "dve": 0}
        self.outs = {"pe": 0, "dve": 0}

    def sem(self, name):
        if name not in self.sems:
            self.sems[name] = self.ctx.enter_context(self.nc.semaphore(name))
        return self.sems[name]

    def vec(self, name, i=0, n=None):
        off, w = VOFF[name]
        return self.V[:, off + i:off + (w if n is None else i + n)]

    def con(self, name, i=0, n=None):
        off, w = COFF[name]
        return self.C[:, off + i:off + (w if n is None else i + n)]

    def phase_end(self, eng, who):
        self.phases[who] += 1
        eng.drain().then_inc(self.phase_done, 1)
        eng.wait_ge(self.phase_done, 3 * self.phases[who])

    def link(self, eng, who, ins):
        self.links[who] += 1
        s = self.chain[who]
        ins.then_inc(s, 1)
        eng.wait_ge(s, self.links[who])

    def chunks(self, pe, name, body, count=None, start=0):
        g0 = FIRST[name] + start
        n = (CHUNKS[name] if count is None else count)
        turns = n // 2
        if turns >= 2:
            with pe.Fori(0, turns) as it:
                for s in range(2):
                    g = g0 + s
                    pe.wait_ge(self.w_loaded[g % 2], it * 16 + 16 * (g // 2 + 1))
                    body(it * 2 + s + start, self.ring[g % 2])
            done = 2 * turns
        else:
            done = 0
        for j in range(done, n):
            g = g0 + j
            pe.wait_ge(self.w_loaded[g % 2], 16 * (g // 2 + 1))
            body(j + start, self.ring[g % 2])

    def counted(self, eng, n, body):
        with eng.Fori(0, n // 2) as it:
            for s in range(2):
                body(it * 2 + s)
        if n % 2:
            body(n - 1)

    def build(self):
        nc = self.nc
        with ExitStack() as ctx:
            self.ctx, self.sems = ctx, {}

            def sb(name, shape):
                return ctx.enter_context(nc.sbuf_tensor(name, shape, F32))
            self.whole_ring = sb("ring", [P, RING * SLOT])
            self.ring = [self.whole_ring[:, i * SLOT:(i + 1) * SLOT] for i in range(RING)]
            self.H = sb("residual", [P, KT, T])
            self.A = sb("layer_input", [P, KT, T])
            arena = sb("arena", [P, FT * T + 32 * LAT + KT * T])
            self.arena = arena[:, :]
            self.B = arena[:, 0:FT * T]
            self.N = arena[:, FT * T:FT * T + 32 * LAT]
            self.X = arena[:, FT * T + 32 * LAT:]
            self.overflow = ctx.enter_context(nc.sbuf_tensor("overflow", [1, 1], mybir.dt.int32))
            self.V = sb("vectors", [P, NVEC])
            self.C = sb("constants", [P, NCONST])
            self.ADA = sb("ada", [P, DEPTH, 48, 2])
            self.S = sb("stats", [P, 256])
            self.R = sb("rstd", [P, T])
            self.bank = [ctx.enter_context(nc.psum_tensor(f"bank{i}", [P, 512], F32)) for i in range(8)]
            self.w_loaded = [self.sem(f"w_loaded{i}") for i in range(RING)]
            self.phase_done = self.sem("phase_done")
            self.chain = {"dve": self.sem("dve_link"), "act": self.sem("act_link")}
            self.const_in, self.bias_in = self.sem("const_in"), self.sem("bias_in")
            block = ctx.enter_context(nc.Block())

            @block.tensor
            def _(pe):
                self.run("pe", pe)

            @block.scalar
            def _(act):
                act.dma_start(self.V[:, :], self.vec_d).then_inc(self.const_in, 16)
                act.dma_start(self.C[:, :], self.const_d).then_inc(self.const_in, 16)
                act.dma_start(self.H[:, :, :], self.xT).then_inc(self.const_in, 16)
                self.run("act", act)

            @block.vector
            def _(dve):
                self.run("dve", dve)

            @block.sync
            def _(sp):
                self.sync_program(sp)

    def stages(self):
        return [self.ada, self.modulate_first, self.mla_in, self.mla_heads, self.mla_out,
                lambda w, e: self.ffn(w, e, 0), self.na_heads, self.na_out,
                lambda w, e: self.ffn(w, e, 1),
                self.proj, self.compress, self.nsa_heads, self.hgrn, self.branches,
                self.router, self.moe, self.final]

    def run(self, who, eng):
        st = self.stages()
        for stage in st:
            stage(who, eng)

    def sync_program(self, sp):
        for name, n, width in STREAM:
            w, g0 = self.W[name], FIRST[name]

            if name == "moe":
                self.load_experts(sp)
                break

            def load(j, s, g):
                sp.dma_start(self.ring[s][:, 0:width], w[j]).then_inc(self.w_loaded[s], 16)
            first = 0
            if g0 == 0:
                for j in range(RING):
                    load(j, j, j)
                first = RING
            while first < min(n, RING):
                g = g0 + first - RING
                before = max((m for m in FIRST if FIRST[m] <= g), key=FIRST.get)
                sem, upto = CHUNK_USED[before]
                sp.wait_ge(self.sem(sem), upto(g - FIRST[before]))
                load(first, (g0 + first) % 2, g0 + first)
                first += 1
            sem, upto = CHUNK_USED[name]
            turns = (n - first) // 2
            if turns >= 2:
                with sp.Fori(0, turns) as it:
                    for s in range(2):
                        g = g0 + first + s
                        sp.wait_ge(self.sem(sem), upto(it * 2 + (first + s - RING)))
                        load(it * 2 + first + s, g % 2, g)
                first += 2 * turns
            for j in range(first, n):
                sp.wait_ge(self.sem(sem), upto(j - RING))
                load(j, (g0 + j) % 2, g0 + j)
        sp.wait_ge(self.phase_done, self.flag_phase)
        n = sp.value_load(self.overflow[0:1, 0:1])
        with sp.If(n != 0):
            self.late("sp", sp)
        sp.wait_ge(self.sem("result_ready"), 1)
        sp.dma_start(self.out.rearrange("a (t p) d -> p (a t) d", p=P),
                     self.result()).then_inc(self.sem("result_out"), 16)
        sp.wait_ge(self.sem("result_out"), 16)

    def expert_slots(self):
        return self.whole_ring[:, :], self.arena[:, FT * T:FT * T + RING * SLOT]

    def load_experts(self, sp):
        loaded = self.expert_loaded()
        slots = self.expert_slots()
        parts = slice(0, UPS), slice(UPS, 2 * SLOT)

        def load(x, e, part):
            sp.dma_start(slots[e][:, parts[part]], self.W["moe"][x][:, parts[part]])\
                .then_inc(loaded[e][part], 16)
        sp.wait_ge(self.sem("w_out_y_ready"), KT)
        for part in range(2):
            load(0, 0, part)
        sp.wait_ge(self.phase_done, self.router_phase)
        for part in range(2):
            load(1, 1, part)
        with sp.Fori(0, EXPERTS // 2 - 1) as it:
            for e in range(2):
                sp.wait_ge(self.sem("moe_up_done"), it * 2 + e + 1)
                load(it * 2 + e + 2, e, 0)
                sp.wait_ge(self.sem("moe_down_done"), it * 2 + e + 1)
                load(it * 2 + e + 2, e, 1)

    def expert_loaded(self):
        return [[self.sem(f"expert{e}_{part}_loaded") for part in ("up", "down")] for e in range(2)]

    def mm(self, pe, out, lhs, rhs):
        for k, (a, b) in enumerate(zip(lhs, rhs)):
            last = pe.matmul(out, a, b, start=(k == 0), stop=(k == len(lhs) - 1))
        return last

    def norm(self, who, eng, c0, write, src=None, tiles=KT, centre=True, dim=D, eps=LN_EPS, sq=None):
        w = T - c0
        src = src or (lambda k: self.H[:, k, c0:T])
        xc = self.X[:, :].rearrange("p (k t) -> p k t", k=KT)
        sq = sq or (lambda k: self.A[:, k, c0:T])
        n = self.norms[who]
        self.norms[who] += 1
        mean_ready, centred, squared, var_ready, dev_ready = \
            [self.sem(x) for x in ("mean_ready", "centred", "squared", "var_ready", "dev_ready")]
        base, cbase, means = self.norm_counts[who]
        self.norm_counts[who] = (base + tiles, cbase + tiles * centre, means + centre)
        val = (lambda k: xc[:, k, 0:w]) if centre else src
        mu, var = self.bank[0][:, 0:w], self.bank[1][:, 0:w]
        if who == "pe":
            if centre:
                self.mm(eng, mu, [self.con("mean")] * tiles, [src(k) for k in range(tiles)])\
                    .then_inc(mean_ready, 1)
            for k in range(tiles):
                eng.wait_ge(squared, base + k + 1)
                last = eng.matmul(var, self.con("mean" if dim == D else "ones"), sq(k),
                                  start=(k == 0), stop=(k == tiles - 1))
            last.then_inc(var_ready, 1)
        if who == "act":
            for k in range(tiles):
                if centre:
                    eng.wait_ge(centred, cbase + k + 1)
                eng.activation(sq(k), val(k), ACT.Square).then_inc(squared, 1)
            eng.wait_ge(dev_ready, 2 * n + 1)
            eng.activation(self.R[:, 0:w], self.R[:, 0:w], ACT.Sqrt).then_inc(dev_ready, 1)
        if who == "dve":
            if centre:
                eng.wait_ge(mean_ready, means + 1)
                for k in range(tiles):
                    eng.tensor_tensor(val(k), src(k), mu, ALU.subtract).then_inc(centred, 1)
            eng.wait_ge(var_ready, n + 1)
            eng.tensor_scalar(self.R[:, 0:w], var, 1.0 if dim == D else 1.0 / dim, eps,
                              ALU.mult, ALU.add).then_inc(dev_ready, 1)
            eng.wait_ge(dev_ready, 2 * n + 2)
            self.link(eng, who, eng.reciprocal(self.R[:, 0:w], self.R[:, 0:w]))
            for k in range(tiles):
                write(k, val(k), self.R[:, 0:w])
        self.phase_end(eng, who)

    def layer_norm(self, who, eng, c0, gain, bias, layer):
        def write(k, x, r):
            self.link(eng, who, eng.tensor_tensor(x, x, r, ALU.mult))
            self.link(eng, who, eng.tensor_scalar(self.H[:, k, c0:T], x, self.vec(gain, layer * KT + k, 1),
                                                  self.vec(bias, layer * KT + k, 1), ALU.mult, ALU.add))
        self.norm(who, eng, c0, write)

    def modulate(self, who, eng, layer, shift, scale, segs):
        if who == "act":
            for k in range(KT):
                for seg in segs:
                    c = slice(CTX * seg, CTX * seg + 256)
                    eng.activation(self.A[:, k, c], self.H[:, k, c], ACT.Identity,
                                   bias=self.ADA[:, layer, shift * KT + k, seg:seg + 1],
                                   scale=self.ADA[:, layer, scale * KT + k, seg:seg + 1])
        self.phase_end(eng, who)

    def project_residual(self, who, eng, name, rhs, nk, per_chunk, gate, layer, segs):
        c0 = CTX * segs[0]
        w = T - c0
        y_ready, y_used = self.sem(name + "_y_ready"), self.sem(name + "_y_used")
        tiles = KT
        if who == "pe":
            def body(j, slot):
                for s in range(per_chunk):
                    oc = j * per_chunk + s
                    first_two = isinstance(oc, int) and oc < 2
                    if not first_two:
                        eng.wait_ge(y_used, oc - 1)
                    o = s % 2
                    m = self.mm(eng, self.bank[o][:, 0:w],
                                [slot[:, (s * nk + k) * P:(s * nk + k + 1) * P] for k in range(nk)],
                                [rhs(k) for k in range(nk)])
                    m.then_inc(y_ready, 1)
            for j in range(CHUNKS[name]):
                g = FIRST[name] + j
                eng.wait_ge(self.w_loaded[g % 2], 16 * (g // 2 + 1))
                body(j, self.ring[g % 2])
        if who == "dve":
            tmp = self.X[:, 0:w]
            for oc in range(tiles):
                eng.wait_ge(y_ready, oc + 1)
                y = self.bank[oc % 2][:, 0:w]
                if gate is None:
                    eng.tensor_tensor(self.H[:, oc, c0:T], self.H[:, oc, c0:T], y, ALU.add)\
                        .then_inc(y_used, 1)
                    continue
                for seg in segs:
                    part = slice(CTX * seg - c0, CTX * seg - c0 + 256)
                    last = eng.tensor_scalar(tmp[:, part], y[:, part],
                                             self.ADA[:, layer, gate * KT + oc, seg:seg + 1], None, ALU.mult)
                self.link(eng, who, last)
                last = eng.scalar_tensor_tensor(out=self.H[:, oc, c0:T], in0=self.H[:, oc, c0:T],
                                                scalar=ALPHA, in1=tmp, op0=ALU.mult, op1=ALU.add)
                last.then_inc(y_used, 1)
                eng.wait_ge(y_used, oc + 1)
        self.phase_end(eng, who)

    def flip(self, who, eng, src, dst, tiles, rows, name):
        n0 = self.flips.get(who, 0)
        self.flips[who] = n0 + tiles
        turned, copied = self.sem("turned"), self.sem("turned_copied")
        if who == "pe":
            for k in range(tiles):
                if n0 + k >= 2:
                    eng.wait_ge(copied, n0 + k - 1)
                for t in range(rows):
                    last = eng.transpose(self.bank[(n0 + k) % 2][:, t * P:(t + 1) * P], src(t, k),
                                         self.con("ident"))
                last.then_inc(turned, 1)
        if who == "dve":
            for k in range(tiles):
                eng.wait_ge(turned, n0 + k + 1)
                eng.tensor_copy(dst(k), self.bank[(n0 + k) % 2][:, 0:rows * P]).then_inc(copied, 1)
        self.phase_end(eng, who)

    def silu(self):
        return self.X[:, 3712:3712 + 32 * KT].rearrange("p (k c) -> p k c", k=KT)

    def ada_group_rows(self, pe, bank, weights, width):
        cs = self.silu()
        for r in range(2):
            for grp in range(4):
                k = 4 * r + grp
                last = pe.matmul(bank[32 * grp:32 * grp + 32, 0:width], cs[:, k, :], weights(k),
                                 start=(r == 0), stop=(r == 1), skip_group_check=True)
        return last

    def ada(self, who, eng):
        silu_ready, used, copied = [self.sem(x) for x in ("silu_ready", "ada_used", "ada_copied")]
        flat = self.ADA[:, :, :, :].rearrange("p l m s -> p (l m) s")
        n = ADA_FIRST
        if who == "dve":
            eng.memset(self.silu(), 0.0).then_inc(silu_ready, 1)
        if who == "act":
            eng.wait_ge(self.const_in, 48)
            eng.wait_ge(silu_ready, 1)
            eng.activation(self.silu()[:, :, 0:2], self.vec("cvec").rearrange("p (k s) -> p k s", s=2), ACT.Silu)\
                .then_inc(silu_ready, 1)
        if who == "pe":
            eng.wait_ge(silu_ready, 2)
            for j in range(CHUNKS["ada"]):
                g = FIRST["ada"] + j
                eng.wait_ge(self.w_loaded[g % 2], 16 * (g // 2 + 1))
                slot = self.ring[g % 2]
                self.ada_group_rows(eng, self.bank[j][:, :], lambda k: slot[:, k * 512:(k + 1) * 512], 512)\
                    .then_inc(used, 1)
            for j in range(CHUNKS["ada"]):
                eng.wait_ge(copied, j + 1)
                for t in range(4):
                    eng.matmul(self.bank[4][:, (4 * j + t) * 2:(4 * j + t) * 2 + 2],
                               self.X[:, j * 512 + t * P:j * 512 + (t + 1) * P], self.con("fold"),
                               start=True, stop=True)
        if who == "dve":
            for j in range(CHUNKS["ada"]):
                eng.wait_ge(used, j + 1)
                eng.tensor_copy(self.X[:, j * 512:(j + 1) * 512], self.bank[j][:, :]).then_inc(copied, 1)
        self.phase_end(eng, who)
        if who == "dve":
            b = self.vec("ada_b", 0, n).unsqueeze(2).to_broadcast([P, n, 2])
            self.link(eng, who, eng.tensor_tensor(
                flat[:, 0:n, :], self.bank[4][:, 0:2 * n].rearrange("p (m s) -> p m s", s=2), b, ALU.add))
            sc = flat[:, KT:2 * KT, :]
            self.link(eng, who, eng.tensor_scalar(sc, sc, 1.0, None, ALU.add))
        self.phase_end(eng, who)

    def ada_rest(self, who, eng):
        if who == "dve":
            n = DEPTH * 48 - ADA_FIRST
            flat = self.ADA[:, :, :, :].rearrange("p l m s -> p (l m) s")
            b = self.vec("ada_b", ADA_FIRST, n).unsqueeze(2).to_broadcast([P, n, 2])
            self.link(eng, who, eng.tensor_tensor(flat[:, ADA_FIRST:, :], flat[:, ADA_FIRST:, :], b, ALU.add))
            for layer, m in ((0, 4), (1, 1), (1, 4)):
                sc = self.ADA[:, layer, m * KT:(m + 1) * KT, :]
                self.link(eng, who, eng.tensor_scalar(sc, sc, 1.0, None, ALU.add))

    def modulate_first(self, who, eng):
        self.modulate(who, eng, 0, 0, 1, (0, 1))

    def mla_views(self):
        b = self.B
        v = {}
        at = 0
        for name, n in (("cq", QLT * T), ("ckv", KVT * T), ("kpe", T), ("kpr", LAT),
                        ("q0", T), ("q1", T), ("qr0", LAT), ("qr1", LAT), ("qt0", LAT), ("qt1", LAT),
                        ("kt0", T), ("kt1", T), ("v0", 4 * DV), ("v1", 4 * DV)):
            v[name] = b[:, at:at + n]
            at += n
        assert at <= FT * T
        v["p"] = self.X[:, 0:1536]
        v["pt"] = self.X[:, 1536:3072]
        v["o"] = self.A[:, :, :].rearrange("p k t -> p (k t)").rearrange("p (t d) -> p t d", t=4)
        return v

    def mla_in(self, who, eng):
        v = self.mla_views()
        cq = v["cq"].rearrange("p (k t) -> p k t", k=QLT)
        ckv = v["ckv"].rearrange("p (k t) -> p k t", k=KVT)
        if who == "pe":
            g = FIRST["mla_in"]
            eng.wait_ge(self.w_loaded[g % 2], 16 * (g // 2 + 1))
            slot = self.ring[g % 2]
            for m in range(6):
                wd = P if m < 5 else QK
                last = self.mm(eng, self.bank[m][0:wd, :],
                               [slot[:, m * D + k * wd:m * D + (k + 1) * wd] for k in range(KT)],
                               [self.A[:, k, :] for k in range(KT)])
            last.then_inc(self.sem("mla_in_used"), 1)
        self.phase_end(eng, who)
        if who == "dve":
            for m in range(3):
                eng.tensor_copy(cq[:, m, :], self.bank[m][:, :])
            for m in range(2):
                eng.tensor_copy(ckv[:, m, :], self.bank[3 + m][:, :])
        if who == "act":
            eng.copy(v["kpe"][0:QK, :], self.bank[5][0:QK, :])
        self.phase_end(eng, who)

        def scaled(dst, gain):
            def write(k, x, r):
                self.link(eng, who, eng.tensor_tensor(x, x, r, ALU.mult))
                self.link(eng, who, eng.tensor_scalar(dst[:, k, :], x, self.vec(gain, k, 1), None, ALU.mult))
            return write
        sq = lambda k: self.A[:, k, :]
        self.norm(who, eng, 0, scaled(cq, "q_norm"), src=lambda k: cq[:, k, :], tiles=QLT, centre=False,
                  dim=QL, eps=RMS_EPS, sq=sq)
        self.norm(who, eng, 0, scaled(ckv, "kv_norm"), src=lambda k: ckv[:, k, :], tiles=KVT, centre=False,
                  dim=KVL, eps=RMS_EPS, sq=sq)
        if who == "pe":
            eng.matmul(self.bank[2][0:QK, 0:LAT], self.con("rot_mla")[0:QK, :], v["kpe"][0:QK, CTX:T],
                       start=True, stop=True)
        self.phase_end(eng, who)
        if who == "dve":
            r = slice(DN, QK)
            self.link(eng, who, eng.tensor_tensor(v["kpr"][r, :], self.bank[2][r, 0:LAT],
                                                  self.con("sin_mla")[r, :], ALU.mult))
            self.link(eng, who, eng.tensor_tensor(v["kt0"][r, CTX:T], v["kpe"][r, CTX:T],
                                                  self.con("cos_mla")[r, :], ALU.mult))
            self.link(eng, who, eng.tensor_tensor(v["kt0"][r, CTX:T], v["kt0"][r, CTX:T],
                                                  v["kpr"][r, :], ALU.add))
            eng.tensor_copy(v["kt1"][r, CTX:T], v["kt0"][r, CTX:T])
            eng.tensor_copy(v["kt0"][r, 0:CTX], v["kpe"][r, 0:CTX])
            eng.tensor_copy(v["kt1"][r, 0:CTX], v["kpe"][r, 0:CTX])
        self.phase_end(eng, who)

    def mla_heads(self, who, eng):
        v = self.mla_views()
        names = ("proj_done", "q_copied", "kv_copied", "rot_done", "rotated", "scored", "max_ready",
                 "exp_done", "turned", "pt_act", "pt_dve", "o_done", "o_used")
        s = {n: self.sem("mla_" + n) for n in names}
        link = self.sem("mla_link")
        ada_rows, ada_copied = self.sem("ada_rows"), self.sem("ada_rows_copied")
        rows = self.X[:, 3072:3072 + ADA_TILES * P]
        half = ADA_TILES * P // 2
        fold_at = slice(half, half + 2 * ADA_TILES)
        flat = self.ADA[:, :, :, :].rearrange("p l m s -> p (l m s)")
        scale = QK ** -0.5
        cq = v["cq"].rearrange("p (k t) -> p k t", k=QLT)
        ckv = v["ckv"].rearrange("p (k t) -> p k t", k=KVT)
        p, pt = v["p"], v["pt"].rearrange("p (b q) -> p b q", q=P)
        ptiles = [p[:, 0:256], p[:, 256:512], p[:, 512:1024], p[:, 1024:1536]]
        mx, nb, rs, rc = [[self.S[:, 64 + 16 * e + 4 * n:64 + 16 * e + 4 * n + 4] for e in range(2)]
                          for n in range(4)]
        bank = self.bank
        g0 = FIRST["mla_head"]

        def pe_project(h, e):
            slot = self.ring[(g0 + e) % 2]
            eng.wait_ge(self.w_loaded[(g0 + e) % 2], (h - e) * 8 + 16 * ((g0 + e) // 2 + 1))
            if isinstance(h, int) and h == 0:
                pass
            else:
                eng.wait_ge(s["rotated"], h)
                eng.wait_ge(s["kv_copied"], 2 * h)
            self.mm(eng, bank[0][0:QK, :], [slot[:, k * QK:(k + 1) * QK] for k in range(QLT)],
                    [cq[:, k, :] for k in range(QLT)])
            o = QLT * QK
            self.mm(eng, bank[1][0:DN, :], [slot[:, o + k * DN:o + (k + 1) * DN] for k in range(KVT)],
                    [ckv[:, k, :] for k in range(KVT)])
            o += KVT * DN
            for t in range(4):
                last = self.mm(eng, bank[2][:, t * DV:(t + 1) * DV],
                               [ckv[:, k, t * P:(t + 1) * P] for k in range(KVT)],
                               [slot[:, o + k * DV:o + (k + 1) * DV] for k in range(KVT)])
            last.then_inc(s["proj_done"], 1)

        def pe_ada_half(e, x):
            o = HEAD_W + x * half
            slot = self.ring[(g0 + e) % 2]
            return self.ada_group_rows(eng, bank[5 + 2 * x][:, :],
                                       lambda k: slot[:, o + k * 2 * half:o + k * 2 * half + half], half)

        def pe_ada_fold():
            for t in range(ADA_TILES):
                last = eng.matmul(bank[5][:, half + 2 * t:half + 2 * t + 2], rows[:, t * P:(t + 1) * P],
                                  self.con("fold"), start=True, stop=True)
            return last

        def dve_ada_copy():
            eng.tensor_copy(rows[:, 0:half], bank[5][:, 0:half])
            eng.tensor_copy(rows[:, half:2 * half], bank[7][:, 0:half]).then_inc(ada_copied, 1)

        def pe_scores(h, e):
            eng.wait_ge(s["q_copied"], h + 1)
            eng.wait_ge(s["kv_copied"], 2 * h + 2)
            eng.matmul(bank[2][0:QK, 256:512], self.con("rot_mla")[0:QK, :], v[f"q{e}"][0:QK, CTX:T],
                       start=True, stop=True).then_inc(s["rot_done"], 1)
            eng.wait_ge(s["o_used"], h + 1)
            q, qr, k = v[f"q{e}"], v[f"qr{e}"], v[f"kt{e}"]
            for t in range(2):
                last = eng.matmul(bank[3][:, t * 256:(t + 1) * 256], q[0:QK, t * P:(t + 1) * P],
                                  k[0:QK, 0:CTX], start=True, stop=True)
            last.then_inc(s["scored"], 1)
            eng.wait_ge(s["rotated"], h + 1)
            eng.wait_ge(ada_copied, h + 1)
            for t in range(2):
                eng.matmul(bank[4 + t][:, 0:CTX], q[0:QK, CTX + t * P:CTX + (t + 1) * P], k[0:QK, 0:CTX],
                           start=True, stop=True)
                eng.matmul(bank[4 + t][:, CTX:T], qr[0:QK, t * P:(t + 1) * P], k[0:QK, CTX:T],
                           start=True, stop=True).then_inc(s["scored"], 1)

        def pe_tail(h, e):
            for n, (b, tile0, blocks) in enumerate(((6, 0, 4), (7, 2, 4), (3, 3, 4))):
                eng.wait_ge(s["exp_done"], 4 * h + (2, 3, 4)[n])
                for j in range(blocks):
                    src = ptiles[j // 2][:, (j % 2) * P:(j % 2 + 1) * P] if n == 0 \
                        else ptiles[tile0][:, j * P:(j + 1) * P]
                    last = eng.transpose(bank[b][:, j * P:(j + 1) * P], src, self.con("ident"))
                last.then_inc(s["turned"], 1)
            last_head = isinstance(h, int) and h == MLA_H - 1
            fold = pe_ada_fold()
            if last_head:
                fold.then_inc(ada_rows, 1)
            else:
                pe_ada_half(1 - e, 0)
            vv = v[f"v{e}"].rearrange("p (t d) -> p t d", t=4)
            eng.wait_ge(s["pt_act"], 2 * h + 2)
            eng.wait_ge(s["pt_dve"], h + 1)
            for t in range(4):
                bl = ((0, 1), (2, 3), (4, 5, 6, 7), (8, 9, 10, 11))[t]
                last = self.mm(eng, bank[4][:, t * DV:(t + 1) * DV], [pt[:, b, :] for b in bl],
                               [vv[:, i, :] for i in range(len(bl))])
            last.then_inc(s["o_done"], 1)
            if not last_head:
                pe_ada_half(1 - e, 1).then_inc(ada_rows, 1)

        def dve_project(h, e):
            eng.wait_ge(s["proj_done"], h + 1)
            eng.tensor_copy(v[f"q{e}"][0:QK, :], bank[0][0:QK, :]).then_inc(s["q_copied"], 1)
            eng.wait_ge(s["q_copied"], h + 1)
            eng.tensor_tensor(v[f"qt{e}"][0:QK, :], v[f"q{e}"][0:QK, CTX:T], self.con("cos_mla")[0:QK, :],
                              ALU.mult).then_inc(link, 1)

        def dve_max(h, e):
            eng.wait_ge(s["rot_done"], h + 1)
            eng.tensor_tensor(v[f"qr{e}"][0:QK, :], bank[2][0:QK, 256:512], self.con("sin_mla")[0:QK, :],
                              ALU.mult).then_inc(link, 1)
            eng.wait_ge(link, self.mla_links(h, 0))
            eng.tensor_tensor(v[f"qr{e}"][0:QK, :], v[f"qr{e}"][0:QK, :], v[f"qt{e}"][0:QK, :],
                              ALU.add).then_inc(s["rotated"], 1)
            eng.wait_ge(s["scored"], 3 * h + 1)
            eng.tensor_reduce(mx[e][:, 0:2], bank[3][:, :].rearrange("p (t k) -> p t k", t=2), AX.X, ALU.max)
            for t in range(2):
                eng.wait_ge(s["scored"], 3 * h + 2 + t)
                last = eng.tensor_reduce(mx[e][:, 2 + t:3 + t], bank[4 + t][:, :], AX.X, ALU.max)
            last.then_inc(link, 1)
            eng.wait_ge(link, self.mla_links(h, 1))
            eng.tensor_scalar(nb[e], mx[e], -scale, None, ALU.mult).then_inc(s["max_ready"], 1)

        def dve_tail(h, e):
            eng.wait_ge(s["exp_done"], 4 * h + 4)
            eng.reciprocal(rc[e], rs[e]).then_inc(link, 1)
            eng.wait_ge(s["turned"], 3 * h + 2)
            eng.tensor_copy(v["pt"][:, 512:1024], bank[7][:, :]).then_inc(s["pt_dve"], 1)
            eng.wait_ge(s["o_done"], h + 1)
            eng.wait_ge(link, self.mla_links(h, 2))
            eng.tensor_tensor(v["o"][:, :, bass.ds(h * DV, DV)],
                              bank[4][:, 0:256].rearrange("p (t d) -> p t d", t=4),
                              rc[e].unsqueeze(2).to_broadcast([P, 4, DV]), ALU.mult).then_inc(s["o_used"], 1)
            eng.wait_ge(ada_rows, h + 2)
            eng.tensor_copy(flat[:, bass.ds(2 * ADA_FIRST + h * 2 * ADA_TILES, 2 * ADA_TILES)],
                            bank[5][:, fold_at])
            if not (isinstance(h, int) and h == MLA_H - 1):
                dve_ada_copy()

        def act_project(h, e):
            eng.wait_ge(s["proj_done"], h + 1)
            eng.copy(v[f"kt{e}"][0:DN, :], bank[1][0:DN, :]).then_inc(s["kv_copied"], 1)
            eng.copy(v[f"v{e}"], bank[2][:, 0:256]).then_inc(s["kv_copied"], 1)

        def act_exp(h, e):
            eng.wait_ge(s["max_ready"], h + 1)
            src = [bank[3][:, 0:256], bank[3][:, 256:512], bank[4][:, :], bank[5][:, :]]
            for t in range(4):
                eng.activation(ptiles[t], src[t], ACT.Exp, bias=nb[e][:, t:t + 1], scale=scale,
                               accum_out=rs[e][:, t:t + 1]).then_inc(s["exp_done"], 1)

        def act_tail(h, e):
            eng.wait_ge(s["turned"], 3 * h + 1)
            eng.copy(v["pt"][:, 0:512], bank[6][:, :]).then_inc(s["pt_act"], 1)
            eng.wait_ge(s["turned"], 3 * h + 3)
            eng.copy(v["pt"][:, 1024:1536], bank[3][:, :]).then_inc(s["pt_act"], 1)

        steps = {"pe": (pe_project, pe_scores, pe_tail), "dve": (dve_project, dve_max, dve_tail),
                 "act": (act_project, act_exp, act_tail)}[who]
        if who == "dve":
            eng.nop().then_inc(s["o_used"], 1)
        if who == "act":
            biases = self.N[:, :].rearrange("p (t h k) -> p t h k", t=2, h=16)
            for row in range(4):
                part = slice(64 * (row % 2), 64 * (row % 2) + 64)
                eng.dma_start(biases[part, row // 2, :, :], self.nab_d[row]).then_inc(self.bias_in, 16)

        def prologue():
            if who == "pe":
                pe_ada_half(0, 0)
                pe_ada_half(0, 1).then_inc(ada_rows, 1)
            if who == "dve":
                eng.wait_ge(ada_rows, 1)
                dve_ada_copy()
        self.pipelined(eng, MLA_H, *steps, prologue)
        self.phase_end(eng, who)
        self.ada_rest(who, eng)
        self.phase_end(eng, who)

    @staticmethod
    def mla_links(h, which):
        return h * 4 + (2, 3, 4 if isinstance(h, int) and h == MLA_H - 1 else 5)[which]

    def pipelined(self, eng, n, project, middle, tail, prologue=None):
        project(0, 0)
        if prologue:
            prologue()
        with eng.Fori(0, n // 2 - 1) as it:
            for e in range(2):
                u = it * 2 + e
                middle(u, e)
                project(u + 1, 1 - e)
                tail(u, e)
        for u in (n - 2, n - 1):
            middle(u, u % 2)
            if u + 1 < n:
                project(u + 1, (u + 1) % 2)
            tail(u, u % 2)

    def mla_out(self, who, eng):
        v = self.mla_views()
        o = v["o"]
        oT = self.B[:, 0:KT * T].rearrange("p (k t) -> p k t", k=KT)
        self.flip(who, eng, lambda t, k: o[:, t, k * P:(k + 1) * P], lambda k: oT[:, k, :], KT, 4, "mla")
        self.project_residual(who, eng, "mla_o", lambda k: oT[:, k, :], KT, 4, 2, 0, (0, 1))
        self.layer_norm(who, eng, 0, "ln1_g", "ln1_b", 0)

    def ffn(self, who, eng, layer):
        segs = (0, 1) if layer == 0 else (1,)
        c0 = CTX * segs[0]
        w = T - c0
        ns = len(segs)
        self.modulate(who, eng, layer, 3, 4, segs)
        name = f"ffn{layer}_"
        up_done, up_used, gate_in, gate_out, hid_done = \
            [self.sem(name + x) for x in ("up_done", "up_used", "gate_in", "gate_out", "hid_done")]
        link = self.sem(name + "link")
        hid = self.B[:, :].rearrange("p (f t) -> p f t", f=FT)
        cw, cb = VOFF["conv_w"][0] + layer * 3 * 2 * FT, VOFF["conv_b"][0] + layer * 2 * FT
        u = [[self.X[:, (2 * e + x) * T:(2 * e + x) * T + w] for x in range(2)] for e in range(2)]
        sg = [self.X[:, (4 + e) * T:(4 + e) * T + w] for e in range(2)]

        if who == "pe":
            def body(j, slot):
                for e in range(2):
                    f = j * 2 + e
                    if not (isinstance(j, int) and j == 0):
                        eng.wait_ge(up_used, f - 1)
                    for x in range(2):
                        m = 2 * x + e
                        last = self.mm(eng, self.bank[2 * e + x][:, 0:w],
                                       [slot[:, (m * KT + k) * P:(m * KT + k + 1) * P] for k in range(KT)],
                                       [self.A[:, k, c0:T] for k in range(KT)])
                    last.then_inc(up_done, 1)
            g = FIRST[f"ffn_in{layer}"]
            eng.wait_ge(self.w_loaded[g % 2], 16 * (g // 2 + 1))
            body(0, self.ring[g % 2])
            self.chunks(eng, f"ffn_in{layer}", body, count=CHUNKS[f"ffn_in{layer}"] - 1, start=1)

        def seg(ap, lo, hi):
            return ap.rearrange("p (s t) -> p s t", s=ns)[:, :, lo:hi]

        def conv(f, e):
            eng.wait_ge(up_done, f + 1)
            for tap, (olo, ohi, ilo, ihi) in enumerate(((None,) * 4, (1, 256, 0, 255), (0, 255, 1, 256))):
                for x in range(2):
                    src, dst = self.bank[2 * e + x][:, 0:w], u[e][x]
                    col = f + x * FT
                    if tap == 0:
                        ins = eng.tensor_scalar(dst, src, self.V[:, bass.ds(cw + 2 * FT + col, 1)],
                                                self.V[:, bass.ds(cb + col, 1)], ALU.mult, ALU.add)
                    else:
                        t = 0 if tap == 1 else 2
                        ins = eng.scalar_tensor_tensor(
                            out=seg(dst, olo, ohi), in0=seg(src, ilo, ihi),
                            scalar=self.V[:, bass.ds(cw + t * 2 * FT + col, 1)],
                            in1=seg(dst, olo, ohi), op0=ALU.mult, op1=ALU.add)
                if tap < 2:
                    ins.then_inc(link, 1)
                    eng.wait_ge(link, f * 2 + tap + 1)
            ins.then_inc(up_used, 1)

        def mult(f, e):
            eng.wait_ge(gate_out, f + 1)
            eng.wait_ge(up_used, f + 1)
            eng.tensor_tensor(hid[:, bass.ds(f, 1), 0:w].rearrange("p a t -> p (a t)"), u[e][0], sg[e],
                              ALU.mult).then_inc(hid_done, 1)
            eng.wait_ge(hid_done, f + 1)

        if who == "dve":
            conv(0, 0)
            with eng.Fori(0, FT // 2 - 1) as it:
                conv(it * 2 + 1, 1)
                mult(it * 2, 0)
                conv(it * 2 + 2, 0)
                mult(it * 2 + 1, 1)
            conv(FT - 1, 1)
            mult(FT - 2, 0)
            mult(FT - 1, 1)
        if who == "act":
            with eng.Fori(0, FT // 2) as it:
                for e in range(2):
                    f = it * 2 + e
                    eng.wait_ge(up_used, f + 1)
                    eng.activation(sg[e], u[e][1], ACT.Silu).then_inc(gate_out, 1)
        self.phase_end(eng, who)
        nm = f"ffn_out{layer}"
        self.project_residual(who, eng, nm, lambda k: hid[:, k, 0:w], FT, 2, 5, layer, segs)
        self.layer_norm(who, eng, c0, "ln2_g", "ln2_b", layer)
        if layer == 0:
            self.modulate(who, eng, 1, 0, 1, (0, 1))

    def na_views(self):
        b, v, at = self.B, {}, 0
        for name, n in (("q0", 2 * LAT), ("q1", 2 * LAT), ("k0", T), ("k1", T), ("v0", 4 * P), ("v1", 4 * P),
                        ("p", 4 * T), ("pt", 4 * T), ("o", 2 * D)):
            v[name] = b[:, at:at + n]
            at += n
        assert at <= FT * T
        return v

    def na_heads(self, who, eng):
        v = self.na_views()
        names = ("proj_done", "q_copied", "k_copied", "v_copied", "scored", "biased", "max_ready", "exp_done",
                 "turned", "pt_copied", "o_done", "o_used")
        s = {n: self.sem("na_" + n) for n in names}
        link = self.sem("na_link")
        bank = self.bank
        scale = 64 ** -0.5
        g0 = FIRST["na_pair"]
        sc = self.X[:, 0:4 * T].rearrange("p (n k) -> p n k", n=4)
        p = v["p"].rearrange("p (n k) -> p n k", n=4)
        pt = v["pt"].rearrange("p (n b q) -> p n b q", n=4, q=P)
        qz = [v[f"q{e}"].rearrange("p (h t) -> p h t", h=2) for e in range(2)]
        o = v["o"].rearrange("p (t d) -> p t d", t=2)
        nb_all = self.N[:, :].rearrange("p (t h k) -> p t h k", t=2, h=16)
        mx, nb, rs, rc = [[self.S[:, 64 + 16 * e + 4 * n:64 + 16 * e + 4 * n + 4] for e in range(2)]
                          for n in range(4)]
        pt_bank = (7, 3, 4, 5)
        if who == "dve":
            eng.wait_ge(self.bias_in, 64)
            for t in range(2):
                eng.tensor_tensor(nb_all[:, t, :, :], nb_all[:, t, :, :],
                                  self.con("na_mask").unsqueeze(1).to_broadcast([P, 16, LAT]), ALU.add)
            for e in range(2):
                eng.memset(qz[e], 0.0)
        self.phase_end(eng, who)

        def pe_project(u, e):
            slot = self.ring[(g0 + e) % 2]
            eng.wait_ge(self.w_loaded[(g0 + e) % 2], (u - e) * 8 + 16 * ((g0 + e) // 2 + 1))
            if not (isinstance(u, int) and u == 0):
                eng.wait_ge(s["q_copied"], u)
                eng.wait_ge(s["k_copied"], u)
                eng.wait_ge(s["v_copied"], u)
            self.mm(eng, bank[0][:, 0:LAT], [slot[:, k * P:(k + 1) * P] for k in range(KT)],
                    [self.A[:, k, CTX:T] for k in range(KT)])
            self.mm(eng, bank[1][:, :], [slot[:, D + k * P:D + (k + 1) * P] for k in range(KT)],
                    [self.A[:, k, :] for k in range(KT)])
            for t in range(4):
                last = self.mm(eng, bank[2][:, t * P:(t + 1) * P],
                               [self.A[:, k, t * P:(t + 1) * P] for k in range(KT)],
                               [slot[:, 2 * D + k * P:2 * D + (k + 1) * P] for k in range(KT)])
            last.then_inc(s["proj_done"], 1)

        def pe_scores(u, e):
            eng.wait_ge(s["q_copied"], u + 1)
            eng.wait_ge(s["k_copied"], u + 1)
            eng.wait_ge(s["o_used"], u + 1)
            for n in range(4):
                h, t = n // 2, n % 2
                eng.matmul(bank[3 + n][:, :], qz[e][:, h, t * P:(t + 1) * P], v[f"k{e}"],
                           start=True, stop=True).then_inc(s["scored"], 1)

        def pe_tail(u, e):
            for n in range(4):
                eng.wait_ge(s["exp_done"], 4 * u + n + 1)
                for b in range(4):
                    last = eng.transpose(bank[pt_bank[n]][:, b * P:(b + 1) * P], p[:, n, b * P:(b + 1) * P],
                                         self.con("ident"))
                last.then_inc(s["turned"], 1)
            eng.wait_ge(s["v_copied"], u + 1)
            vv = v[f"v{e}"].rearrange("p (t d) -> p t d", t=4)
            for n in range(4):
                eng.wait_ge(s["pt_copied"], 4 * u + n + 1)
                h = n // 2
                last = self.mm(eng, bank[6][:, n * 64:(n + 1) * 64], [pt[:, n, b, :] for b in range(4)],
                               [vv[:, b, h * 64:(h + 1) * 64] for b in range(4)])
            last.then_inc(s["o_done"], 1)

        def dve_project(u, e):
            eng.wait_ge(s["proj_done"], u + 1)
            eng.tensor_copy(qz[e][0:64, 0, :], bank[0][0:64, 0:LAT])
            eng.tensor_copy(qz[e][64:128, 1, :], bank[0][64:128, 0:LAT]).then_inc(s["q_copied"], 1)

        def dve_max(u, e):
            for n in range(4):
                h, t = n // 2, n % 2
                eng.wait_ge(s["scored"], 4 * u + n + 1)
                eng.tensor_scalar(sc[:, n, 0:CTX], bank[3 + n][:, 0:CTX], scale, None, ALU.mult)
                bias = nb_all[:, t, bass.ds(u * 2 + h, 1), :].rearrange("p a k -> p (a k)")
                eng.scalar_tensor_tensor(out=sc[:, n, CTX:T], in0=bank[3 + n][:, CTX:T], scalar=scale,
                                         in1=bias, op0=ALU.mult, op1=ALU.add).then_inc(s["biased"], 1)
            eng.wait_ge(s["biased"], 4 * u + 4)
            eng.tensor_reduce(mx[e], sc, AX.X, ALU.max).then_inc(link, 1)
            eng.wait_ge(link, 2 * u + 1)
            eng.tensor_scalar(nb[e], mx[e], -1.0, None, ALU.mult).then_inc(s["max_ready"], 1)

        def dve_tail(u, e):
            eng.wait_ge(s["exp_done"], 4 * u + 4)
            eng.reciprocal(rc[e], rs[e]).then_inc(link, 1)
            for n in range(4):
                eng.wait_ge(s["turned"], 4 * u + n + 1)
                eng.tensor_copy(v["pt"][:, n * T:(n + 1) * T], bank[pt_bank[n]][:, :])\
                    .then_inc(s["pt_copied"], 1)
            eng.wait_ge(s["o_done"], u + 1)
            eng.wait_ge(link, 2 * u + 2)
            for h in range(2):
                ins = eng.tensor_tensor(o[:, :, bass.ds(u * P + h * 64, 64)],
                                        bank[6][:, h * P:(h + 1) * P].rearrange("p (t d) -> p t d", t=2),
                                        rc[e][:, 2 * h:2 * h + 2].unsqueeze(2).to_broadcast([P, 2, 64]),
                                        ALU.mult)
            ins.then_inc(s["o_used"], 1)

        def act_project(u, e):
            eng.wait_ge(s["proj_done"], u + 1)
            eng.copy(v[f"k{e}"], bank[1][:, :]).then_inc(s["k_copied"], 1)
            eng.copy(v[f"v{e}"], bank[2][:, :]).then_inc(s["v_copied"], 1)

        def act_exp(u, e):
            eng.wait_ge(s["max_ready"], u + 1)
            for n in range(4):
                eng.activation(p[:, n, :], sc[:, n, :], ACT.Exp, bias=nb[e][:, n:n + 1], scale=1.0,
                               accum_out=rs[e][:, n:n + 1]).then_inc(s["exp_done"], 1)

        def act_tail(u, e):
            pass

        steps = {"pe": (pe_project, pe_scores, pe_tail), "dve": (dve_project, dve_max, dve_tail),
                 "act": (act_project, act_exp, act_tail)}[who]
        if who == "dve":
            eng.nop().then_inc(s["o_used"], 1)
        self.pipelined(eng, NA_PAIRS, *steps)
        self.phase_end(eng, who)

    def na_out(self, who, eng):
        v = self.na_views()
        o = v["o"].rearrange("p (t d) -> p t d", t=2)
        oT = self.X[:, 512:512 + KT * LAT].rearrange("p (k t) -> p k t", k=KT)
        self.flip(who, eng, lambda t, k: o[:, t, k * P:(k + 1) * P], lambda k: oT[:, k, :], KT, 2, "na")
        self.project_residual(who, eng, "na_o", lambda k: oT[:, k, :], KT, 4, 2, 1, (1,))
        self.layer_norm(who, eng, CTX, "ln1_g", "ln1_b", 1)

    def rms_to_input(self, who, eng, gain):
        def write(k, x, r):
            a = self.A[:, k, CTX:T]
            self.link(eng, who, eng.tensor_tensor(a, x, r, ALU.mult))
            self.link(eng, who, eng.tensor_scalar(a, a, self.vec(gain, k, 1), None, ALU.mult))
        self.norm(who, eng, CTX, write, centre=False, eps=RMS_EPS)

    def tile2(self, t, n=1):
        return self.B[:, t * LAT:(t + n) * LAT]

    def proj(self, who, eng):
        self.rms_to_input(who, eng, "attn_norm")
        done, used = self.sem("proj_tile_done"), self.sem("proj_tile_used")
        if who == "pe":
            def body(j, slot):
                for t in range(6):
                    if not (isinstance(j, int) and j == 0):
                        eng.wait_ge(used, j * 6 + t - 5)
                    last = self.mm(eng, self.bank[t][:, 0:LAT],
                                   [slot[:, (t * KT + k) * P:(t * KT + k + 1) * P] for k in range(KT)],
                                   [self.A[:, k, CTX:T] for k in range(KT)])
                    last.then_inc(done, 1)
            g = FIRST["proj"]
            eng.wait_ge(self.w_loaded[g % 2], 16 * (g // 2 + 1))
            body(0, self.ring[g % 2])
            self.chunks(eng, "proj", body, count=CHUNKS["proj"] - 1, start=1)
            for t in range(2):
                self.mm(eng, self.bank[6][:, t * 24:(t + 1) * 24],
                        [self.A[:, k, CTX + t * P:CTX + (t + 1) * P] for k in range(KT)],
                        [self.vec("w_gate24", k * 24, 24) for k in range(KT)])
        if who == "dve":
            with eng.Fori(0, CHUNKS["proj"]) as j:
                for t in range(6):
                    eng.wait_ge(done, j * 6 + t + 1)
                    eng.tensor_copy(self.B[:, bass.ds(j * (6 * LAT) + t * LAT, LAT)], self.bank[t][:, 0:LAT])\
                        .then_inc(used, 1)
        self.phase_end(eng, who)
        if who == "act":
            eng.activation(self.S[:, 0:48], self.bank[6][:, 0:48], ACT.Sigmoid)
            eng.activation(self.tile2(T_HF, 4), self.tile2(T_HF, 4), ACT.Sigmoid)
            eng.activation(self.tile2(T_MN, 16), self.tile2(T_MN, 16), ACT.Sigmoid)
            eng.activation(self.tile2(T_HGATE, 4), self.tile2(T_HGATE, 4), ACT.Silu)
        self.phase_end(eng, who)

    def nsa_views(self):
        n, x, v, at = self.N, self.X, {}, 0
        for name, w in (("qr", 4 * LAT), ("sk", LAT), ("wk", LAT), ("kc", 16), ("vc", P), ("vtok", 12 * P),
                        ("qz0", 2 * LAT // 2), ("qz1", 2 * LAT // 2), ("o_hg", 4 * LAT),
                        ("s0", 800), ("s1", 800), ("p0", 800), ("p1", 800)):
            v[name] = n[:, at:at + w]
            at += w
        assert at <= 16 * 2 * LAT, at
        v["at"] = v["s0"].offset
        at = 0
        for name, w in (("pt", 16 * P), ("o", 2 * 512), ("t0", 384), ("t1", 384)):
            v[name] = x[:, at:at + w]
            at += w
        assert at <= KT * T
        return v

    def compress(self, who, eng):
        v = self.nsa_views()
        bank = self.bank
        blk = [self.A[:, :, :].rearrange("p k t -> p (k t)")[:, 512 * x:512 * x + NCMP * 32]
               .rearrange("p (n l) -> p n l", l=32) for x in range(2)]
        vct = self.S[:, 48:64]
        if who == "dve":
            for x, tile in enumerate((T_CK, T_CV)):
                rows = self.tile2(tile).rearrange("p (n b) -> p n b", b=16)
                for a in range(2):
                    pos = self.vec("cmp_pos", 16 * a, 16).unsqueeze(1).to_broadcast([P, NCMP, 16])
                    eng.tensor_tensor(blk[x][:, :, 16 * a:16 * a + 16], rows[:, a:a + NCMP, :], pos, ALU.add)
            eng.memset(v["kc"], 0.0)
            eng.memset(vct, 0.0)
        self.phase_end(eng, who)
        tiles = [T_Q, T_Q + 1, T_Q + 2, T_Q + 3, T_SK, T_WK]
        turn = [T_SV, T_WV, T_HI, T_HI + 1, T_HI + 2, T_HI + 3]
        vtok = v["vtok"].rearrange("p (t m d) -> p t m d", t=2, m=6)
        if who == "pe":
            for x in range(2):
                g = FIRST["cmp"] + x
                eng.wait_ge(self.w_loaded[g % 2], 16 * (g // 2 + 1))
                slot = self.ring[g % 2]
                self.mm(eng, bank[x][:, 0:NCMP], [slot[:, l * P:(l + 1) * P] for l in range(32)],
                        [blk[x][:, :, l] for l in range(32)]).then_inc(self.sem("cmp_used"), 1)
            for i, t in enumerate(tiles):
                eng.matmul(bank[2 + i // 2][:, (i % 2) * LAT:(i % 2 + 1) * LAT], self.con("rot_nsa"),
                           self.tile2(t), start=True, stop=True)
            for i, t in enumerate(turn):
                for tt in range(2):
                    b = 5 + i // 2
                    c = (i % 2) * LAT + tt * P
                    eng.transpose(bank[b][:, c:c + P], self.tile2(t)[:, tt * P:(tt + 1) * P], self.con("ident"))
        self.phase_end(eng, who)
        if who == "dve":
            eng.tensor_copy(v["kc"][:, 0:NCMP], bank[0][:, 0:NCMP])
            eng.tensor_copy(vct[:, 0:NCMP], bank[1][:, 0:NCMP])
            for i, t in enumerate(tiles):
                dst = v["qr"][:, i * LAT:(i + 1) * LAT] if i < 4 else v["sk" if i == 4 else "wk"]
                src = self.tile2(t)
                self.link(eng, who, eng.tensor_tensor(src, src, self.con("cos_nsa"), ALU.mult))
                self.link(eng, who, eng.tensor_tensor(dst, bank[2 + i // 2][:, (i % 2) * LAT:(i % 2 + 1) * LAT],
                                                      self.con("sin_nsa"), ALU.mult))
                self.link(eng, who, eng.tensor_tensor(dst, dst, src, ALU.add))
        if who == "act":
            for i in range(6):
                for tt in range(2):
                    c = (i % 2) * LAT + tt * P
                    eng.copy(vtok[:, tt, i, :], bank[5 + i // 2][:, c:c + P])
        self.phase_end(eng, who)
        if who == "pe":
            eng.matmul(bank[0][:, 0:16], self.con("rot_nsa"), v["kc"], start=True, stop=True)
            eng.transpose(bank[1][0:16, 0:P], vct, self.con("ident"))
        self.phase_end(eng, who)
        if who == "dve":
            at16 = [self.con(c).rearrange("p (n b) -> p n b", b=16)[:, :, 0] for c in ("cos_nsa", "sin_nsa")]
            tmp = self.S[:, 64:80]
            self.link(eng, who, eng.tensor_tensor(tmp, bank[0][:, 0:16], at16[1], ALU.mult))
            self.link(eng, who, eng.tensor_tensor(v["kc"], v["kc"], at16[0], ALU.mult))
            eng.tensor_tensor(v["kc"], v["kc"], tmp, ALU.add)
            eng.tensor_copy(v["vc"][0:16, :], bank[1][0:16, 0:P])
            eng.memset(v["qz0"], 0.0)
            eng.memset(v["qz1"], 0.0)
        self.phase_end(eng, who)

    def nsa_heads(self, who, eng):
        v = self.nsa_views()
        names = ("q_ready", "scored", "max_ready", "exp_done", "kept", "turned", "pt_copied", "o_done")
        s = {n: self.sem("nsa_" + n) for n in names}
        link = self.sem("nsa_link")
        bank = self.bank
        scale = 64 ** -0.5
        qz = [v["qz0"], v["qz1"]]
        sc, p = [v["s0"], v["s1"]], [v["p0"], v["p1"]]
        pt = v["pt"].rearrange("p (e b q) -> p e b q", e=2, q=P)
        o = v["o"].rearrange("p (t d) -> p t d", t=2)
        tmp = [v[f"t{e}"].rearrange("p (b t d) -> p b t d", b=3, t=2) for e in range(2)]
        vtok = v["vtok"].rearrange("p (t m d) -> p t m d", t=2, m=6)
        mx, nb, rs, fc = [[self.S[:, 64 + 32 * e + 6 * n:64 + 32 * e + 6 * n + 6] for e in range(2)]
                          for n in range(4)]
        segs = [(0, 128), (128, 384), (384, 400), (400, 416), (416, 544), (544, 800)]
        sb = [(3, 4), (5, 6)]
        tb = [(7, 0), (1, 2)]
        blocks = [(0, 128), (128, 256), (256, 384), (384, 400), (416, 544), (544, 672), (672, 800), (400, 416)]
        gates = self.S[:, 0:48].rearrange("p (t c) -> p t c", t=2)
        LINKS = 8
        with eng.Fori(0, NSA_PAIRS) as it:
            if who == "pe":
                eng.wait_ge(s["q_ready"], it + 1)
                for e in range(2):
                    a, b = (bank[i] for i in sb[e])
                    q = qz[e]
                    for k, bk in ((v["sk"], a), (v["wk"], b)):
                        eng.matmul(bk[:, 0:128], q[:, 0:P], k[:, 0:P], start=True, stop=True)
                        last = eng.matmul(bk[:, 128:384], q[:, P:LAT], k, start=True, stop=True)
                    for t in range(2):
                        last = eng.matmul(a[:, 384 + 16 * t:400 + 16 * t], q[:, t * P:(t + 1) * P], v["kc"],
                                          start=True, stop=True)
                    last.then_inc(s["scored"], 1)
                for e in range(2):
                    eng.wait_ge(s["kept"], it * 2 + e + 1)
                    for i, (lo, hi) in enumerate(blocks):
                        last = eng.transpose(bank[tb[e][i // 4]][0:hi - lo, (i % 4) * P:(i % 4 + 1) * P],
                                             p[e][:, lo:hi], self.con("ident"))
                    last.then_inc(s["turned"], 1)
                for e in range(2):
                    eng.wait_ge(s["pt_copied"], it * 4 + 2 * e + 2)
                    ob = bank[sb[e][0]]
                    g = slice(64 * e, 64 * e + 64)

                    def out(i):
                        return ob[:, i * 64:(i + 1) * 64]
                    for br, m, b0 in ((0, 0, 0), (2, 1, 4)):
                        eng.matmul(out(2 * br), pt[:, e, b0, :], vtok[:, 0, m, g], start=True, stop=True)
                        self.mm(eng, out(2 * br + 1), [pt[:, e, b0 + 1, :], pt[:, e, b0 + 2, :]],
                                [vtok[:, 0, m, g], vtok[:, 1, m, g]])
                    for t in range(2):
                        last = eng.matmul(out(2 + t), pt[0:16, e, (3, 7)[t], :], v["vc"][0:16, g],
                                          start=True, stop=True)
                    last.then_inc(s["o_done"], 1)
            if who == "dve":
                for e in range(2):
                    r = slice(64 * e, 64 * e + 64)
                    last = eng.tensor_copy(qz[e][r, :], v["qr"][r, bass.ds(it * LAT, LAT)])
                last.then_inc(s["q_ready"], 1)
                for e in range(2):
                    eng.wait_ge(s["scored"], it * 2 + e + 1)
                    eng.scalar_tensor_tensor(out=sc[e][:, 0:416], in0=bank[sb[e][0]][:, 0:416], scalar=scale,
                                             in1=self.con("nsa_mask"), op0=ALU.mult, op1=ALU.add)
                    eng.scalar_tensor_tensor(out=sc[e][:, 416:800], in0=bank[sb[e][1]][:, 0:384],
                                             scalar=scale, in1=self.con("nsa_mask", 0, 384), op0=ALU.mult,
                                             op1=ALU.add).then_inc(link, 1)
                    eng.wait_ge(link, it * LINKS + 2 * e + 1)
                    for i, (lo, hi) in enumerate(segs):
                        last = eng.tensor_reduce(mx[e][:, i:i + 1], sc[e][:, lo:hi], AX.X, ALU.max)
                    last.then_inc(link, 1)
                    eng.wait_ge(link, it * LINKS + 2 * e + 2)
                    eng.tensor_scalar(nb[e], mx[e], -1.0, None, ALU.mult).then_inc(s["max_ready"], 1)
                for e in range(2):
                    eng.wait_ge(s["exp_done"], it * 2 + e + 1)
                    eng.tensor_tensor(p[e][:, 384:416], p[e][:, 384:416], self.con("cmp_keep"), ALU.mult)\
                        .then_inc(s["kept"], 1)
                    eng.reciprocal(fc[e], rs[e]).then_inc(link, 1)
                    eng.wait_ge(link, it * LINKS + 2 * e + 5)
                    f = fc[e].rearrange("p (b t) -> p b t", t=2)
                    eng.tensor_tensor(f, f, gates[:, :, bass.ds(it * 6 + 3 * e, 3)].rearrange("p t b -> p b t"),
                                      ALU.mult).then_inc(link, 1)
                for e in range(2):
                    eng.wait_ge(s["turned"], it * 2 + e + 1)
                    for half in range(2):
                        eng.tensor_copy(pt[:, e, 4 * half:4 * half + 3, :],
                                        bank[tb[e][half]][:, 0:384].rearrange("p (b q) -> p b q", q=P))
                        eng.tensor_copy(pt[0:16, e, 4 * half + 3, :], bank[tb[e][half]][0:16, 384:512])\
                            .then_inc(s["pt_copied"], 1)
                for e in range(2):
                    eng.wait_ge(s["o_done"], it * 2 + e + 1)
                    eng.wait_ge(link, it * LINKS + 2 * e + 6)
                    eng.tensor_tensor(v[f"t{e}"].rearrange("p (i d) -> p i d", d=64),
                                      bank[sb[e][0]][:, 0:384].rearrange("p (i d) -> p i d", d=64),
                                      fc[e].unsqueeze(2).to_broadcast([P, 6, 64]), ALU.mult)\
                        .then_inc(self.sem("nsa_weighted"), 1)
                    eng.wait_ge(self.sem("nsa_weighted"), it * 4 + 2 * e + 1)
                    dst = o[:, :, bass.ds(it * 64 + 256 * e, 64)]
                    eng.tensor_tensor(tmp[e][:, 0, :, :], tmp[e][:, 0, :, :], tmp[e][:, 1, :, :], ALU.add)\
                        .then_inc(self.sem("nsa_weighted"), 1)
                    eng.wait_ge(self.sem("nsa_weighted"), it * 4 + 2 * e + 2)
                    eng.tensor_tensor(dst, tmp[e][:, 0, :, :], tmp[e][:, 2, :, :], ALU.add)
            if who == "act":
                for e in range(2):
                    eng.wait_ge(s["max_ready"], it * 2 + e + 1)
                    for i, (lo, hi) in enumerate(segs):
                        last = eng.activation(p[e][:, lo:hi], sc[e][:, lo:hi], ACT.Exp, bias=nb[e][:, i:i + 1],
                                              scale=1.0, accum_out=rs[e][:, i:i + 1])
                    last.then_inc(s["exp_done"], 1)
        self.phase_end(eng, who)

    def hgrn(self, who, eng):
        v = self.nsa_views()
        bank = self.bank
        af = self.A[:, :, :].rearrange("p k t -> p (k t)")
        logf, K, E, KL = [af[:, 1024 * i:1024 * (i + 1)] for i in range(4)]
        QL = self.X[:, 0:1024]
        b = self.X[:, 3072:4096]
        n0 = 16 * 2 * LAT - 3 * 1024
        diag = self.N[:, n0:n0 + 1024]
        tmp = self.N[:, n0 + 1024:n0 + 2048]
        off = self.N[:, n0 + 2048:n0 + 2560]
        q, f = self.tile2(T_HQ, 4), self.tile2(T_HF, 4)
        o = v["o_hg"]
        vtok = v["vtok"].rearrange("p (t m d) -> p t m d", t=2, m=6)
        lo = self.S[:, 64:96]
        if who == "dve":
            a0, a1 = self.vec("hg_lb", 0, HG), self.vec("hg_lb", HG, HG)
            self.link(eng, who, eng.tensor_tensor(lo[:, 8:12], a0, a1, ALU.max))
            eng.tensor_tensor(lo[:, 0:4], a0, lo[:, 8:12], ALU.subtract)
            eng.tensor_tensor(lo[:, 4:8], a1, lo[:, 8:12], ALU.subtract)
        self.phase_end(eng, who)
        if who == "act":
            eng.activation(lo[:, 0:8], lo[:, 0:8], ACT.Exp)
        self.phase_end(eng, who)
        if who == "dve":
            self.link(eng, who, eng.tensor_tensor(lo[:, 8:12], lo[:, 0:4], lo[:, 4:8], ALU.add))
            self.link(eng, who, eng.reciprocal(lo[:, 8:12], lo[:, 8:12]))
            self.link(eng, who, eng.tensor_tensor(lo[:, 0:4], lo[:, 0:4], lo[:, 8:12], ALU.mult))
            self.link(eng, who, eng.tensor_scalar(lo[:, 4:8], lo[:, 0:4], -1.0, 1.0, ALU.mult, ALU.add))
            for h in range(HG):
                fh = f[:, h * LAT:(h + 1) * LAT]
                last = eng.tensor_scalar(fh, fh, lo[:, 4 + h:5 + h], lo[:, h:h + 1], ALU.mult, ALU.add)
            self.link(eng, who, last)
            eng.tensor_scalar(K, f, -1.0, 1.0, ALU.mult, ALU.add)
        self.phase_end(eng, who)
        if who == "act":
            eng.activation(logf, f, ACT.Ln)
        self.phase_end(eng, who)
        if who == "dve":
            for h in range(HG):
                c = slice(h * LAT, (h + 1) * LAT)
                last = eng.tensor_tensor_scan(b[:, c], self.con("scan_keep"), logf[:, c], 0.0,
                                              ALU.mult, ALU.add)
            self.link(eng, who, last)

        def exponents(level):
            if level == 128:
                bb, ee = [x.rearrange("p (h c t) -> p h c t", h=HG, c=4) for x in (b, E)]
                end = lambda c: bb[:, :, c, 63:64].to_broadcast([P, HG, 64])
                eng.tensor_tensor(ee[:, :, 1, :], end(1), bb[:, :, 1, :], ALU.subtract)
                self.link(eng, who, eng.tensor_tensor(ee[:, :, 0, :], end(0), bb[:, :, 0, :], ALU.subtract))
                eng.tensor_tensor(ee[:, :, 0, :], ee[:, :, 0, :], end(1), ALU.add)
                eng.tensor_copy(ee[:, :, 2, :], bb[:, :, 2, :])
                return eng.tensor_tensor(ee[:, :, 3, :], bb[:, :, 3, :], end(2), ALU.add)
            m = level
            bb, ee = [x.rearrange("p (n s t) -> p n s t", s=2, t=m) for x in (b, E)]
            n = 1024 // (2 * m)
            ref = bb[:, :, 0, m - 1:m].to_broadcast([P, n, m])
            eng.tensor_tensor(ee[:, :, 0, :], ref, bb[:, :, 0, :], ALU.subtract)
            if m == 64:
                return eng.tensor_copy(ee[:, :, 1, :], bb[:, :, 1, :])
            return eng.tensor_tensor(ee[:, :, 1, :], bb[:, :, 1, :], ref, ALU.subtract)

        e_ready, x_ready, kq_ready, mm_done = \
            [self.sem("hg_" + x) for x in ("exponents", "decays", "decayed", "products")]
        levels = [128] + LEVELS
        nl = len(levels)
        if who == "dve":
            exponents(128).then_inc(e_ready, 1)
            for i in range(nl + 1):
                if i < nl:
                    eng.wait_ge(x_ready, i + 1)
                    eng.tensor_tensor(KL, K, E, ALU.mult)
                    eng.tensor_tensor(QL, q, E, ALU.mult).then_inc(kq_ready, 1)
                if i + 1 < nl:
                    eng.wait_ge(kq_ready, i + 1)
                    exponents(levels[i + 1]).then_inc(e_ready, 1)
                eng.wait_ge(mm_done, i + 1)
                if i == 0:
                    eng.tensor_copy(off, bank[0][:, :])
                    continue
                mask = self.con("level_mask", (i - 1) * P, P).unsqueeze(1).to_broadcast([P, 4, P])
                for half in range(2):
                    src = bank[2 * (i % 2) + half][:, :].rearrange("p (n t) -> p n t", n=4)
                    dst = (diag if i == 1 else tmp)[:, 512 * half:512 * half + 512]
                    last = eng.tensor_tensor(dst.rearrange("p (n t) -> p n t", n=4), src, mask, ALU.mult)
                self.link(eng, who, last)
                if i > 1:
                    self.link(eng, who, eng.tensor_tensor(diag, diag, tmp, ALU.add))
        if who == "act":
            for i in range(nl):
                eng.wait_ge(e_ready, i + 1)
                eng.activation(E, E, ACT.Exp).then_inc(x_ready, 1)
        if who == "pe":
            for i in range(nl + 1):
                if i < nl:
                    eng.wait_ge(kq_ready, i + 1)
                kk, qq = (KL, QL) if i < nl else (K, q)
                for h in range(HG):
                    if i == 0:
                        last = eng.matmul(bank[0][:, h * P:(h + 1) * P], kk[:, h * LAT:h * LAT + P],
                                          qq[:, h * LAT + P:(h + 1) * LAT], start=True, stop=True)
                        continue
                    for st in range(2):
                        c = slice(h * LAT + st * P, h * LAT + (st + 1) * P)
                        j = 2 * h + st
                        last = eng.matmul(bank[2 * (i % 2) + j // 4][:, (j % 4) * P:(j % 4 + 1) * P],
                                          kk[:, c], qq[:, c], start=True, stop=True)
                last.then_inc(mm_done, 1)
        self.phase_end(eng, who)
        if who == "pe":
            for h in range(HG):
                ob = bank[4 + h // 2][:, (h % 2) * LAT:(h % 2 + 1) * LAT]
                eng.matmul(ob[:, 0:P], vtok[:, 0, 2 + h, :], diag[:, 2 * h * P:(2 * h + 1) * P],
                           start=True, stop=True)
                self.mm(eng, ob[:, P:LAT], [vtok[:, 0, 2 + h, :], vtok[:, 1, 2 + h, :]],
                        [off[:, h * P:(h + 1) * P], diag[:, (2 * h + 1) * P:(2 * h + 2) * P]])
        self.phase_end(eng, who)
        if who == "act":
            for i in range(2):
                eng.activation(KL[:, 512 * i:512 * i + 512], bank[4 + i][:, :], ACT.Square)
        self.phase_end(eng, who)
        if who == "pe":
            for i in range(2):
                eng.matmul(bank[i][:, :], self.con("ones"), KL[:, 512 * i:512 * i + 512], start=True, stop=True)
        self.phase_end(eng, who)
        if who == "dve":
            for i in range(2):
                eng.tensor_scalar(QL[:, 512 * i:512 * i + 512], bank[i][:, :], 1.0 / P, RMS_EPS,
                                  ALU.mult, ALU.add)
        self.phase_end(eng, who)
        if who == "act":
            eng.activation(QL, QL, ACT.Sqrt)
        self.phase_end(eng, who)
        if who == "dve":
            self.link(eng, who, eng.reciprocal(QL, QL))
            for i in range(2):
                c = slice(512 * i, 512 * i + 512)
                last = eng.tensor_tensor(o[:, c], bank[4 + i][:, :], QL[:, c], ALU.mult)
            self.link(eng, who, last)
            self.link(eng, who, eng.scalar_tensor_tensor(out=o, in0=o, scalar=self.vec("hg_norm"),
                                                         in1=self.tile2(T_HGATE, 4), op0=ALU.mult, op1=ALU.mult))
        self.phase_end(eng, who)

    def branches(self, who, eng):
        v = self.nsa_views()
        o = v["o"].rearrange("p (t d) -> p t d", t=2)
        oT = v["qr"].rearrange("p (k t) -> p k t", k=4)
        oh = v["o_hg"].rearrange("p (k t) -> p k t", k=4)
        self.flip(who, eng, lambda t, k: o[:, t, k * P:(k + 1) * P], lambda k: oT[:, k, :], 4, 2, "nsa")
        done, used = self.sem("branch_done"), self.sem("branch_used")
        bank = self.bank
        mixed = self.B[:, 0:KT * LAT].rearrange("p (k t) -> p k t", k=KT)
        tmp = self.X[:, 0:LAT]
        if who == "pe":
            g = FIRST["branch"]
            for s in range(2):
                eng.wait_ge(self.w_loaded[(g + s) % 2], 16 * ((g + s) // 2 + 1))
            for oc in range(KT):
                if oc >= 2:
                    eng.wait_ge(used, oc - 1)
                for s, r in enumerate((oT, oh)):
                    slot = self.ring[(g + s) % 2]
                    last = self.mm(eng, bank[2 * (oc % 2) + s][:, 0:LAT],
                                   [slot[:, (oc * 4 + k) * P:(oc * 4 + k + 1) * P] for k in range(4)],
                                   [r[:, k, :] for k in range(4)])
                last.then_inc(done, 1)
        if who == "dve":
            for oc in range(KT):
                eng.wait_ge(done, oc + 1)
                self.link(eng, who, eng.tensor_tensor(tmp, bank[2 * (oc % 2)][:, 0:LAT], self.tile2(T_MN + oc),
                                                      ALU.mult))
                eng.tensor_tensor(mixed[:, oc, :], bank[2 * (oc % 2) + 1][:, 0:LAT], self.tile2(T_MH + oc),
                                  ALU.mult).then_inc(used, 1)
                eng.wait_ge(used, oc + 1)
                self.link(eng, who, eng.tensor_tensor(mixed[:, oc, :], mixed[:, oc, :], tmp, ALU.add))
        self.phase_end(eng, who)
        self.project_residual(who, eng, "w_out", lambda k: mixed[:, k, :], KT, 4, None, 0, (1,))

    def router(self, who, eng):
        self.rms_to_input(who, eng, "ffn_norm")
        if who == "pe":
            for t in range(2):
                self.mm(eng, self.bank[0][:, t * 36:(t + 1) * 36],
                        [self.A[:, k, CTX + t * P:CTX + (t + 1) * P] for k in range(KT)],
                        [self.vec("w_route", k * 36, 36) for k in range(KT)])
        self.phase_end(eng, who)
        x = self.X
        lg = x[:, 0:72].rearrange("p (t c) -> p t c", t=2)
        at = [72]

        def small(*shape):
            n = 2 * int(np.prod(shape)) if shape else 2
            r = x[:, at[0]:at[0] + n]
            at[0] += n
            return r.rearrange("p (t c) -> p t c", t=2)
        gm, ge, gs, gp = small(1), small(4), small(1), small(1)
        oneg, pref, pm = small(4), small(8), small(1)
        sel, ing = small(32), small(8)
        m1, o1, m2, o2, x2 = small(1), small(8), small(1), small(8), small(8)
        d, w1, w2 = small(1), small(1), small(1)
        comb = small(8)
        member, late, count = x[:, at[0]:at[0] + 64], x[:, at[0] + 64:at[0] + 128], x[:, at[0] + 128:at[0] + 129]
        C = self.S[:, 0:64].rearrange("p (t g c) -> p t g c", t=2, g=GROUPS)

        def L(ins):
            self.link(eng, who, ins)

        def one_hot(dst, src, m, first, n):
            pr = pref[:, :, 0:n]
            L(eng.tensor_tensor(dst, src, m.to_broadcast([P, 2, n]), ALU.is_equal))
            L(eng.tensor_tensor(pr, dst, self.con(first).unsqueeze(1).to_broadcast([P, 2, n]), ALU.mult))
            L(eng.tensor_reduce(pm, pr, AX.X, ALU.max))
            L(eng.tensor_tensor(dst, pr, pm.to_broadcast([P, 2, n]), ALU.is_equal))
        if who == "dve":
            br = self.vec("b_route").unsqueeze(1).to_broadcast([P, 2, 36])
            L(eng.tensor_tensor(lg, self.bank[0][:, 0:72].rearrange("p (t c) -> p t c", t=2), br, ALU.add))
            gl, el = lg[:, :, 0:4], lg[:, :, 4:36].rearrange("p t (g c) -> p t g c", g=GROUPS)
            L(eng.tensor_reduce(gm, gl, AX.X, ALU.max))
            L(eng.tensor_tensor(ge, gl, gm.to_broadcast([P, 2, 4]), ALU.subtract))
            one_hot(oneg, gl, gm, "first4", 4)
            s4 = sel.rearrange("p t (g c) -> p t g c", g=GROUPS)
            for t in range(2):
                L(eng.tensor_tensor(s4[:, t, :, :], el[:, t, :, :],
                                    oneg[:, t, :].unsqueeze(2).to_broadcast([P, 4, 8]), ALU.mult))
                L(eng.tensor_reduce(ing[:, t, :], s4[:, t, :, :].rearrange("p g c -> p c g"), AX.X, ALU.add))
            L(eng.tensor_reduce(m1, ing, AX.X, ALU.max))
            one_hot(o1, ing, m1, "first8", 8)
            L(eng.scalar_tensor_tensor(out=x2, in0=o1, scalar=-HUGE, in1=ing, op0=ALU.mult, op1=ALU.add))
            L(eng.tensor_reduce(m2, x2, AX.X, ALU.max))
            one_hot(o2, x2, m2, "first8", 8)
            L(eng.tensor_tensor(d, m2, m1, ALU.subtract))
        self.phase_end(eng, who)
        if who == "act":
            eng.activation(ge, ge, ACT.Exp)
            eng.activation(d, d, ACT.Exp)
        self.phase_end(eng, who)
        if who == "dve":
            L(eng.tensor_reduce(gs, ge, AX.X, ALU.add))
            L(eng.reciprocal(gp, gs))
            L(eng.tensor_scalar(w1, d, 1.0, None, ALU.add))
            L(eng.reciprocal(w1, w1))
            L(eng.tensor_tensor(w1, w1, gp, ALU.mult))
            L(eng.tensor_tensor(w2, w1, d, ALU.mult))
            L(eng.tensor_tensor(o1, o1, w1.to_broadcast([P, 2, 8]), ALU.mult))
            L(eng.tensor_tensor(o2, o2, w2.to_broadcast([P, 2, 8]), ALU.mult))
            L(eng.tensor_tensor(comb, o1, o2, ALU.add))
            for t in range(2):
                L(eng.tensor_tensor(C[:, t, :, :], comb[:, t, :].unsqueeze(1).to_broadcast([P, 4, 8]),
                                    oneg[:, t, :].unsqueeze(2).to_broadcast([P, 4, 8]), ALU.mult))
            eng.memset(self.rank(), -1.0)
            L(eng.tensor_scalar(member, self.S[:, 0:64], 0.0, None, ALU.not_equal))
        self.phase_end(eng, who)
        if who == "pe":
            eng.matmul(self.bank[0][:, 0:32], self.con("before"), member[:, 0:32], start=True, stop=True)
            self.mm(eng, self.bank[0][:, 32:64], [self.con("before"), self.con("ones")],
                    [member[:, 32:64], member[:, 0:32]])
        self.phase_end(eng, who)
        if who == "dve":
            r = self.rank()
            L(eng.scalar_tensor_tensor(out=late, in0=self.bank[0][:, 0:64], scalar=1.0, in1=member,
                                       op0=ALU.add, op1=ALU.mult))
            L(eng.tensor_scalar(r[:, :, 0:EXPERTS], late.rearrange("p (t c) -> p t c", t=2), -1.0, None, ALU.add))
            L(eng.tensor_scalar(late.rearrange("p (t c) -> p t c", t=2), r[:, :, 0:EXPERTS], float(SLOTS), None,
                                ALU.is_ge))
            eng.tensor_reduce(count, late, AX.X, ALU.add)
            eng.tensor_tensor(self.late_weights(), self.S[:, 0:64], late, ALU.mult)
        self.phase_end(eng, who)
        if who == "pe":
            eng.matmul(self.bank[0][0:1, 0:1], self.con("ones", 0, 1), count, start=True, stop=True)
            for t in range(2):
                for k in range(KT):
                    eng.transpose(self.bank[1 + 2 * t + k // 4][:, (k % 4) * P:(k % 4 + 1) * P],
                                  self.A[:, k, CTX + t * P:CTX + (t + 1) * P], self.con("ident"))
        self.phase_end(eng, who)
        m = self.moe_views()
        if who == "dve":
            eng.tensor_copy(self.overflow[:, :], self.bank[0][0:1, 0:1])
            for j in range(2):
                eng.tensor_copy(m["xt"][:, 512 * j:512 * j + 512], self.bank[1 + j][:, :])
            for n in ("zero", "gwt", "ya", "yb"):
                eng.memset(m[n], 0.0)
        if who == "act":
            for j in range(2, 4):
                eng.copy(m["xt"][:, 512 * j:512 * j + 512], self.bank[1 + j][:, :])
        self.phase_end(eng, who)
        self.router_phase = 3 * self.phases[who]

    def rank(self):
        return self.S[:, 64:64 + 2 * (EXPERTS + 2)].rearrange("p (t c) -> p t c", t=2)

    def late_weights(self):
        return self.S[:, 132:196]

    def moe_views(self):
        v, at = {}, 0
        for name, n in (("acc", 2 * D), ("xt", 2 * D), ("xe", KT * P), ("zero", 512), ("g", 2 * P),
                        ("gwa", 2 * P), ("gwb", 2 * P), ("gwt", 4 * P), ("sg", 256), ("hid", 256),
                        ("hidt", 256), ("ya", 512), ("yb", 512), ("late_sg", FET * LAT),
                        ("late_hid", FET * LAT)):
            v[name] = self.arena[:, at:at + n]
            at += n
        assert at <= FT * T
        return v

    def moe(self, who, eng):
        v = self.moe_views()
        names = ("g_ready", "gw_ready", "gathered", "xe_act", "xe_dve", "gate_done", "up_done", "silu_done",
                 "hid_ready", "gwt_turned", "gwt_copied", "hid_turned", "hidt_copied", "down_done",
                 "y_copied")
        s = {n: self.sem("moe_" + n) for n in names}
        link = self.sem("moe_link")
        bank = self.bank
        slots, loaded = self.expert_slots(), self.expert_loaded()
        xt = v["xt"].rearrange("p (t d) -> p t d", t=2)
        xe = v["xe"].rearrange("p (k c) -> p k c", k=KT)
        gm, gwa, gwb = [v[n].rearrange("p (t e c) -> p t e c", t=2, e=2) for n in ("g", "gwa", "gwb")]
        gwt = v["gwt"].rearrange("p (n c) -> p n c", n=4)
        hidt = v["hidt"]
        C = self.S[:, 0:64].rearrange("p (t c) -> p t c", t=2)
        rank = self.rank()
        lo, hi = slice(0, 64), slice(64, 128)

        def gather(n):
            eng.wait_ge(s["g_ready"], n)
            for k in range(KT):
                last = self.mm(eng, bank[k // 4][:, (k % 4) * P:(k % 4 + 1) * P],
                               [xt[:, t, k * P:(k + 1) * P] for t in range(2)],
                               [gm[:, t, :, :].rearrange("p e c -> p (e c)") for t in range(2)])
            last.then_inc(s["gathered"], 1)

        def one_hots(pair):
            for t in range(2):
                ins = eng.tensor_tensor(gm[:, t, :, :], self.con("slot").unsqueeze(1).to_broadcast([P, 2, SLOTS]),
                                        rank[:, t, bass.ds(pair * 2, 2)].unsqueeze(2).to_broadcast([P, 2, SLOTS]),
                                        ALU.is_equal)
            ins.then_inc(s["g_ready"], 1)

        def project(x, e):
            for k in range(KT):
                for half in range(2):
                    o = (x * KT + k) * FE + half * 256
                    last = eng.matmul(bank[x][64 * half:64 * half + 64, 0:256], xe[:, k, 64 * e:64 * e + 64],
                                      slots[e][:, o:o + 256], start=(k == 0), stop=(k == KT - 1),
                                      skip_group_check=True)
            return last

        def turn_hidden():
            for c in range(2):
                last = eng.transpose(bank[3][:, c * P:(c + 1) * P], v["hid"][:, c * P:(c + 1) * P],
                                     self.con("ident"))
            last.then_inc(s["hid_turned"], 1)

        def down(e):
            for f in range(FET):
                for h in range(2):
                    grp = h if e == 0 else 1 - h
                    o = UPS + f * D + h * 512
                    at = (f % 2) * P + (f // 2) * 64
                    last = eng.matmul(bank[2][64 * grp:64 * grp + 64, :], hidt[:, at:at + 64],
                                      slots[e][:, o:o + 512], start=(f == 0), stop=(f == FET - 1),
                                      skip_group_check=True)
            last.then_inc(s["down_done"], 1)

        def scatter():
            for h, y in enumerate((v["ya"], v["yb"])):
                for t in range(2):
                    eng.matmul(bank[4 + 2 * t + h][:, :], gwt[:, 2 * h + t, :], y, start=False,
                               stop=False, skip_group_check=True)

        if who == "pe":
            for b in range(4, 8):
                eng.matmul(bank[b][:, :], v["zero"][:, 0:P], v["zero"], start=True, stop=False,
                           skip_group_check=True)
            eng.nop().then_inc(s["y_copied"], 1)
            gather(1)
            with eng.Fori(0, EXPERTS // 2) as i:
                x0 = i * 2
                eng.wait_ge(s["xe_act"], i + 1)
                eng.wait_ge(s["xe_dve"], i + 1)
                eng.wait_ge(loaded[0][0], i * 16 + 16)
                project(0, 0).then_inc(s["gate_done"], 1)
                eng.wait_ge(s["y_copied"], x0 + 1)
                scatter()
                eng.wait_ge(s["gw_ready"], i + 1)
                for n, w in enumerate((gwa, gwb)):
                    for t in range(2):
                        last = eng.transpose(bank[2][:, (2 * n + t) * P:(2 * n + t + 1) * P],
                                             w[:, t, :, :].rearrange("p e c -> p (e c)"), self.con("ident"))
                last.then_inc(s["gwt_turned"], 1)
                project(1, 0).then_inc(s["up_done"], 1)
                eng.wait_ge(s["silu_done"], x0 + 1)
                eng.wait_ge(loaded[1][0], i * 16 + 16)
                project(0, 1).then_inc(s["gate_done"], 1)
                eng.wait_ge(s["hid_ready"], x0 + 1)
                turn_hidden()
                project(1, 1).then_inc(s["up_done"], 1)
                eng.wait_ge(s["gwt_copied"], i + 1)
                eng.wait_ge(s["hidt_copied"], x0 + 1)
                eng.wait_ge(loaded[0][1], i * 16 + 16)
                down(0)
                eng.wait_ge(s["hid_ready"], x0 + 2)
                gather(i + 2)
                turn_hidden()
                eng.wait_ge(s["y_copied"], x0 + 2)
                eng.wait_ge(s["hidt_copied"], x0 + 2)
                eng.wait_ge(loaded[1][1], i * 16 + 16)
                down(1)
            eng.wait_ge(s["y_copied"], EXPERTS + 1)
            scatter()
            for b in range(4, 8):
                eng.matmul(bank[b][:, :], v["zero"][:, 0:P], v["zero"], start=False, stop=True,
                           skip_group_check=True)
        if who == "act":
            def copy_xe(n):
                eng.wait_ge(s["gathered"], n)
                eng.copy(v["xe"][:, 0:512], bank[0][:, :]).then_inc(s["xe_act"], 1)
            copy_xe(1)
            with eng.Fori(0, EXPERTS // 2) as i:
                for e in range(2):
                    eng.wait_ge(s["gate_done"], i * 2 + e + 1)
                    if e == 1:
                        eng.wait_ge(s["hid_ready"], i * 2 + 1)
                    eng.activation(v["sg"], bank[0][:, 0:256], ACT.Silu).then_inc(s["silu_done"], 1)
                copy_xe(i + 2)
        if who == "dve":
            def copy_xe(n):
                eng.wait_ge(s["gathered"], n)
                eng.tensor_copy(v["xe"][:, 512:1024], bank[1][:, :]).then_inc(s["xe_dve"], 1)

            def hidden(x):
                eng.wait_ge(s["silu_done"], x + 1)
                eng.wait_ge(s["up_done"], x + 1)
                eng.tensor_tensor(v["hid"], v["sg"], bank[1][:, 0:256], ALU.mult).then_inc(s["hid_ready"], 1)

            def copy_hidden(x):
                eng.wait_ge(s["hid_turned"], x + 1)
                eng.tensor_copy(v["hidt"], bank[3][:, 0:256]).then_inc(s["hidt_copied"], 1)

            def copy_rows(x, a, b):
                eng.wait_ge(s["down_done"], x + 1)
                eng.tensor_copy(v["ya"][a, :], bank[2][a, :])
                eng.tensor_copy(v["yb"][b, :], bank[2][b, :]).then_inc(s["y_copied"], 1)
            one_hots(0)
            copy_xe(1)
            with eng.Fori(0, EXPERTS // 2) as i:
                x0 = i * 2
                for t in range(2):
                    last = eng.tensor_tensor(gwa[:, t, :, :], gm[:, t, :, :],
                                             C[:, t, bass.ds(i * 2, 2)].unsqueeze(2)
                                             .to_broadcast([P, 2, SLOTS]), ALU.mult)
                last.then_inc(link, 1)
                eng.wait_ge(link, i + 1)
                eng.tensor_copy(gwb[:, :, 0, :], gwa[:, :, 1, :])
                eng.tensor_copy(gwb[:, :, 1, :], gwa[:, :, 0, :]).then_inc(s["gw_ready"], 1)
                one_hots(i + 1)
                eng.wait_ge(s["gwt_turned"], i + 1)
                eng.tensor_copy(v["gwt"], bank[2][:, :]).then_inc(s["gwt_copied"], 1)
                hidden(x0)
                copy_hidden(x0)
                hidden(x0 + 1)
                copy_rows(x0, lo, hi)
                copy_xe(i + 2)
                copy_hidden(x0 + 1)
                copy_rows(x0 + 1, hi, lo)
        self.phase_end(eng, who)
        if who == "dve":
            for t in range(2):
                for h in range(2):
                    eng.tensor_copy(v["acc"][:, t * D + h * 512:t * D + h * 512 + 512], bank[4 + 2 * t + h][:, :])
        self.phase_end(eng, who)
        self.flag_phase = 3 * self.phases[who]
        n = eng.value_load(self.overflow[0:1, 0:1])
        with eng.If(n != 0):
            self.late(who, eng)
        self.phase_end(eng, who)

    def late(self, who, eng):
        names = ("up_done", "silu_done", "hid_done", "down_done", "acc_used")
        up_done, silu_done, hid_done, down_done, acc_used = [self.sem("late_" + x) for x in names]
        loaded = self.sem("late_loaded")
        v = self.moe_views()
        bank = self.bank
        slot = self.expert_slots()[0]
        if who == "sp":
            with eng.Fori(0, EXPERTS) as e:
                eng.wait_ge(self.sem("late_free"), e + 1)
                eng.dma_start(slot, self.W["moe"][e]).then_inc(loaded, 16)
            return
        acc = v["acc"].rearrange("p (t h d) -> p t h d", t=2, h=2)
        sg = v["late_sg"].rearrange("p (f t) -> p f t", f=FET)
        hid = v["late_hid"].rearrange("p (f t) -> p f t", f=FET)
        C = self.late_weights().rearrange("p (t c) -> p t c", t=2)
        if who == "dve":
            eng.nop().then_inc(acc_used, 4)
        if who == "pe":
            eng.nop().then_inc(self.sem("late_free"), 1)
        with eng.Fori(0, EXPERTS) as e:
            if who == "pe":
                eng.wait_ge(loaded, e * 16 + 16)

                def up(x, f, k, w):
                    return eng.matmul(bank[f][:, x * LAT:(x + 1) * LAT], w[:, f * P:(f + 1) * P],
                                      self.A[:, k, CTX:T], start=(k == 0), stop=(k == KT - 1))
                for x in range(2):
                    for f in range(FET):
                        for k in range(KT):
                            c = x * KT + k
                            w = slot[:, c * FE:(c + 1) * FE]
                            last = up(x, f, k, w)
                        if x:
                            last.then_inc(up_done, 1)
                eng.wait_ge(acc_used, e * 4 + 4)
                for f in range(FET):
                    eng.wait_ge(hid_done, e * 4 + f + 1)
                for t in range(2):
                    for h in range(2):
                        for f in range(FET):
                            o = UPS + f * D + h * 512
                            last = eng.matmul(bank[4 + 2 * t + h][:, :], hid[:, f, t * P:(t + 1) * P],
                                              slot[:, o:o + 512], start=(f == 0), stop=(f == FET - 1))
                        last.then_inc(down_done, 1)
                eng.drain().then_inc(self.sem("late_free"), 1)
            if who == "act":
                for f in range(FET):
                    eng.wait_ge(up_done, e * 4 + f + 1)
                    eng.activation(sg[:, f, :], bank[f][:, 0:LAT], ACT.Silu).then_inc(silu_done, 1)
            if who == "dve":
                for f in range(FET):
                    eng.wait_ge(silu_done, e * 4 + f + 1)
                    eng.tensor_tensor(hid[:, f, :], sg[:, f, :], bank[f][:, LAT:2 * LAT], ALU.mult)\
                        .then_inc(hid_done, 1)
                for t in range(2):
                    c = C[:, t, bass.ds(e, 1)]
                    for h in range(2):
                        eng.wait_ge(down_done, e * 4 + 2 * t + h + 1)
                        eng.scalar_tensor_tensor(out=acc[:, t, h, :], in0=bank[4 + 2 * t + h][:, :], scalar=c,
                                                 in1=acc[:, t, h, :], op0=ALU.mult, op1=ALU.add)\
                            .then_inc(acc_used, 1)
        if who == "dve":
            eng.wait_ge(acc_used, 4 * EXPERTS + 4)

    def result(self):
        return self.moe_views()["acc"].rearrange("p (t d) -> p t d", t=2)

    def final(self, who, eng):
        acc = self.result()
        bank = self.bank
        if who == "pe":
            for t in range(2):
                for k in range(KT):
                    eng.transpose(bank[t * 2 + k // 4][:, (k % 4) * P:(k % 4 + 1) * P],
                                  self.H[:, k, CTX + t * P:CTX + (t + 1) * P], self.con("ident"))
        self.phase_end(eng, who)
        ss = self.S[:, 128:130]
        if who == "dve":
            for t in range(2):
                for h in range(2):
                    c = acc[:, t, 512 * h:512 * h + 512]
                    eng.tensor_tensor(c, c, bank[t * 2 + h][:, :], ALU.add)
        self.phase_end(eng, who)
        if who == "act":
            for t in range(2):
                eng.activation(self.X[:, t * D:(t + 1) * D], acc[:, t, :], ACT.Square,
                               accum_out=ss[:, t:t + 1])
        self.phase_end(eng, who)
        if who == "dve":
            eng.tensor_scalar(ss, ss, 1.0 / D, RMS_EPS, ALU.mult, ALU.add)
        self.phase_end(eng, who)
        if who == "act":
            eng.activation(ss, ss, ACT.Sqrt)
        self.phase_end(eng, who)
        if who == "dve":
            self.link(eng, who, eng.reciprocal(ss, ss))
            for t in range(2):
                last = eng.scalar_tensor_tensor(out=acc[:, t, :], in0=acc[:, t, :], scalar=ss[:, t:t + 1],
                                                in1=self.vec("final_norm"), op0=ALU.mult, op1=ALU.mult)
                self.link(eng, who, last)
            eng.nop().then_inc(self.sem("result_ready"), 1)


def constants():
    c = {}
    i = np.arange(P)
    c["ident"] = np.eye(P)
    c["ones"] = np.ones((P, P))
    c["mean"] = np.full((P, P), 1.0 / D)

    def rotation(base, half, n):
        r = np.zeros((P, n))
        for j in range(half):
            for at in base:
                r[at + half + j, at + j] = -1.0
                r[at + j, at + half + j] = 1.0
        return r
    tok = np.arange(LAT)
    nf = DR // 4
    inv = (10000.0 ** (-np.arange(nf, dtype=np.float32) / np.float32(nf))).astype(np.float32)
    row, col = (tok // GRID_W).astype(np.float32), (tok % GRID_W).astype(np.float32)
    ang = np.concatenate([row[:, None] * inv, col[:, None] * inv], -1).T.astype(np.float32)
    cos, sin = np.ones((P, LAT)), np.zeros((P, LAT))
    for h in range(2):
        cos[DN + 16 * h:DN + 16 * h + 16] = np.cos(ang)
        sin[DN + 16 * h:DN + 16 * h + 16] = np.sin(ang)
    c["rot_mla"], c["cos_mla"], c["sin_mla"] = rotation([DN], DR // 2, QK), cos, sin
    inv = (500000.0 ** (-np.arange(8, dtype=np.float32) / np.float32(8))).astype(np.float32)
    ang = (tok.astype(np.float32)[:, None] * inv).T.astype(np.float32)
    cos, sin = np.ones((P, LAT)), np.zeros((P, LAT))
    for at in (0, 8, 64, 72):
        cos[at:at + 8], sin[at:at + 8] = np.cos(ang), np.sin(ang)
    c["rot_nsa"], c["cos_nsa"], c["sin_nsa"] = rotation([0, 64], 8, P), cos, sin
    qc, kc = i % GRID_W, np.arange(LAT) % GRID_W
    start = np.clip(qc - 8, 0, GRID_W - 16)
    ok = (kc[None, :] >= start[:, None]) & (kc[None, :] < start[:, None] + 16)
    c["na_mask"] = np.where(ok, 0.0, NEG)
    m = np.full((P, 416), NEG)
    tri = np.where(i[None, :] <= i[:, None], 0.0, NEG)
    m[:, 0:128] = tri
    m[:, 128:256] = 0.0
    m[:, 256:384] = tri
    keep = np.zeros((P, 32))
    for t in range(2):
        n = np.arange(16)
        ok = (16 * n + 31)[None, :] <= (i + P * t)[:, None]
        ok &= (n < NCMP)[None, :]
        m[:, 384 + 16 * t:400 + 16 * t] = np.where(ok, 0.0, NEG)
        keep[:, 16 * t:16 * t + 16] = ok
    c["nsa_mask"], c["cmp_keep"] = m, keep
    s, t = i[:, None], i[None, :]
    masks = [(s // (2 * v) == t // (2 * v)) & (s // v % 2 == 0) & (t // v % 2 == 1) for v in LEVELS]
    c["level_mask"] = np.concatenate(masks + [s == t], 1)
    c["scan_keep"] = np.broadcast_to((tok % 64 != 0), (P, LAT))
    c["fold"] = i[:, None] % 32 == np.arange(2)
    c["before"] = i[:, None] < i[None, :]
    c["slot"] = np.broadcast_to(np.arange(SLOTS), (P, SLOTS))
    c["first4"] = np.broadcast_to(4.0 - np.arange(4), (P, 4))
    c["first8"] = np.broadcast_to(8.0 - np.arange(8), (P, 8))
    out = np.zeros((P, NCONST), np.float32)
    for n, w in CONSTS:
        out[:, COFF[n][0]:COFF[n][0] + w] = c[n]
    return out


def tiled(w, tiles_per_chunk):
    k, n = w.shape
    w = w.reshape(k // P, P, n // P // tiles_per_chunk, tiles_per_chunk, P)
    return np.ascontiguousarray(w.transpose(2, 1, 3, 0, 4)).reshape(w.shape[2], P, -1)


def columns(v):
    return np.asarray(v).reshape(-1, P).T


def lay_out(a):
    W = {}
    w = np.concatenate([a["ada_w"][i] for i in range(DEPTH)], 1).reshape(KT, P, -1)
    n = ADA_FIRST * P
    W["ada"] = w[:, :, :n].reshape(KT, P, 4, 512).transpose(2, 1, 0, 3).reshape(4, P, -1)
    ada = w[:, :, n:].reshape(KT, P, MLA_H, ADA_TILES * P).transpose(2, 1, 0, 3).reshape(MLA_H, P, -1)
    w = a["mla_w_in"][0]
    pe = np.zeros((D, QK), np.float32)
    pe[:, DN:] = w[:, QL + KVL:]
    W["mla_in"] = np.concatenate(
        [tiled(w[:, :QL + KVL], 5)[0], pe.reshape(KT, P, QK).transpose(1, 0, 2).reshape(P, -1)], 1)[None]
    q = a["mla_w_qb"][0].reshape(QLT, P, MLA_H, QK).transpose(2, 1, 0, 3).reshape(MLA_H, P, -1)
    kv = a["mla_w_kvb"][0].reshape(KVT, P, MLA_H, 2, DN).transpose(2, 1, 3, 0, 4).reshape(MLA_H, P, -1)
    W["mla_head"] = np.concatenate([q, kv, ada], 2)
    W["mla_o"] = tiled(a["mla_w_o"][0], 4)
    for i in range(DEPTH):
        u = a["ffn_w_in"][i].reshape(KT, P, 2, FT // 2, 2, P)
        W[f"ffn_in{i}"] = u.transpose(3, 1, 2, 4, 0, 5).reshape(FT // 2, P, -1)
        W[f"ffn_out{i}"] = tiled(a["ffn_w_out"][i], 2)
    W["na_pair"] = a["na_w_qkv"][0].reshape(KT, P, 3, NA_PAIRS, P).transpose(3, 1, 2, 0, 4)\
        .reshape(NA_PAIRS, P, -1)
    W["na_o"] = tiled(a["na_w_o"][0], 4)
    w = a["w_in_2"][0]
    q = w[:, :512].reshape(D, 2, 4, 64).transpose(0, 2, 1, 3).reshape(D, 512)
    W["proj"] = tiled(np.concatenate([q, w[:, 512:1280], w[:, 1304:]], 1), 6)
    cmp = np.zeros((2, P, 32, P), np.float32)
    for x, n in enumerate(("w_cmp_k_2", "w_cmp_v_2")):
        c = a[n][0].reshape(32, 64, 64).transpose(1, 0, 2)
        cmp[x, 0:64, :, 0:64] = c
        cmp[x, 64:128, :, 64:128] = c
    W["cmp"] = cmp.reshape(2, P, -1)
    W["branch"] = np.concatenate([tiled(a["w_br_nsa_2"][0], 8), tiled(a["w_br_hg_2"][0], 8)])
    W["w_out"] = tiled(a["w_out_2"][0], 4)
    g, u = [a[n][0].reshape(EXPERTS, KT, P, FE).transpose(0, 2, 1, 3).reshape(EXPERTS, P, -1)
            for n in ("w_gate_2", "w_up_2")]
    dn = a["w_down_2"][0].reshape(EXPERTS, FET, P, D).transpose(0, 2, 1, 3).reshape(EXPERTS, P, -1)
    W["moe"] = np.concatenate([g, u, dn], 2)

    v = {}
    v["cvec"] = np.stack([columns(a["c_ctx"]), columns(a["c"][0])], 2).reshape(P, -1)
    for n in ("ada_b", "ln1_g", "ln1_b", "ln2_g", "ln2_b"):
        v[n] = columns(a[n])
    v["conv_w"], v["conv_b"] = columns(a["ffn_conv_w"]), columns(a["ffn_conv_b"])
    v["q_norm"], v["kv_norm"] = columns(a["mla_q_norm"]), columns(a["mla_kv_norm"])
    v["attn_norm"], v["ffn_norm"] = columns(a["attn_norm_2"]), columns(a["ffn_norm_2"])
    v["hg_lb"], v["hg_norm"] = columns(a["hg_lb_logits_2"]), columns(a["hg_norm_2"])
    v["cmp_pos"] = np.concatenate([a["cmp_pos_2"][0].T] * 2)
    w = a["w_in_2"][0][:, 1280:1304].reshape(KT, P, 2, 4, 3)[..., [1, 0, 2]]
    v["w_gate24"] = w.transpose(1, 0, 3, 2, 4).reshape(P, -1)
    w = np.concatenate([a["w_grp_2"][0], a["w_rtr_2"][0]], 1)
    v["w_route"] = w.reshape(KT, P, 36).transpose(1, 0, 2).reshape(P, -1)
    v["b_route"] = np.broadcast_to(np.concatenate([a["b_grp_2"][0], a["b_rtr_2"][0]]), (P, 36))
    v["final_norm"] = np.broadcast_to(a["final_norm_2"], (P, D))
    vec = np.zeros((P, NVEC), np.float32)
    for n, wd in VECS:
        vec[:, VOFF[n][0]:VOFF[n][0] + wd] = v[n]

    xT = np.concatenate([a["ctx"][0], a["x"][0]]).T.reshape(KT, P, T).transpose(1, 0, 2)
    r = a["na_rpb"][0]
    wide = np.zeros((16, 7, 2 * GRID_W - 1), np.float32)
    wide[:, :, 48:79] = r[:, 4:11, :]
    nab = np.empty((4, GRID_W, 16, 4, GRID_W), np.float32)
    for qr in range(4):
        for qc in range(GRID_W):
            nab[qr, qc] = wide[:, 3 - qr:7 - qr, 63 - qc:127 - qc]
    return W, vec, np.ascontiguousarray(xT), nab.reshape(4, GRID_W, 16, LAT)


def kernel(**inputs):
    import concourse.bacc as _bacc
    from concourse.bass_utils import run_bass_kernel_spmd as _run

    weights, vectors, x_t, na_bias = lay_out({k: np.asarray(v) for k, v in inputs.items()})
    nc = _bacc.Bacc("TRN2", target_bir_lowering=False, num_devices=1)
    arrays = {"in_vectors": vectors, "in_constants": constants(), "in_x_t": x_t, "in_na_bias": na_bias}
    arrays |= {"w_" + n: weights[n] for n, _, _ in STREAM}
    arrays = {n: np.ascontiguousarray(v) for n, v in arrays.items()}
    d = {n: nc.dram_tensor(n, v.shape, F32, kind="ExternalInput").ap() for n, v in arrays.items()}
    out = nc.dram_tensor("out", (1, LAT, D), F32, kind="ExternalOutput").ap()
    program = Kernel(nc, {n: d["w_" + n] for n, _, _ in STREAM}, d["in_vectors"], d["in_constants"],
                     d["in_x_t"], d["in_na_bias"], out)
    program.build()
    r = _run(nc, [arrays], core_ids=[0])
    return r.results[0]["out"]
```

```python
import math
from contextlib import ExitStack

import numpy as np
import concourse.bass as bass
from concourse import mybir

F32 = mybir.dt.float32
ACT = mybir.ActivationFunctionType
ALU = mybir.AluOpType
AX = mybir.AxisListType

P = 128
D = 1024
KT = D // P
CTX = 256
LAT = 256
T = CTX + LAT
DEPTH = 2
ALPHA = (2.0 * DEPTH) ** 0.25
LN_EPS, RMS_EPS = 1e-5, 1e-6
NEG = -1e30
HUGE = 3.0e38
GRID_W = 64

MLA_H, DN, DR, DV = 16, 64, 32, 64
QK = DN + DR
QL, KVL = 384, 256
QLT, KVT = QL // P, KVL // P
NA_PAIRS = 8
FFN = 2816
FT = FFN // P
NSA_PAIRS = 4
NCMP = 15
HG = 4
EXPERTS, GROUPS, PER_GROUP = 32, 4, 8
FE = 512
SLOTS = 64
FET = FE // P

SLOT = 6144
RING = 2

VECS = [("cvec", KT * 2), ("ada_b", DEPTH * 48),
        ("ln1_g", DEPTH * KT), ("ln1_b", DEPTH * KT), ("ln2_g", DEPTH * KT), ("ln2_b", DEPTH * KT),
        ("conv_w", DEPTH * 3 * 2 * FT), ("conv_b", DEPTH * 2 * FT),
        ("q_norm", QLT), ("kv_norm", KVT), ("attn_norm", KT), ("ffn_norm", KT),
        ("hg_lb", 2 * HG), ("hg_norm", 1), ("cmp_pos", 32),
        ("w_gate24", KT * 24), ("w_route", KT * 36), ("b_route", 36), ("final_norm", D)]
VOFF, _at = {}, 0
for _n, _w in VECS:
    VOFF[_n] = (_at, _w)
    _at += _w
NVEC = _at

LEVELS = [64, 32, 16, 8, 4, 2, 1]
CONSTS = [("ident", P), ("fold", 2), ("ones", P), ("mean", P), ("rot_mla", QK), ("cos_mla", LAT), ("sin_mla", LAT),
          ("rot_nsa", P), ("cos_nsa", LAT), ("sin_nsa", LAT), ("na_mask", LAT),
          ("nsa_mask", 416), ("cmp_keep", 32), ("level_mask", (len(LEVELS) + 1) * P), ("scan_keep", LAT),
          ("cmp_fold", 16), ("spread", 4 * P), ("first4", GROUPS), ("first8", PER_GROUP), ("before", P), ("slot", SLOTS)]
COFF, _at = {}, 0
for _n, _w in CONSTS:
    COFF[_n] = (_at, _w)
    _at += _w
NCONST = _at
EARLY_V, EARLY_C = VOFF["ln1_g"][0], COFF["ones"][0]

T_Q, T_CK, T_CV, T_SK, T_SV, T_WK, T_WV, T_HQ, T_HF, T_HI, T_HGATE, T_MN, T_MH = \
    0, 4, 5, 6, 7, 8, 9, 10, 14, 18, 22, 26, 34
NPROJ = 42

HEAD_W = QLT * QK + KVT * DN
ADA_FIRST, ADA_TILES = 4 * 4, 5
STREAM = [("ada", 4, KT * 512), ("mla_in", 1, 5 * D + 8 * QK), ("mla_v", 1, KVT * D),
          ("mla_head", 16, HEAD_W + KT * ADA_TILES * P), ("mla_o", 2, 4096),
          ("ffn_in0", 11, 4096), ("ffn_out0", 4, 5632),
          ("na_pair", NA_PAIRS, 3072), ("na_o", 2, 4096),
          ("ffn_in1", 11, 4096), ("ffn_out1", 4, 5632),
          ("proj", 7, 6144), ("cmp", 2, 4096), ("branch", 2, 4096), ("w_out", 2, 4096),
          ("moe", EXPERTS, (2 * KT + 2 * FET) * FE)]
UPS = 2 * KT * FE
FIRST, _at = {}, 0
for _n, _c, _w in STREAM:
    FIRST[_n] = _at
    _at += _c
CHUNKS = {n: c for n, c, _ in STREAM}


def each(k):
    return lambda c: c * k + k


CHUNK_USED = {
    "ada": ("ada_used", each(1)), "mla_in": ("mla_in_used", each(1)),
    "mla_v": ("mla_v_done", each(8)), "mla_head": ("ada_rows", each(1)), "mla_o": ("mla_o_y_ready", each(4)),
    "ffn_in0": ("ffn0_up_done", each(2)), "ffn_out0": ("ffn_out0_y_ready", each(2)),
    "na_pair": ("na_proj_done", each(1)), "na_o": ("na_o_y_ready", each(4)),
    "ffn_in1": ("ffn1_up_done", each(2)), "ffn_out1": ("ffn_out1_y_ready", each(2)),
    "proj": ("proj_tile_done", each(6)), "cmp": ("cmp_used", each(1)),
    "branch": ("branch_done", lambda c: KT), "w_out": ("w_out_y_ready", each(4)),
}


class Kernel:

    def __init__(self, nc, W, vec, const, xT, na_bias, out):
        self.nc, self.W, self.vec_d, self.const_d, self.xT, self.nab_d, self.out = \
            nc, W, vec, const, xT, na_bias, out
        self.phases = {"pe": 0, "act": 0, "dve": 0}
        self.links = {"act": 0, "dve": 0}
        self.norms = {"pe": 0, "act": 0, "dve": 0}
        self.normed = {"pe": 0, "act": 0, "dve": 0}
        self.norm_counts = {w: (0, 0, 0) for w in self.norms}
        self.flips = {"pe": 0, "dve": 0}
        self.outs = {"pe": 0, "dve": 0}

    def sem(self, name):
        if name not in self.sems:
            self.sems[name] = self.ctx.enter_context(self.nc.semaphore(name))
        return self.sems[name]

    def vec(self, name, i=0, n=None):
        off, w = VOFF[name]
        return self.V[:, off + i:off + (w if n is None else i + n)]

    def con(self, name, i=0, n=None):
        off, w = COFF[name]
        return self.C[:, off + i:off + (w if n is None else i + n)]

    def phase_end(self, eng, who):
        self.phases[who] += 1
        eng.drain().then_inc(self.phase_done, 1)
        eng.wait_ge(self.phase_done, 3 * self.phases[who])

    def link(self, eng, who, ins):
        self.links[who] += 1
        s = self.chain[who]
        ins.then_inc(s, 1)
        eng.wait_ge(s, self.links[who])

    def chunks(self, pe, name, body, count=None, start=0):
        g0 = FIRST[name] + start
        n = (CHUNKS[name] if count is None else count)
        turns = n // 2
        if turns >= 2:
            with pe.Fori(0, turns) as it:
                for s in range(2):
                    g = g0 + s
                    pe.wait_ge(self.w_loaded[g % 2], it * 16 + 16 * (g // 2 + 1))
                    body(it * 2 + s + start, self.ring[g % 2])
            done = 2 * turns
        else:
            done = 0
        for j in range(done, n):
            g = g0 + j
            pe.wait_ge(self.w_loaded[g % 2], 16 * (g // 2 + 1))
            body(j + start, self.ring[g % 2])

    def counted(self, eng, n, body):
        with eng.Fori(0, n // 2) as it:
            for s in range(2):
                body(it * 2 + s)
        if n % 2:
            body(n - 1)

    def build(self):
        nc = self.nc
        with ExitStack() as ctx:
            self.ctx, self.sems = ctx, {}

            def sb(name, shape):
                return ctx.enter_context(nc.sbuf_tensor(name, shape, F32))
            self.whole_ring = sb("ring", [P, RING * SLOT])
            self.ring = [self.whole_ring[:, i * SLOT:(i + 1) * SLOT] for i in range(RING)]
            self.H = sb("residual", [P, KT, T])
            self.A = sb("layer_input", [P, KT, T])
            arena = sb("arena", [P, FT * T + 32 * LAT + KT * T])
            self.arena = arena[:, :]
            self.B = arena[:, 0:FT * T]
            self.N = arena[:, FT * T:FT * T + 32 * LAT]
            self.X = arena[:, FT * T + 32 * LAT:]
            self.overflow = ctx.enter_context(nc.sbuf_tensor("overflow", [1, 1], mybir.dt.int32))
            self.V = sb("vectors", [P, NVEC])
            self.C = sb("constants", [P, NCONST])
            self.ADA = sb("ada", [P, DEPTH, 48, 2])
            self.S = sb("stats", [P, 256])
            self.R = sb("rstd", [P, T // 4])
            self.bank = [ctx.enter_context(nc.psum_tensor(f"bank{i}", [P, 512], F32)) for i in range(8)]
            self.w_loaded = [self.sem(f"w_loaded{i}") for i in range(RING)]
            self.phase_done = self.sem("phase_done")
            self.chain = {"dve": self.sem("dve_link"), "act": self.sem("act_link")}
            self.cvec_in, self.const_in, self.rest_in, self.bias_in = \
                [self.sem(x) for x in ("cvec_in", "const_in", "rest_in", "bias_in")]
            block = ctx.enter_context(nc.Block())

            @block.tensor
            def _(pe):
                self.run("pe", pe)

            @block.scalar
            def _(act):
                act.dma_start(self.V[:, 0:2 * KT], self.vec_d[:, 0:2 * KT]).then_inc(self.cvec_in, 16)
                act.dma_start(self.V[:, 2 * KT:EARLY_V], self.vec_d[:, 2 * KT:EARLY_V])\
                    .then_inc(self.const_in, 16)
                act.dma_start(self.C[:, 0:EARLY_C], self.const_d[:, 0:EARLY_C]).then_inc(self.const_in, 16)
                act.dma_start(self.H[:, :, :], self.xT).then_inc(self.const_in, 16)
                self.run("act", act)

            @block.vector
            def _(dve):
                self.run("dve", dve)

            @block.sync
            def _(sp):
                self.sync_program(sp)

    def stages(self):
        return [self.ada, self.modulate_first, self.mla_in, self.mla_heads, self.mla_out,
                lambda w, e: self.ffn(w, e, 0), self.na_heads, self.na_out,
                lambda w, e: self.ffn(w, e, 1),
                self.proj, self.compress, self.nsa_heads, self.hgrn, self.branches,
                self.router, self.moe, self.final]

    def run(self, who, eng):
        st = self.stages()
        for stage in st:
            stage(who, eng)

    def sync_program(self, sp):
        for name, n, width in STREAM:
            w, g0 = self.W[name], FIRST[name]

            if name == "moe":
                self.load_experts(sp)
                break

            def load(j, s, g):
                sp.dma_start(self.ring[s][:, 0:width], w[j]).then_inc(self.w_loaded[s], 16)
            first = 0
            if g0 == 0:
                for j in range(RING):
                    load(j, j, j)
                first = RING
            while first < min(n, RING):
                g = g0 + first - RING
                before = max((m for m in FIRST if FIRST[m] <= g), key=FIRST.get)
                sem, upto = CHUNK_USED[before]
                sp.wait_ge(self.sem(sem), upto(g - FIRST[before]))
                load(first, (g0 + first) % 2, g0 + first)
                first += 1
            sem, upto = CHUNK_USED[name]
            turns = (n - first) // 2
            if turns >= 2:
                with sp.Fori(0, turns) as it:
                    for s in range(2):
                        g = g0 + first + s
                        sp.wait_ge(self.sem(sem), upto(it * 2 + (first + s - RING)))
                        load(it * 2 + first + s, g % 2, g)
                first += 2 * turns
            for j in range(first, n):
                sp.wait_ge(self.sem(sem), upto(j - RING))
                load(j, (g0 + j) % 2, g0 + j)
        sp.wait_ge(self.phase_done, self.flag_phase)
        n = sp.value_load(self.overflow[0:1, 0:1])
        with sp.If(n != 0):
            self.late("sp", sp)
        sp.wait_ge(self.sem("result_ready"), 1)
        sp.dma_start(self.out.rearrange("a (t p) d -> p (a t) d", p=P),
                     self.result()).then_inc(self.sem("result_out"), 16)
        sp.wait_ge(self.sem("result_out"), 16)

    def expert_slots(self):
        return self.whole_ring[:, :], self.arena[:, FT * T:FT * T + RING * SLOT]

    def load_experts(self, sp):
        loaded = self.expert_loaded()
        slots = self.expert_slots()
        parts = slice(0, UPS // 2), slice(UPS // 2, UPS), slice(UPS, 2 * SLOT)

        def load(x, e, part):
            sp.dma_start(slots[e][:, parts[part]], self.W["moe"][x][:, parts[part]])\
                .then_inc(loaded[e][part], 16)
        sp.wait_ge(self.sem("w_out_y_ready"), KT)
        for e in range(2):
            for part in range(3):
                load(e, e, part)
        with sp.Fori(0, EXPERTS // 2 - 1) as it:
            for e in range(2):
                for part, used in enumerate(("moe_gate_done", "moe_up_done", "moe_down_done")):
                    sp.wait_ge(self.sem(used), it * 2 + e + 1)
                    load(it * 2 + e + 2, e, part)

    def expert_loaded(self):
        return [[self.sem(f"expert{e}_{part}_loaded") for part in ("gate", "up", "down")] for e in range(2)]

    def mm(self, pe, out, lhs, rhs):
        for k, (a, b) in enumerate(zip(lhs, rhs)):
            last = pe.matmul(out, a, b, start=(k == 0), stop=(k == len(lhs) - 1))
        return last

    def norm(self, who, eng, c0, write, act_write=None, src=None, tiles=KT, centre=True, dim=D, eps=LN_EPS, sq=None):
        w = T - c0
        src = src or (lambda k: self.H[:, k, c0:T])
        xc = self.X[:, :].rearrange("p (k t) -> p k t", k=KT)
        sq = sq or (lambda k: self.A[:, k, c0:T])
        n = self.norms[who]
        self.norms[who] += 1
        mean_ready, centred, squared, var_ready, dev_ready, rstd_ready, spread = \
            [self.sem(x) for x in ("mean_ready", "centred", "squared", "var_ready", "dev_ready", "rstd_ready",
                                   "rstd_spread")]
        base, cbase, means = self.norm_counts[who]
        self.norm_counts[who] = (base + tiles, cbase + tiles * centre, means + centre)
        val = (lambda k: xc[:, k, 0:w]) if centre else src
        q = w // 4
        mu, var, small = self.bank[0][:, 0:w], self.bank[1][:, 0:q], self.R[:, 0:q]
        rstd = self.bank[0][:, 0:w]
        if who == "pe":
            if centre:
                eng.matmul(mu, self.con("mean"), self.tile_sum(w), start=True, stop=True)\
                    .then_inc(mean_ready, 1)
            for k in range(tiles):
                eng.wait_ge(squared, base + k + 1)
                for j in range(4):
                    last = eng.matmul(var[32 * j:32 * j + 32, :], self.con("mean" if dim == D else "ones", 0, 32),
                                      sq(k)[:, j * q:(j + 1) * q], start=(k == 0), stop=(k == tiles - 1),
                                      skip_group_check=True)
            last.then_inc(var_ready, 1)
            eng.wait_ge(rstd_ready, n + 1)
            for j in range(4):
                last = eng.matmul(rstd[:, j * q:(j + 1) * q], self.con("spread", j * P, P), small,
                                  start=True, stop=True)
            last.then_inc(spread, 1)
        if who == "act":
            for k in range(tiles):
                if centre:
                    eng.wait_ge(centred, cbase + k + 1)
                eng.activation(sq(k), val(k), ACT.Square).then_inc(squared, 1)
            eng.wait_ge(dev_ready, 2 * n + 1)
            eng.activation(small, small, ACT.Sqrt).then_inc(dev_ready, 1)
            if act_write:
                act_write(val)
        if who == "dve":
            if centre:
                eng.wait_ge(mean_ready, means + 1)
                for k in range(tiles):
                    eng.tensor_tensor(val(k), src(k), mu, ALU.subtract).then_inc(centred, 1)
            eng.wait_ge(var_ready, n + 1)
            eng.tensor_scalar(small, var, 1.0 if dim == D else 1.0 / dim, eps, ALU.mult, ALU.add)\
                .then_inc(dev_ready, 1)
            eng.wait_ge(dev_ready, 2 * n + 2)
            eng.reciprocal(small, small).then_inc(rstd_ready, 1)
            eng.wait_ge(spread, n + 1)
            write(val, rstd)
        self.phase_end(eng, who)

    def tile_sum(self, w):
        return self.X[:, w:2 * w]

    def layer_norm(self, who, eng, c0, gain, bias, layer, then=None):
        normed = self.sem("normed")
        base = self.normed[who]
        self.normed[who] += KT
        g, b = self.vec(gain, layer * KT, KT), self.vec(bias, layer * KT, KT)
        ga, ba = [self.S[:, 196 + 16 * i:212 + 16 * i].rearrange("p (k s) -> p k s", s=2) for i in range(2)]
        if who == "dve" and then:
            to, shift, scale, _ = then
            sh, sc = [self.ADA[:, to, m * KT:(m + 1) * KT, :] for m in (shift, scale)]
            eng.tensor_tensor(ga, g.unsqueeze(2).to_broadcast([P, KT, 2]), sc, ALU.mult)
            self.link(eng, who, eng.tensor_tensor(ba, b.unsqueeze(2).to_broadcast([P, KT, 2]), sc, ALU.mult))
            self.link(eng, who, eng.tensor_tensor(ba, ba, sh, ALU.add))

        def write(x, r):
            for k in range(KT + 1):
                if k < KT:
                    eng.tensor_tensor(x(k), x(k), r, ALU.mult).then_inc(normed, 1)
                if k:
                    eng.wait_ge(normed, base + k)
                    eng.tensor_scalar(self.H[:, k - 1, c0:T], x(k - 1), g[:, k - 1:k], b[:, k - 1:k],
                                      ALU.mult, ALU.add)

        def act_write(x):
            for k in range(KT):
                eng.wait_ge(normed, base + k + 1)
                for seg in then[3]:
                    c = slice(CTX * seg, CTX * seg + 256)
                    eng.activation(self.A[:, k, c], x(k)[:, CTX * seg - c0:CTX * seg - c0 + 256], ACT.Identity,
                                   bias=ba[:, k, seg:seg + 1], scale=ga[:, k, seg:seg + 1])
        self.norm(who, eng, c0, write, act_write if then else None)

    def modulate(self, who, eng, layer, shift, scale, segs):
        if who == "act":
            for k in range(KT):
                for seg in segs:
                    c = slice(CTX * seg, CTX * seg + 256)
                    eng.activation(self.A[:, k, c], self.H[:, k, c], ACT.Identity,
                                   bias=self.ADA[:, layer, shift * KT + k, seg:seg + 1],
                                   scale=self.ADA[:, layer, scale * KT + k, seg:seg + 1])
        self.phase_end(eng, who)

    def project_residual(self, who, eng, name, rhs, nk, per_chunk, gate, layer, segs):
        c0 = CTX * segs[0]
        w = T - c0
        y_ready, y_used = self.sem(name + "_y_ready"), self.sem(name + "_y_used")
        tiles = KT
        if who == "pe":
            def body(j, slot):
                for s in range(per_chunk):
                    oc = j * per_chunk + s
                    first_two = isinstance(oc, int) and oc < 2
                    if not first_two:
                        eng.wait_ge(y_used, oc - 1)
                    o = s % 2
                    m = self.mm(eng, self.bank[o][:, 0:w],
                                [slot[:, (s * nk + k) * P:(s * nk + k + 1) * P] for k in range(nk)],
                                [rhs(k) for k in range(nk)])
                    m.then_inc(y_ready, 1)
            for j in range(CHUNKS[name]):
                g = FIRST[name] + j
                eng.wait_ge(self.w_loaded[g % 2], 16 * (g // 2 + 1))
                body(j, self.ring[g % 2])
        if who == "dve":
            tmp = self.X[:, 0:w]
            for oc in range(tiles):
                eng.wait_ge(y_ready, oc + 1)
                y = self.bank[oc % 2][:, 0:w]
                if gate is None:
                    eng.tensor_tensor(self.H[:, oc, c0:T], self.H[:, oc, c0:T], y, ALU.add)\
                        .then_inc(y_used, 1)
                    continue
                for seg in segs:
                    part = slice(CTX * seg - c0, CTX * seg - c0 + 256)
                    last = eng.tensor_scalar(tmp[:, part], y[:, part],
                                             self.ADA[:, layer, gate * KT + oc, seg:seg + 1], None, ALU.mult)
                self.link(eng, who, last)
                last = eng.scalar_tensor_tensor(out=self.H[:, oc, c0:T], in0=self.H[:, oc, c0:T],
                                                scalar=ALPHA, in1=tmp, op0=ALU.mult, op1=ALU.add)
                last.then_inc(y_used, 1)
                eng.wait_ge(y_used, oc + 1)
                if oc == 1:
                    eng.tensor_tensor(self.tile_sum(w), self.H[:, 0, c0:T], self.H[:, 1, c0:T], ALU.add)
                if oc > 1:
                    eng.tensor_tensor(self.tile_sum(w), self.tile_sum(w), self.H[:, oc, c0:T], ALU.add)
        self.phase_end(eng, who)

    def flip(self, who, eng, src, dst, tiles, rows, name):
        n0 = self.flips.get(who, 0)
        self.flips[who] = n0 + tiles
        turned, copied = self.sem("turned"), self.sem("turned_copied")
        if who == "pe":
            for k in range(tiles):
                if n0 + k >= 2:
                    eng.wait_ge(copied, n0 + k - 1)
                for t in range(rows):
                    last = eng.transpose(self.bank[(n0 + k) % 2][:, t * P:(t + 1) * P], src(t, k),
                                         self.con("ident"))
                last.then_inc(turned, 1)
        if who == "dve":
            for k in range(tiles):
                eng.wait_ge(turned, n0 + k + 1)
                eng.tensor_copy(dst(k), self.bank[(n0 + k) % 2][:, 0:rows * P]).then_inc(copied, 1)
        self.phase_end(eng, who)

    def silu(self):
        return self.X[:, 3712:3712 + 32 * KT].rearrange("p (k c) -> p k c", k=KT)

    def ada_group_rows(self, pe, bank, weights, width):
        cs = self.silu()
        for r in range(2):
            for grp in range(4):
                k = 4 * r + grp
                last = pe.matmul(bank[32 * grp:32 * grp + 32, 0:width], cs[:, k, :], weights(k),
                                 start=(r == 0), stop=(r == 1), skip_group_check=True)
        return last

    def ada(self, who, eng):
        silu_ready, used, copied = [self.sem(x) for x in ("silu_ready", "ada_used", "ada_copied")]
        flat = self.ADA[:, :, :, :].rearrange("p l m s -> p (l m) s")
        n = ADA_FIRST
        if who == "dve":
            eng.memset(self.silu(), 0.0).then_inc(silu_ready, 1)
        if who == "act":
            eng.wait_ge(self.cvec_in, 16)
            eng.wait_ge(silu_ready, 1)
            eng.activation(self.silu()[:, :, 0:2], self.vec("cvec").rearrange("p (k s) -> p k s", s=2), ACT.Silu)\
                .then_inc(silu_ready, 1)
        if who == "pe":
            eng.wait_ge(silu_ready, 2)
            for j in range(CHUNKS["ada"]):
                g = FIRST["ada"] + j
                eng.wait_ge(self.w_loaded[g % 2], 16 * (g // 2 + 1))
                slot = self.ring[g % 2]
                self.ada_group_rows(eng, self.bank[j][:, :], lambda k: slot[:, k * 512:(k + 1) * 512], 512)\
                    .then_inc(used, 1)
            eng.wait_ge(self.const_in, 48)
            for j in range(CHUNKS["ada"]):
                eng.wait_ge(copied, j + 1)
                for t in range(4):
                    eng.matmul(self.bank[4][:, (4 * j + t) * 2:(4 * j + t) * 2 + 2],
                               self.X[:, j * 512 + t * P:j * 512 + (t + 1) * P], self.con("fold"),
                               start=True, stop=True)
        if who == "dve":
            for j in range(CHUNKS["ada"]):
                eng.wait_ge(used, j + 1)
                eng.tensor_copy(self.X[:, j * 512:(j + 1) * 512], self.bank[j][:, :]).then_inc(copied, 1)
        self.phase_end(eng, who)
        if who == "dve":
            eng.wait_ge(self.const_in, 48)
            b = self.vec("ada_b", 0, n).unsqueeze(2).to_broadcast([P, n, 2])
            self.link(eng, who, eng.tensor_tensor(
                flat[:, 0:n, :], self.bank[4][:, 0:2 * n].rearrange("p (m s) -> p m s", s=2), b, ALU.add))
            sc = flat[:, KT:2 * KT, :]
            self.link(eng, who, eng.tensor_scalar(sc, sc, 1.0, None, ALU.add))
        self.phase_end(eng, who)

    def ada_rest(self, who, eng):
        if who == "dve":
            n = DEPTH * 48 - ADA_FIRST
            flat = self.ADA[:, :, :, :].rearrange("p l m s -> p (l m) s")
            b = self.vec("ada_b", ADA_FIRST, n).unsqueeze(2).to_broadcast([P, n, 2])
            self.link(eng, who, eng.tensor_tensor(flat[:, ADA_FIRST:, :], flat[:, ADA_FIRST:, :], b, ALU.add))
            for layer, m in ((0, 4), (1, 1), (1, 4)):
                sc = self.ADA[:, layer, m * KT:(m + 1) * KT, :]
                self.link(eng, who, eng.tensor_scalar(sc, sc, 1.0, None, ALU.add))

    def modulate_first(self, who, eng):
        if who == "act":
            eng.wait_ge(self.const_in, 48)
            eng.dma_start(self.V[:, EARLY_V:], self.vec_d[:, EARLY_V:]).then_inc(self.rest_in, 16)
            eng.dma_start(self.C[:, EARLY_C:], self.const_d[:, EARLY_C:]).then_inc(self.rest_in, 16)
        self.modulate(who, eng, 0, 0, 1, (0, 1))

    def mla_views(self):
        b = self.B
        v = {}
        at = 0
        for name, n in (("cq", QLT * T), ("ckv", KVT * T), ("kpe", T), ("kpr", LAT),
                        ("q0", T), ("q1", T), ("qr0", LAT), ("qr1", LAT), ("qt0", LAT), ("qt1", LAT),
                        ("kt0", T), ("kt1", T), ("v0", 4 * DV), ("v1", 4 * DV), ("values", 4 * D)):
            v[name] = b[:, at:at + n]
            at += n
        assert at <= FT * T
        v["p"] = self.X[:, 0:1536]
        v["pt"] = self.X[:, 1536:3072]
        return v

    def mla_in(self, who, eng):
        v = self.mla_views()
        cq = v["cq"].rearrange("p (k t) -> p k t", k=QLT)
        ckv = v["ckv"].rearrange("p (k t) -> p k t", k=KVT)
        if who == "pe":
            g = FIRST["mla_in"]
            eng.wait_ge(self.w_loaded[g % 2], 16 * (g // 2 + 1))
            slot = self.ring[g % 2]
            for m in range(6):
                wd = P if m < 5 else QK
                last = self.mm(eng, self.bank[m][0:wd, :],
                               [slot[:, m * D + k * wd:m * D + (k + 1) * wd] for k in range(KT)],
                               [self.A[:, k, :] for k in range(KT)])
            last.then_inc(self.sem("mla_in_used"), 1)
        eng.wait_ge(self.rest_in, 32)
        self.phase_end(eng, who)
        if who == "dve":
            for m in range(3):
                eng.tensor_copy(cq[:, m, :], self.bank[m][:, :])
            for m in range(2):
                eng.tensor_copy(ckv[:, m, :], self.bank[3 + m][:, :])
        if who == "act":
            eng.copy(v["kpe"][0:QK, :], self.bank[5][0:QK, :])
        self.phase_end(eng, who)

        def scaled(dst, gain):
            def write(x, r):
                for k in range(dst.shape[1]):
                    eng.scalar_tensor_tensor(out=dst[:, k, :], in0=x(k), scalar=self.vec(gain, k, 1), in1=r,
                                             op0=ALU.mult, op1=ALU.mult)
            return write
        sq = lambda k: self.A[:, k, :]
        self.norm(who, eng, 0, scaled(cq, "q_norm"), src=lambda k: cq[:, k, :], tiles=QLT, centre=False,
                  dim=QL, eps=RMS_EPS, sq=sq)
        self.norm(who, eng, 0, scaled(ckv, "kv_norm"), src=lambda k: ckv[:, k, :], tiles=KVT, centre=False,
                  dim=KVL, eps=RMS_EPS, sq=sq)
        if who == "pe":
            eng.matmul(self.bank[2][0:QK, 0:LAT], self.con("rot_mla")[0:QK, :], v["kpe"][0:QK, CTX:T],
                       start=True, stop=True)
        self.phase_end(eng, who)
        if who == "dve":
            r = slice(DN, QK)
            self.link(eng, who, eng.tensor_tensor(v["kpr"][r, :], self.bank[2][r, 0:LAT],
                                                  self.con("sin_mla")[r, :], ALU.mult))
            self.link(eng, who, eng.tensor_tensor(v["kt0"][r, CTX:T], v["kpe"][r, CTX:T],
                                                  self.con("cos_mla")[r, :], ALU.mult))
            self.link(eng, who, eng.tensor_tensor(v["kt0"][r, CTX:T], v["kt0"][r, CTX:T],
                                                  v["kpr"][r, :], ALU.add))
            eng.tensor_copy(v["kt1"][r, CTX:T], v["kt0"][r, CTX:T])
            eng.tensor_copy(v["kt0"][r, 0:CTX], v["kpe"][r, 0:CTX])
            eng.tensor_copy(v["kt1"][r, 0:CTX], v["kpe"][r, 0:CTX])
        self.phase_end(eng, who)
        v_done = self.sem("mla_v_done")
        if who == "pe":
            g = FIRST["mla_v"]
            eng.wait_ge(self.w_loaded[g % 2], 16 * (g // 2 + 1))
            slot = self.ring[g % 2]
            for t in range(4):
                for h in range(2):
                    self.mm(eng, self.bank[2 * t + h][:, :], [ckv[:, k, t * P:(t + 1) * P] for k in range(KVT)],
                            [slot[:, k * D + h * 512:k * D + h * 512 + 512] for k in range(KVT)])\
                        .then_inc(v_done, 1)
        else:
            h, copy = (0, eng.tensor_copy) if who == "dve" else (1, eng.copy)
            for t in range(4):
                eng.wait_ge(v_done, 2 * t + h + 1)
                copy(v["values"][:, t * D + h * 512:t * D + h * 512 + 512], self.bank[2 * t + h][:, :])
        self.phase_end(eng, who)

    def mla_heads(self, who, eng):
        v = self.mla_views()
        names = ("proj_done", "q_copied", "kv_copied", "rot_done", "rotated", "scored", "max_ready",
                 "exp_done", "scaled", "turned", "pt_act", "pt_dve", "o_done", "o_used")
        s = {n: self.sem("mla_" + n) for n in names}
        link = self.sem("mla_link")
        ada_rows, ada_copied = self.sem("ada_rows"), self.sem("ada_rows_copied")
        rows = self.X[:, 3072:3072 + ADA_TILES * P]
        half = ADA_TILES * P // 2
        fold_at = slice(half, half + 2 * ADA_TILES)
        flat = self.ADA[:, :, :, :].rearrange("p l m s -> p (l m s)")
        scale = QK ** -0.5
        cq = v["cq"].rearrange("p (k t) -> p k t", k=QLT)
        ckv = v["ckv"].rearrange("p (k t) -> p k t", k=KVT)
        p, pt = v["p"], v["pt"].rearrange("p (b t q) -> p b t q", t=2, q=P)
        values = v["values"].rearrange("p (t d) -> p t d", t=4)
        out = self.A[:, :, :].rearrange("p k t -> p (k t)")
        ptiles = [p[:, 0:256], p[:, 256:512], p[:, 512:1024], p[:, 1024:1536]]
        mx, nb, rs, rc = [[self.S[:, 64 + 16 * e + 4 * n:64 + 16 * e + 4 * n + 4] for e in range(2)]
                          for n in range(4)]
        bank = self.bank
        g0 = FIRST["mla_head"]

        def pe_project(h, e):
            slot = self.ring[(g0 + e) % 2]
            eng.wait_ge(self.w_loaded[(g0 + e) % 2], (h - e) * 8 + 16 * ((g0 + e) // 2 + 1))
            if isinstance(h, int) and h == 0:
                pass
            else:
                eng.wait_ge(s["rotated"], h)
                eng.wait_ge(s["kv_copied"], 2 * h)
            self.mm(eng, bank[0][0:QK, :], [slot[:, k * QK:(k + 1) * QK] for k in range(QLT)],
                    [cq[:, k, :] for k in range(QLT)])
            o = QLT * QK
            self.mm(eng, bank[1][0:DN, :], [slot[:, o + k * DN:o + (k + 1) * DN] for k in range(KVT)],
                    [ckv[:, k, :] for k in range(KVT)]).then_inc(s["proj_done"], 1)

        def pe_ada_half(e, x):
            o = HEAD_W + x * half
            slot = self.ring[(g0 + e) % 2]
            return self.ada_group_rows(eng, bank[5 + 2 * x][:, :],
                                       lambda k: slot[:, o + k * 2 * half:o + k * 2 * half + half], half)

        def pe_ada_fold():
            for t in range(ADA_TILES):
                last = eng.matmul(bank[5][:, half + 2 * t:half + 2 * t + 2], rows[:, t * P:(t + 1) * P],
                                  self.con("fold"), start=True, stop=True)
            return last

        def dve_ada_copy():
            eng.tensor_copy(rows[:, 0:half], bank[5][:, 0:half])
            eng.tensor_copy(rows[:, half:2 * half], bank[7][:, 0:half]).then_inc(ada_copied, 1)

        def pe_scores(h, e):
            eng.wait_ge(s["q_copied"], h + 1)
            eng.wait_ge(s["kv_copied"], 2 * h + 2)
            eng.matmul(bank[2][0:QK, 256:512], self.con("rot_mla")[0:QK, :], v[f"q{e}"][0:QK, CTX:T],
                       start=True, stop=True).then_inc(s["rot_done"], 1)
            eng.wait_ge(s["o_used"], h + 1)
            q, qr, k = v[f"q{e}"], v[f"qr{e}"], v[f"kt{e}"]
            for t in range(2):
                last = eng.matmul(bank[3][:, t * 256:(t + 1) * 256], q[0:QK, t * P:(t + 1) * P],
                                  k[0:QK, 0:CTX], start=True, stop=True)
            last.then_inc(s["scored"], 1)
            eng.wait_ge(s["rotated"], h + 1)
            eng.wait_ge(ada_copied, h + 1)
            for t in range(2):
                eng.matmul(bank[4 + t][:, 0:CTX], q[0:QK, CTX + t * P:CTX + (t + 1) * P], k[0:QK, 0:CTX],
                           start=True, stop=True)
                eng.matmul(bank[4 + t][:, CTX:T], qr[0:QK, t * P:(t + 1) * P], k[0:QK, CTX:T],
                           start=True, stop=True).then_inc(s["scored"], 1)

        def pe_tail(h, e):
            for n, b in enumerate((6, 7, 3)):
                eng.wait_ge(s["scaled"], 4 * h + 2 + n)
                for j in range(4):
                    tile, block = (j % 2, j // 2) if n == 0 else (n + 1, j)
                    last = eng.transpose(bank[b][:, j * P:(j + 1) * P],
                                         ptiles[tile][:, block * P:(block + 1) * P], self.con("ident"))
                last.then_inc(s["turned"], 1)
            last_head = isinstance(h, int) and h == MLA_H - 1
            fold = pe_ada_fold()
            if last_head:
                fold.then_inc(ada_rows, 1)
            else:
                pe_ada_half(1 - e, 0)
            vv = v[f"v{e}"].rearrange("p (t d) -> p t d", t=4)
            eng.wait_ge(s["pt_act"], 2 * h + 2)
            eng.wait_ge(s["pt_dve"], h + 1)
            for seg in range(2):
                last = self.mm(eng, bank[4][e * DV:(e + 1) * DV, seg * 256:seg * 256 + 256],
                               [vv[:, i, :] for i in range(2 + 2 * seg)],
                               [pt[:, 2 * seg + i, :, :].rearrange("p t q -> p (t q)") for i in range(2 + 2 * seg)])
            last.then_inc(s["o_done"], 1)
            if not last_head:
                pe_ada_half(1 - e, 1).then_inc(ada_rows, 1)

        def dve_project(h, e):
            eng.wait_ge(s["proj_done"], h + 1)
            eng.tensor_copy(v[f"q{e}"][0:QK, :], bank[0][0:QK, :]).then_inc(s["q_copied"], 1)
            eng.wait_ge(s["q_copied"], h + 1)
            eng.tensor_tensor(v[f"qt{e}"][0:QK, :], v[f"q{e}"][0:QK, CTX:T], self.con("cos_mla")[0:QK, :],
                              ALU.mult).then_inc(link, 1)

        def dve_max(h, e):
            eng.wait_ge(s["rot_done"], h + 1)
            eng.tensor_tensor(v[f"qr{e}"][0:QK, :], bank[2][0:QK, 256:512], self.con("sin_mla")[0:QK, :],
                              ALU.mult).then_inc(link, 1)
            eng.wait_ge(link, self.mla_links(h, 0))
            eng.tensor_tensor(v[f"qr{e}"][0:QK, :], v[f"qr{e}"][0:QK, :], v[f"qt{e}"][0:QK, :],
                              ALU.add).then_inc(s["rotated"], 1)
            eng.wait_ge(s["scored"], 3 * h + 1)
            eng.tensor_reduce(mx[e][:, 0:2], bank[3][:, :].rearrange("p (t k) -> p t k", t=2), AX.X, ALU.max)
            for t in range(2):
                eng.wait_ge(s["scored"], 3 * h + 2 + t)
                last = eng.tensor_reduce(mx[e][:, 2 + t:3 + t], bank[4 + t][:, :], AX.X, ALU.max)
            last.then_inc(link, 1)
            eng.wait_ge(link, self.mla_links(h, 1))
            eng.tensor_scalar(nb[e], mx[e], -scale, None, ALU.mult).then_inc(s["max_ready"], 1)
            dve_scale(h, e)

        def dve_scale(h, e):
            for half in range(2):
                eng.wait_ge(s["exp_done"], 4 * h + 2 * half + 2)
                c = slice(2 * half, 2 * half + 2)
                eng.reciprocal(rc[e][:, c], rs[e][:, c]).then_inc(link, 1)
                eng.wait_ge(link, self.mla_links(h, 2 + half))
                for t in (2 * half, 2 * half + 1):
                    eng.tensor_scalar(ptiles[t], ptiles[t], rc[e][:, t:t + 1], None, ALU.mult)\
                        .then_inc(s["scaled"], 1)

        def dve_tail(h, e):
            eng.wait_ge(s["turned"], 3 * h + 2)
            eng.tensor_copy(pt[:, 2:6, 0, :], bank[7][:, :].rearrange("p (b q) -> p b q", b=4))\
                .then_inc(s["pt_dve"], 1)
            eng.wait_ge(s["o_done"], h + 1)
            rows_e = slice(e * DV, (e + 1) * DV)
            eng.tensor_copy(out[rows_e, bass.ds((h - e) * (T // 2), T)], bank[4][rows_e, :])\
                .then_inc(s["o_used"], 1)
            eng.wait_ge(ada_rows, h + 2)
            eng.tensor_copy(flat[:, bass.ds(2 * ADA_FIRST + h * 2 * ADA_TILES, 2 * ADA_TILES)],
                            bank[5][:, fold_at])
            if not (isinstance(h, int) and h == MLA_H - 1):
                dve_ada_copy()

        def act_project(h, e):
            eng.wait_ge(s["proj_done"], h + 1)
            eng.copy(v[f"kt{e}"][0:DN, :], bank[1][0:DN, :]).then_inc(s["kv_copied"], 1)
            eng.copy(v[f"v{e}"].rearrange("p (t d) -> p t d", t=4), values[:, :, bass.ds(h * DV, DV)])\
                .then_inc(s["kv_copied"], 1)

        def act_exp(h, e):
            eng.wait_ge(s["max_ready"], h + 1)
            src = [bank[3][:, 0:256], bank[3][:, 256:512], bank[4][:, :], bank[5][:, :]]
            for t in range(4):
                eng.activation(ptiles[t], src[t], ACT.Exp, bias=nb[e][:, t:t + 1], scale=scale,
                               accum_out=rs[e][:, t:t + 1]).then_inc(s["exp_done"], 1)

        def act_tail(h, e):
            eng.wait_ge(s["turned"], 3 * h + 1)
            eng.copy(v["pt"][:, 0:512], bank[6][:, :]).then_inc(s["pt_act"], 1)
            eng.wait_ge(s["turned"], 3 * h + 3)
            eng.copy(pt[:, 2:6, 1, :], bank[3][:, :].rearrange("p (b q) -> p b q", b=4))\
                .then_inc(s["pt_act"], 1)

        steps = {"pe": (pe_project, pe_scores, pe_tail), "dve": (dve_project, dve_max, dve_tail),
                 "act": (act_project, act_exp, act_tail)}[who]
        if who == "dve":
            eng.nop().then_inc(s["o_used"], 1)
        if who == "act":
            biases = self.N[:, :].rearrange("p (t h k) -> p t h k", t=2, h=16)
            for row in range(4):
                part = slice(64 * (row % 2), 64 * (row % 2) + 64)
                eng.dma_start(biases[part, row // 2, :, :], self.nab_d[row]).then_inc(self.bias_in, 16)

        def prologue():
            if who == "pe":
                pe_ada_half(0, 0)
                pe_ada_half(0, 1).then_inc(ada_rows, 1)
            if who == "dve":
                eng.wait_ge(ada_rows, 1)
                dve_ada_copy()
        self.pipelined(eng, MLA_H, *steps, prologue)
        self.phase_end(eng, who)
        self.ada_rest(who, eng)
        self.phase_end(eng, who)

    @staticmethod
    def mla_links(h, which):
        return h * 5 + 2 + which

    def pipelined(self, eng, n, project, middle, tail, prologue=None):
        project(0, 0)
        if prologue:
            prologue()
        with eng.Fori(0, n // 2 - 1) as it:
            for e in range(2):
                u = it * 2 + e
                middle(u, e)
                project(u + 1, 1 - e)
                tail(u, e)
        for u in (n - 2, n - 1):
            middle(u, u % 2)
            if u + 1 < n:
                project(u + 1, (u + 1) % 2)
            tail(u, u % 2)

    def mla_out(self, who, eng):
        self.project_residual(who, eng, "mla_o", lambda k: self.A[:, k, :], KT, 4, 2, 0, (0, 1))
        self.layer_norm(who, eng, 0, "ln1_g", "ln1_b", 0, (0, 3, 4, (0, 1)))

    def ffn(self, who, eng, layer):
        segs = (0, 1) if layer == 0 else (1,)
        c0 = CTX * segs[0]
        w = T - c0
        ns = len(segs)
        name = f"ffn{layer}_"
        up_done, up_used, gate_in, gate_out, hid_done = \
            [self.sem(name + x) for x in ("up_done", "up_used", "gate_in", "gate_out", "hid_done")]
        link = self.sem(name + "link")
        hid = self.B[:, :].rearrange("p (f t) -> p f t", f=FT)
        cw, cb = VOFF["conv_w"][0] + layer * 3 * 2 * FT, VOFF["conv_b"][0] + layer * 2 * FT
        u = [[self.X[:, (2 * e + x) * T:(2 * e + x) * T + w] for x in range(2)] for e in range(2)]
        sg = [self.X[:, (4 + e) * T:(4 + e) * T + w] for e in range(2)]

        if who == "pe":
            def body(j, slot):
                for e in range(2):
                    f = j * 2 + e
                    if not (isinstance(j, int) and j == 0):
                        eng.wait_ge(up_used, f - 1)
                    for x in range(2):
                        m = 2 * x + e
                        last = self.mm(eng, self.bank[2 * e + x][:, 0:w],
                                       [slot[:, (m * KT + k) * P:(m * KT + k + 1) * P] for k in range(KT)],
                                       [self.A[:, k, c0:T] for k in range(KT)])
                    last.then_inc(up_done, 1)
            g = FIRST[f"ffn_in{layer}"]
            eng.wait_ge(self.w_loaded[g % 2], 16 * (g // 2 + 1))
            body(0, self.ring[g % 2])
            self.chunks(eng, f"ffn_in{layer}", body, count=CHUNKS[f"ffn_in{layer}"] - 1, start=1)

        def seg(ap, lo, hi):
            return ap.rearrange("p (s t) -> p s t", s=ns)[:, :, lo:hi]

        def conv(f, e):
            eng.wait_ge(up_done, f + 1)
            for tap, (olo, ohi, ilo, ihi) in enumerate(((None,) * 4, (1, 256, 0, 255), (0, 255, 1, 256))):
                for x in range(2):
                    src, dst = self.bank[2 * e + x][:, 0:w], u[e][x]
                    col = f + x * FT
                    if tap == 0:
                        ins = eng.tensor_scalar(dst, src, self.V[:, bass.ds(cw + 2 * FT + col, 1)],
                                                self.V[:, bass.ds(cb + col, 1)], ALU.mult, ALU.add)
                    else:
                        t = 0 if tap == 1 else 2
                        ins = eng.scalar_tensor_tensor(
                            out=seg(dst, olo, ohi), in0=seg(src, ilo, ihi),
                            scalar=self.V[:, bass.ds(cw + t * 2 * FT + col, 1)],
                            in1=seg(dst, olo, ohi), op0=ALU.mult, op1=ALU.add)
                if tap < 2:
                    ins.then_inc(link, 1)
                    eng.wait_ge(link, f * 2 + tap + 1)
            ins.then_inc(up_used, 1)

        def mult(f, e):
            eng.wait_ge(gate_out, f + 1)
            eng.wait_ge(up_used, f + 1)
            eng.tensor_tensor(hid[:, bass.ds(f, 1), 0:w].rearrange("p a t -> p (a t)"), u[e][0], sg[e],
                              ALU.mult).then_inc(hid_done, 1)
            eng.wait_ge(hid_done, f + 1)

        if who == "dve":
            conv(0, 0)
            with eng.Fori(0, FT // 2 - 1) as it:
                conv(it * 2 + 1, 1)
                mult(it * 2, 0)
                conv(it * 2 + 2, 0)
                mult(it * 2 + 1, 1)
            conv(FT - 1, 1)
            mult(FT - 2, 0)
            mult(FT - 1, 1)
        if who == "act":
            with eng.Fori(0, FT // 2) as it:
                for e in range(2):
                    f = it * 2 + e
                    eng.wait_ge(up_used, f + 1)
                    eng.activation(sg[e], u[e][1], ACT.Silu).then_inc(gate_out, 1)
        self.phase_end(eng, who)
        if layer == 0 and who == "dve":
            eng.wait_ge(self.bias_in, 64)
            biases = self.N[:, :].rearrange("p (t h k) -> p t h k", t=2, h=16)
            for t in range(2):
                eng.tensor_tensor(biases[:, t, :, :], biases[:, t, :, :],
                                  self.con("na_mask").unsqueeze(1).to_broadcast([P, 16, LAT]), ALU.add)
        nm = f"ffn_out{layer}"
        self.project_residual(who, eng, nm, lambda k: hid[:, k, 0:w], FT, 2, 5, layer, segs)
        self.layer_norm(who, eng, c0, "ln2_g", "ln2_b", layer, (1, 0, 1, (0, 1)) if layer == 0 else None)

    def na_views(self):
        b, v, at = self.B, {}, 0
        for name, n in (("q0", 2 * LAT), ("q1", 2 * LAT), ("k0", T), ("k1", T), ("v0", 4 * P), ("v1", 4 * P),
                        ("p", 4 * T), ("pt", 4 * T)):
            v[name] = b[:, at:at + n]
            at += n
        assert at <= FT * T
        v["oT"] = self.X[:, 4 * T:4 * T + KT * LAT]
        return v

    def na_heads(self, who, eng):
        v = self.na_views()
        names = ("proj_done", "q_copied", "k_copied", "v_copied", "scored", "biased", "max_ready", "exp_done",
                 "scaled", "turned", "pt_act", "pt_dve", "o_done", "o_used")
        s = {n: self.sem("na_" + n) for n in names}
        link = self.sem("na_link")
        bank = self.bank
        scale = 64 ** -0.5
        g0 = FIRST["na_pair"]
        sc = self.X[:, 0:4 * T].rearrange("p (n k) -> p n k", n=4)
        p = v["p"].rearrange("p (n k) -> p n k", n=4)
        pt = v["pt"].rearrange("p (h b t q) -> p h b t q", h=2, b=4, q=P)
        qz = [v[f"q{e}"].rearrange("p (h t) -> p h t", h=2) for e in range(2)]
        nb_all = self.N[:, :].rearrange("p (t h k) -> p t h k", t=2, h=16)
        mx, nb, rs, rc = [[self.S[:, 64 + 16 * e + 4 * n:64 + 16 * e + 4 * n + 4] for e in range(2)]
                          for n in range(4)]
        pt_bank = (7, 3, 4, 5)
        if who == "dve":
            for e in range(2):
                eng.memset(qz[e], 0.0)
        self.phase_end(eng, who)

        def pe_project(u, e):
            slot = self.ring[(g0 + e) % 2]
            eng.wait_ge(self.w_loaded[(g0 + e) % 2], (u - e) * 8 + 16 * ((g0 + e) // 2 + 1))
            if not (isinstance(u, int) and u == 0):
                eng.wait_ge(s["q_copied"], u)
                eng.wait_ge(s["k_copied"], u)
                eng.wait_ge(s["v_copied"], u)
            self.mm(eng, bank[0][:, 0:LAT], [slot[:, k * P:(k + 1) * P] for k in range(KT)],
                    [self.A[:, k, CTX:T] for k in range(KT)])
            self.mm(eng, bank[1][:, :], [slot[:, D + k * P:D + (k + 1) * P] for k in range(KT)],
                    [self.A[:, k, :] for k in range(KT)])
            for t in range(4):
                last = self.mm(eng, bank[2][:, t * P:(t + 1) * P],
                               [self.A[:, k, t * P:(t + 1) * P] for k in range(KT)],
                               [slot[:, 2 * D + k * P:2 * D + (k + 1) * P] for k in range(KT)])
            last.then_inc(s["proj_done"], 1)

        def pe_scores(u, e):
            eng.wait_ge(s["q_copied"], u + 1)
            eng.wait_ge(s["k_copied"], u + 1)
            eng.wait_ge(s["o_used"], u + 1)
            for n in range(4):
                h, t = n // 2, n % 2
                eng.matmul(bank[3 + n][:, :], qz[e][:, h, t * P:(t + 1) * P], v[f"k{e}"],
                           start=True, stop=True).then_inc(s["scored"], 1)

        def pe_tail(u, e):
            for n in range(4):
                eng.wait_ge(s["scaled"], 4 * u + n + 1)
                for b in range(4):
                    last = eng.transpose(bank[pt_bank[n]][:, b * P:(b + 1) * P], p[:, n, b * P:(b + 1) * P],
                                         self.con("ident"))
                last.then_inc(s["turned"], 1)
            eng.wait_ge(s["v_copied"], u + 1)
            vv = v[f"v{e}"].rearrange("p (t d) -> p t d", t=4)
            eng.wait_ge(s["pt_dve"], 2 * u + 2)
            eng.wait_ge(s["pt_act"], 2 * u + 2)
            for b in range(4):
                for h in range(2):
                    last = eng.matmul(bank[6][h * 64:(h + 1) * 64, 0:LAT], vv[:, b, h * 64:(h + 1) * 64],
                                      pt[:, h, b, :, :].rearrange("p t q -> p (t q)"), start=(b == 0),
                                      stop=(b == 3), skip_group_check=True)
            last.then_inc(s["o_done"], 1)

        def dve_project(u, e):
            eng.wait_ge(s["proj_done"], u + 1)
            eng.tensor_copy(qz[e][0:64, 0, :], bank[0][0:64, 0:LAT])
            eng.tensor_copy(qz[e][64:128, 1, :], bank[0][64:128, 0:LAT]).then_inc(s["q_copied"], 1)

        def dve_max(u, e):
            for n in range(4):
                h, t = n // 2, n % 2
                eng.wait_ge(s["scored"], 4 * u + n + 1)
                eng.tensor_scalar(sc[:, n, 0:CTX], bank[3 + n][:, 0:CTX], scale, None, ALU.mult)
                bias = nb_all[:, t, bass.ds(u * 2 + h, 1), :].rearrange("p a k -> p (a k)")
                eng.scalar_tensor_tensor(out=sc[:, n, CTX:T], in0=bank[3 + n][:, CTX:T], scalar=scale,
                                         in1=bias, op0=ALU.mult, op1=ALU.add).then_inc(s["biased"], 1)
            eng.wait_ge(s["biased"], 4 * u + 4)
            eng.tensor_reduce(mx[e], sc, AX.X, ALU.max).then_inc(link, 1)
            eng.wait_ge(link, 3 * u + 1)
            eng.tensor_scalar(nb[e], mx[e], -1.0, None, ALU.mult).then_inc(s["max_ready"], 1)
            for h in range(2):
                eng.wait_ge(s["exp_done"], 4 * u + 2 * h + 2)
                c = slice(2 * h, 2 * h + 2)
                eng.reciprocal(rc[e][:, c], rs[e][:, c]).then_inc(link, 1)
                eng.wait_ge(link, 3 * u + 2 + h)
                for n in (2 * h, 2 * h + 1):
                    eng.tensor_scalar(p[:, n, :], p[:, n, :], rc[e][:, n:n + 1], None, ALU.mult)\
                        .then_inc(s["scaled"], 1)

        def dve_tail(u, e):
            copy_turned(u, 0, eng.tensor_copy, "pt_dve")
            eng.wait_ge(s["o_done"], u + 1)
            eng.tensor_copy(v["oT"][:, bass.ds(u * LAT, LAT)], bank[6][:, 0:LAT]).then_inc(s["o_used"], 1)

        def copy_turned(u, t, copy, sem):
            for h in range(2):
                n = 2 * h + t
                eng.wait_ge(s["turned"], 4 * u + n + 1)
                copy(pt[:, h, :, t, :], bank[pt_bank[n]][:, :].rearrange("p (b q) -> p b q", b=4))\
                    .then_inc(s[sem], 1)

        def act_project(u, e):
            eng.wait_ge(s["proj_done"], u + 1)
            eng.copy(v[f"k{e}"], bank[1][:, :]).then_inc(s["k_copied"], 1)
            eng.copy(v[f"v{e}"], bank[2][:, :]).then_inc(s["v_copied"], 1)

        def act_exp(u, e):
            eng.wait_ge(s["max_ready"], u + 1)
            for n in range(4):
                eng.activation(p[:, n, :], sc[:, n, :], ACT.Exp, bias=nb[e][:, n:n + 1], scale=1.0,
                               accum_out=rs[e][:, n:n + 1]).then_inc(s["exp_done"], 1)

        def act_tail(u, e):
            copy_turned(u, 1, eng.copy, "pt_act")

        steps = {"pe": (pe_project, pe_scores, pe_tail), "dve": (dve_project, dve_max, dve_tail),
                 "act": (act_project, act_exp, act_tail)}[who]
        if who == "dve":
            eng.nop().then_inc(s["o_used"], 1)
        self.pipelined(eng, NA_PAIRS, *steps)
        self.phase_end(eng, who)

    def na_out(self, who, eng):
        oT = self.na_views()["oT"].rearrange("p (k t) -> p k t", k=KT)
        self.project_residual(who, eng, "na_o", lambda k: oT[:, k, :], KT, 4, 2, 1, (1,))
        self.layer_norm(who, eng, CTX, "ln1_g", "ln1_b", 1, (1, 3, 4, (1,)))

    def rms_to_input(self, who, eng, gain):
        def write(x, r):
            for k in range(KT):
                eng.scalar_tensor_tensor(out=self.A[:, k, CTX:T], in0=x(k), scalar=self.vec(gain, k, 1), in1=r,
                                         op0=ALU.mult, op1=ALU.mult)
        self.norm(who, eng, CTX, write, centre=False, eps=RMS_EPS)

    def tile2(self, t, n=1):
        return self.B[:, t * LAT:(t + n) * LAT]

    def proj(self, who, eng):
        self.rms_to_input(who, eng, "attn_norm")
        done, used = self.sem("proj_tile_done"), self.sem("proj_tile_used")
        if who == "pe":
            def body(j, slot):
                for t in range(6):
                    if not (isinstance(j, int) and j == 0):
                        eng.wait_ge(used, j * 6 + t - 5)
                    last = self.mm(eng, self.bank[t][:, 0:LAT],
                                   [slot[:, (t * KT + k) * P:(t * KT + k + 1) * P] for k in range(KT)],
                                   [self.A[:, k, CTX:T] for k in range(KT)])
                    last.then_inc(done, 1)
            g = FIRST["proj"]
            eng.wait_ge(self.w_loaded[g % 2], 16 * (g // 2 + 1))
            body(0, self.ring[g % 2])
            self.chunks(eng, "proj", body, count=CHUNKS["proj"] - 1, start=1)
            for t in range(2):
                self.mm(eng, self.bank[6][:, t * 24:(t + 1) * 24],
                        [self.A[:, k, CTX + t * P:CTX + (t + 1) * P] for k in range(KT)],
                        [self.vec("w_gate24", k * 24, 24) for k in range(KT)])
        if who == "dve":
            with eng.Fori(0, CHUNKS["proj"]) as j:
                for t in range(6):
                    eng.wait_ge(done, j * 6 + t + 1)
                    eng.tensor_copy(self.B[:, bass.ds(j * (6 * LAT) + t * LAT, LAT)], self.bank[t][:, 0:LAT])\
                        .then_inc(used, 1)
        self.phase_end(eng, who)
        if who == "act":
            eng.activation(self.S[:, 0:48], self.bank[6][:, 0:48], ACT.Sigmoid)
            eng.activation(self.tile2(T_HF, 4), self.tile2(T_HF, 4), ACT.Sigmoid)
            eng.activation(self.tile2(T_MN, 16), self.tile2(T_MN, 16), ACT.Sigmoid)
            eng.activation(self.tile2(T_HGATE, 4), self.tile2(T_HGATE, 4), ACT.Silu)
        self.phase_end(eng, who)

    def nsa_views(self):
        n, x, v, at = self.N, self.X, {}, 0
        for name, w in (("qr", 4 * LAT), ("sk", LAT), ("wk", LAT), ("kc", 16), ("vc", P), ("vtok", 12 * P),
                        ("qz0", 2 * LAT // 2), ("qz1", 2 * LAT // 2), ("o_hg", 4 * LAT),
                        ("s0", 800), ("s1", 800), ("p0", 800), ("p1", 800)):
            v[name] = n[:, at:at + w]
            at += w
        assert at <= 16 * 2 * LAT, at
        v["at"] = v["s0"].offset
        at = 0
        for name, w in (("pt", 16 * P), ("o", 2 * 512), ("t0", 384), ("t1", 384)):
            v[name] = x[:, at:at + w]
            at += w
        assert at <= KT * T
        return v

    def compress(self, who, eng):
        v = self.nsa_views()
        bank = self.bank
        af = self.A[:, :, :].rearrange("p k t -> p (k t)")
        blk = [af[:, 1024 * x:1024 * x + 1024].rearrange("p (n l) -> p n l", l=32) for x in range(2)]
        parts = [af[:, 2048 + P * x:2048 + P * (x + 1)] for x in range(2)]
        if who == "dve":
            self.link(eng, who, eng.memset(af[:, 0:2048], 0.0))
            for x, tile in enumerate((T_CK, T_CV)):
                rows = self.tile2(tile).rearrange("p (n b) -> p n b", b=16)
                for a in range(2):
                    pos = self.vec("cmp_pos", 16 * a, 16).unsqueeze(1).to_broadcast([P, NCMP, 16])
                    eng.tensor_tensor(blk[x][:, 0:NCMP, 16 * a:16 * a + 16], rows[:, a:a + NCMP, :], pos, ALU.add)
        self.phase_end(eng, who)
        tiles = [T_Q, T_Q + 1, T_Q + 2, T_Q + 3, T_SK, T_WK]
        turn = [T_SV, T_WV, T_HI, T_HI + 1, T_HI + 2, T_HI + 3]
        vtok = v["vtok"].rearrange("p (t m d) -> p t m d", t=2, m=6)
        if who == "pe":
            for x in range(2):
                g = FIRST["cmp"] + x
                eng.wait_ge(self.w_loaded[g % 2], 16 * (g // 2 + 1))
                slot = self.ring[g % 2]
                for l in range(32):
                    rows = slice(32 * (l % 4), 32 * (l % 4) + 32)
                    last = eng.matmul(bank[x][rows, 0:P], blk[x][:, :, l], slot[:, l * P:(l + 1) * P],
                                      start=(l < 4), stop=(l >= 28), skip_group_check=True)
                last.then_inc(self.sem("cmp_used"), 1)
            for i, t in enumerate(tiles):
                eng.matmul(bank[2 + i // 2][:, (i % 2) * LAT:(i % 2 + 1) * LAT], self.con("rot_nsa"),
                           self.tile2(t), start=True, stop=True)
            for i, t in enumerate(turn):
                for tt in range(2):
                    b = 5 + i // 2
                    c = (i % 2) * LAT + tt * P
                    eng.transpose(bank[b][:, c:c + P], self.tile2(t)[:, tt * P:(tt + 1) * P], self.con("ident"))
        self.phase_end(eng, who)
        if who == "dve":
            for x in range(2):
                eng.tensor_copy(parts[x], bank[x][:, 0:P])
            for i, t in enumerate(tiles):
                dst = v["qr"][:, i * LAT:(i + 1) * LAT] if i < 4 else v["sk" if i == 4 else "wk"]
                src = self.tile2(t)
                self.link(eng, who, eng.tensor_tensor(src, src, self.con("cos_nsa"), ALU.mult))
                self.link(eng, who, eng.tensor_tensor(dst, bank[2 + i // 2][:, (i % 2) * LAT:(i % 2 + 1) * LAT],
                                                      self.con("sin_nsa"), ALU.mult))
                self.link(eng, who, eng.tensor_tensor(dst, dst, src, ALU.add))
        if who == "act":
            for i in range(6):
                for tt in range(2):
                    c = (i % 2) * LAT + tt * P
                    eng.copy(vtok[:, tt, i, :], bank[5 + i // 2][:, c:c + P])
        self.phase_end(eng, who)
        if who == "pe":
            eng.matmul(bank[0][:, 0:16], parts[0], self.con("cmp_fold"), start=True, stop=True)
            eng.matmul(bank[1][0:16, 0:P], self.con("cmp_fold"), parts[1], start=True, stop=True)
        self.phase_end(eng, who)
        if who == "dve":
            eng.tensor_copy(v["kc"], bank[0][:, 0:16])
        self.phase_end(eng, who)
        if who == "pe":
            eng.matmul(bank[0][:, 0:16], self.con("rot_nsa"), v["kc"], start=True, stop=True)
        self.phase_end(eng, who)
        if who == "dve":
            at16 = [self.con(c).rearrange("p (n b) -> p n b", b=16)[:, :, 0] for c in ("cos_nsa", "sin_nsa")]
            tmp = self.S[:, 64:80]
            self.link(eng, who, eng.tensor_tensor(tmp, bank[0][:, 0:16], at16[1], ALU.mult))
            self.link(eng, who, eng.tensor_tensor(v["kc"], v["kc"], at16[0], ALU.mult))
            eng.tensor_tensor(v["kc"], v["kc"], tmp, ALU.add)
            eng.tensor_copy(v["vc"][0:16, :], bank[1][0:16, 0:P])
            eng.memset(v["qz0"], 0.0)
            eng.memset(v["qz1"], 0.0)
        self.phase_end(eng, who)

    def nsa_heads(self, who, eng):
        v = self.nsa_views()
        names = ("q_ready", "scored", "max_ready", "exp_done", "kept", "turned", "pt_copied", "o_done", "o_used",
                 "added")
        s = {n: self.sem("nsa_" + n) for n in names}
        front_link, tail_link = self.sem("nsa_front_link"), self.sem("nsa_tail_link")
        bank = self.bank
        scale = 64 ** -0.5
        qz = [v["qz0"], v["qz1"]]
        sc, p = [v["s0"], v["s1"]], [v["p0"], v["p1"]]
        pt = v["pt"].rearrange("p (e b q) -> p e b q", e=2, q=P)
        o = v["o"].rearrange("p (t d) -> p t d", t=2)
        tmp = [v[f"t{e}"].rearrange("p (b t d) -> p b t d", b=3, t=2) for e in range(2)]
        vtok = v["vtok"].rearrange("p (t m d) -> p t m d", t=2, m=6)
        mx, nb, rs, fc = [[self.S[:, 64 + 32 * e + 6 * n:64 + 32 * e + 6 * n + 6] for e in range(2)]
                          for n in range(4)]
        segs = [(0, 128), (128, 384), (384, 400), (400, 416), (416, 544), (544, 800)]
        sb = [(3, 4), (5, 6)]
        tb = [(7, 0), (1, 2)]
        blocks = [(0, 128), (128, 256), (256, 384), (384, 400), (416, 544), (544, 672), (672, 800), (400, 416)]
        gates = self.S[:, 0:48].rearrange("p (t c) -> p t c", t=2)

        def pe_scores(u, e):
            eng.wait_ge(s["q_ready"], u + 1)
            a, b = (bank[i] for i in sb[e])
            q = qz[e]
            for k, bk in ((v["sk"], a), (v["wk"], b)):
                eng.matmul(bk[:, 0:128], q[:, 0:P], k[:, 0:P], start=True, stop=True)
                eng.matmul(bk[:, 128:384], q[:, P:LAT], k, start=True, stop=True)
            for t in range(2):
                last = eng.matmul(a[:, 384 + 16 * t:400 + 16 * t], q[:, t * P:(t + 1) * P], v["kc"],
                                  start=True, stop=True)
            last.then_inc(s["scored"], 1)

        def pe_next(u, e):
            if isinstance(u, int) and u == 0:
                pe_scores(0, 0)
            if not (isinstance(u, int) and u + 1 == 2 * NSA_PAIRS):
                pe_scores(u + 1, 1 - e)

        def pe_turn(u, e):
            eng.wait_ge(s["kept"], u + 1)
            for i, (lo, hi) in enumerate(blocks):
                last = eng.transpose(bank[tb[e][i // 4]][0:hi - lo, (i % 4) * P:(i % 4 + 1) * P],
                                     p[e][:, lo:hi], self.con("ident"))
            last.then_inc(s["turned"], 1)

        def pe_out(u, e):
            eng.wait_ge(s["pt_copied"], 2 * u + 2)
            ob = bank[tb[e][0]]
            g = slice(64 * e, 64 * e + 64)

            def out(i):
                return ob[:, i * 64:(i + 1) * 64]
            for br, m, b0 in ((0, 0, 0), (2, 1, 4)):
                eng.matmul(out(2 * br), pt[:, e, b0, :], vtok[:, 0, m, g], start=True, stop=True)
                self.mm(eng, out(2 * br + 1), [pt[:, e, b0 + 1, :], pt[:, e, b0 + 2, :]],
                        [vtok[:, 0, m, g], vtok[:, 1, m, g]])
            for t in range(2):
                last = eng.matmul(out(2 + t), pt[0:16, e, (3, 7)[t], :], v["vc"][0:16, g],
                                  start=True, stop=True)
            last.then_inc(s["o_done"], 1)

        def dve_query(u, e):
            r = slice(64 * e, 64 * e + 64)
            eng.tensor_copy(qz[e][r, :], v["qr"][r, bass.ds((u - e) * (LAT // 2), LAT)]).then_inc(s["q_ready"], 1)

        def dve_front(u, e):
            eng.wait_ge(s["scored"], u + 1)
            eng.scalar_tensor_tensor(out=sc[e][:, 0:416], in0=bank[sb[e][0]][:, 0:416], scalar=scale,
                                     in1=self.con("nsa_mask"), op0=ALU.mult, op1=ALU.add)
            eng.scalar_tensor_tensor(out=sc[e][:, 416:800], in0=bank[sb[e][1]][:, 0:384],
                                     scalar=scale, in1=self.con("nsa_mask", 0, 384), op0=ALU.mult,
                                     op1=ALU.add).then_inc(front_link, 1)
            eng.wait_ge(front_link, 2 * u + 1)
            for i, (lo, hi) in enumerate(segs):
                last = eng.tensor_reduce(mx[e][:, i:i + 1], sc[e][:, lo:hi], AX.X, ALU.max)
            last.then_inc(front_link, 1)
            eng.wait_ge(front_link, 2 * u + 2)
            eng.tensor_scalar(nb[e], mx[e], -1.0, None, ALU.mult).then_inc(s["max_ready"], 1)

        def dve_turn(u, e):
            if not (isinstance(u, int) and u + 2 >= 2 * NSA_PAIRS):
                dve_query(u + 2, e)
            eng.wait_ge(s["exp_done"], u + 1)
            eng.tensor_tensor(p[e][:, 384:416], p[e][:, 384:416], self.con("cmp_keep"), ALU.mult)\
                .then_inc(s["kept"], 1)
            eng.reciprocal(fc[e], rs[e]).then_inc(tail_link, 1)
            eng.wait_ge(tail_link, 2 * u + 1)
            f = fc[e].rearrange("p (b t) -> p b t", t=2)
            eng.tensor_tensor(f, f, gates[:, :, bass.ds((u - e) * 3 + 3 * e, 3)].rearrange("p t b -> p b t"),
                              ALU.mult).then_inc(tail_link, 1)
            eng.wait_ge(s["turned"], u + 1)
            for half in range(2):
                eng.tensor_copy(pt[:, e, 4 * half:4 * half + 3, :],
                                bank[tb[e][half]][:, 0:384].rearrange("p (b q) -> p b q", q=P))
                eng.tensor_copy(pt[0:16, e, 4 * half + 3, :], bank[tb[e][half]][0:16, 384:512])\
                    .then_inc(s["pt_copied"], 1)

        def dve_out(u, e):
            eng.wait_ge(s["o_done"], u + 1)
            eng.wait_ge(tail_link, 2 * u + 2)
            eng.tensor_tensor(v[f"t{e}"].rearrange("p (i d) -> p i d", d=64),
                              bank[tb[e][0]][:, 0:384].rearrange("p (i d) -> p i d", d=64),
                              fc[e].unsqueeze(2).to_broadcast([P, 6, 64]), ALU.mult).then_inc(s["o_used"], 1)
            eng.wait_ge(s["o_used"], u + 1)
            dst = o[:, :, bass.ds((u - e) * 32 + 256 * e, 64)]
            eng.tensor_tensor(tmp[e][:, 0, :, :], tmp[e][:, 0, :, :], tmp[e][:, 1, :, :], ALU.add)\
                .then_inc(s["added"], 1)
            eng.wait_ge(s["added"], u + 1)
            eng.tensor_tensor(dst, tmp[e][:, 0, :, :], tmp[e][:, 2, :, :], ALU.add)

        def act_front(u, e):
            eng.wait_ge(s["max_ready"], u + 1)
            for i, (lo, hi) in enumerate(segs):
                last = eng.activation(p[e][:, lo:hi], sc[e][:, lo:hi], ACT.Exp, bias=nb[e][:, i:i + 1],
                                      scale=1.0, accum_out=rs[e][:, i:i + 1])
            last.then_inc(s["exp_done"], 1)

        def nothing(u, e):
            pass
        steps = {"pe": (pe_next, pe_turn, pe_out), "dve": (dve_front, dve_turn, dve_out),
                 "act": (act_front, nothing, nothing)}[who]
        if who == "dve":
            dve_query(0, 0)
            dve_query(1, 1)
        self.pipelined(eng, 2 * NSA_PAIRS, *steps)
        self.phase_end(eng, who)

    def hgrn(self, who, eng):
        v = self.nsa_views()
        bank = self.bank
        af = self.A[:, :, :].rearrange("p k t -> p (k t)")
        logf, K, E0, KL = [af[:, 1024 * i:1024 * (i + 1)] for i in range(4)]
        QL = self.X[:, 0:1024]
        Es = [E0, self.X[:, 1024:2048]]
        b = self.X[:, 3072:4096]
        n0 = 16 * 2 * LAT - 3 * 1024
        diag = self.N[:, n0:n0 + 1024]
        tmp = self.N[:, n0 + 1024:n0 + 2048]
        off = self.N[:, n0 + 2048:n0 + 2560]
        q, f = self.tile2(T_HQ, 4), self.tile2(T_HF, 4)
        o = v["o_hg"]
        vtok = v["vtok"].rearrange("p (t m d) -> p t m d", t=2, m=6)
        lo = self.S[:, 64:96]
        if who == "dve":
            a0, a1 = self.vec("hg_lb", 0, HG), self.vec("hg_lb", HG, HG)
            self.link(eng, who, eng.tensor_tensor(lo[:, 8:12], a0, a1, ALU.max))
            eng.tensor_tensor(lo[:, 0:4], a0, lo[:, 8:12], ALU.subtract)
            eng.tensor_tensor(lo[:, 4:8], a1, lo[:, 8:12], ALU.subtract)
        self.phase_end(eng, who)
        if who == "act":
            eng.activation(lo[:, 0:8], lo[:, 0:8], ACT.Exp)
        self.phase_end(eng, who)
        if who == "dve":
            self.link(eng, who, eng.tensor_tensor(lo[:, 8:12], lo[:, 0:4], lo[:, 4:8], ALU.add))
            self.link(eng, who, eng.reciprocal(lo[:, 8:12], lo[:, 8:12]))
            self.link(eng, who, eng.tensor_tensor(lo[:, 0:4], lo[:, 0:4], lo[:, 8:12], ALU.mult))
            self.link(eng, who, eng.tensor_scalar(lo[:, 4:8], lo[:, 0:4], -1.0, 1.0, ALU.mult, ALU.add))
            for h in range(HG):
                fh = f[:, h * LAT:(h + 1) * LAT]
                last = eng.tensor_scalar(fh, fh, lo[:, 4 + h:5 + h], lo[:, h:h + 1], ALU.mult, ALU.add)
            self.link(eng, who, last)
            eng.tensor_scalar(K, f, -1.0, 1.0, ALU.mult, ALU.add)
        self.phase_end(eng, who)
        if who == "act":
            eng.activation(logf, f, ACT.Ln)
        self.phase_end(eng, who)
        if who == "dve":
            for h in range(HG):
                c = slice(h * LAT, (h + 1) * LAT)
                last = eng.tensor_tensor_scan(b[:, c], self.con("scan_keep"), logf[:, c], 0.0,
                                              ALU.mult, ALU.add)
            self.link(eng, who, last)

        def exponents(level, E):
            if level == 128:
                bb, ee = [x.rearrange("p (h c t) -> p h c t", h=HG, c=4) for x in (b, E)]
                end = lambda c: bb[:, :, c, 63:64].to_broadcast([P, HG, 64])
                eng.tensor_tensor(ee[:, :, 1, :], end(1), bb[:, :, 1, :], ALU.subtract)
                self.link(eng, who, eng.tensor_tensor(ee[:, :, 0, :], end(0), bb[:, :, 0, :], ALU.subtract))
                eng.tensor_tensor(ee[:, :, 0, :], ee[:, :, 0, :], end(1), ALU.add)
                eng.tensor_copy(ee[:, :, 2, :], bb[:, :, 2, :])
                return eng.tensor_tensor(ee[:, :, 3, :], bb[:, :, 3, :], end(2), ALU.add)
            m = level
            bb, ee = [x.rearrange("p (n s t) -> p n s t", s=2, t=m) for x in (b, E)]
            n = 1024 // (2 * m)
            ref = bb[:, :, 0, m - 1:m].to_broadcast([P, n, m])
            eng.tensor_tensor(ee[:, :, 0, :], ref, bb[:, :, 0, :], ALU.subtract)
            if m == 64:
                return eng.tensor_copy(ee[:, :, 1, :], bb[:, :, 1, :])
            return eng.tensor_tensor(ee[:, :, 1, :], bb[:, :, 1, :], ref, ALU.subtract)

        e_ready, x_ready, kq_ready, mm_done, consumed = \
            [self.sem("hg_" + x) for x in ("exponents", "decays", "decayed", "products", "consumed")]
        levels = [128] + LEVELS
        nl = len(levels)
        if who == "dve":
            def consume(i):
                eng.wait_ge(mm_done, i + 1)
                if i == 0:
                    eng.tensor_copy(off, bank[0][:, :]).then_inc(consumed, 1)
                    return
                mask = self.con("level_mask", (i - 1) * P, P).unsqueeze(1).to_broadcast([P, 4, P])
                for half in range(2):
                    src = bank[2 * (i % 2) + half][:, :].rearrange("p (n t) -> p n t", n=4)
                    dst = (diag if i == 1 else tmp)[:, 512 * half:512 * half + 512]
                    last = eng.tensor_tensor(dst.rearrange("p (n t) -> p n t", n=4), src, mask, ALU.mult)
                last.then_inc(consumed, 1)
                eng.wait_ge(consumed, i + 1)
                if i > 1:
                    self.link(eng, who, eng.tensor_tensor(diag, diag, tmp, ALU.add))

            exponents(128, Es[0]).then_inc(e_ready, 1)
            for i in range(nl):
                if i + 1 < nl:
                    if i:
                        eng.wait_ge(kq_ready, i)
                    exponents(levels[i + 1], Es[(i + 1) % 2]).then_inc(e_ready, 1)
                eng.wait_ge(x_ready, i + 1)
                if i:
                    eng.wait_ge(mm_done, i)
                eng.tensor_tensor(KL, K, Es[i % 2], ALU.mult)
                eng.tensor_tensor(QL, q, Es[i % 2], ALU.mult).then_inc(kq_ready, 1)
                if i:
                    consume(i - 1)
            consume(nl - 1)
            consume(nl)
        if who == "act":
            for i in range(nl):
                eng.wait_ge(e_ready, i + 1)
                eng.activation(Es[i % 2], Es[i % 2], ACT.Exp).then_inc(x_ready, 1)
        if who == "pe":
            for i in range(nl + 1):
                if i < nl:
                    eng.wait_ge(kq_ready, i + 1)
                if i > 1:
                    eng.wait_ge(consumed, i - 1)
                kk, qq = (KL, QL) if i < nl else (K, q)
                for h in range(HG):
                    if i == 0:
                        last = eng.matmul(bank[0][:, h * P:(h + 1) * P], kk[:, h * LAT:h * LAT + P],
                                          qq[:, h * LAT + P:(h + 1) * LAT], start=True, stop=True)
                        continue
                    for st in range(2):
                        c = slice(h * LAT + st * P, h * LAT + (st + 1) * P)
                        j = 2 * h + st
                        last = eng.matmul(bank[2 * (i % 2) + j // 4][:, (j % 4) * P:(j % 4 + 1) * P],
                                          kk[:, c], qq[:, c], start=True, stop=True)
                last.then_inc(mm_done, 1)
        self.phase_end(eng, who)
        if who == "pe":
            for h in range(HG):
                ob = bank[4 + h // 2][:, (h % 2) * LAT:(h % 2 + 1) * LAT]
                eng.matmul(ob[:, 0:P], vtok[:, 0, 2 + h, :], diag[:, 2 * h * P:(2 * h + 1) * P],
                           start=True, stop=True)
                self.mm(eng, ob[:, P:LAT], [vtok[:, 0, 2 + h, :], vtok[:, 1, 2 + h, :]],
                        [off[:, h * P:(h + 1) * P], diag[:, (2 * h + 1) * P:(2 * h + 2) * P]])
        self.phase_end(eng, who)
        small = QL[:, 0:LAT]
        if who == "act":
            for i in range(2):
                c = slice(512 * i, 512 * i + 512)
                eng.activation(KL[:, c], bank[4 + i][:, :], ACT.Square)
        self.phase_end(eng, who)
        if who == "pe":
            for j in range(HG):
                eng.matmul(bank[0][32 * j:32 * j + 32, 0:LAT], self.con("ones", 0, 32),
                           KL[:, j * LAT:(j + 1) * LAT], start=True, stop=True, skip_group_check=True)
        self.phase_end(eng, who)
        if who == "dve":
            eng.tensor_scalar(small, bank[0][:, 0:LAT], 1.0 / P, RMS_EPS, ALU.mult, ALU.add)
        self.phase_end(eng, who)
        if who == "act":
            eng.activation(small, small, ACT.Sqrt)
        self.phase_end(eng, who)
        if who == "dve":
            eng.reciprocal(small, small)
        if who == "act":
            for i in range(2):
                eng.copy(o[:, 512 * i:512 * i + 512], bank[4 + i][:, :])
        self.phase_end(eng, who)
        if who == "pe":
            for j in range(HG):
                eng.matmul(bank[2 + j // 2][:, (j % 2) * LAT:(j % 2 + 1) * LAT], self.con("spread", j * P, P),
                           small, start=True, stop=True)
        self.phase_end(eng, who)
        if who == "dve":
            for i in range(2):
                c = slice(512 * i, 512 * i + 512)
                last = eng.tensor_tensor(o[:, c], o[:, c], bank[2 + i][:, :], ALU.mult)
            self.link(eng, who, last)
            self.link(eng, who, eng.scalar_tensor_tensor(out=o, in0=o, scalar=self.vec("hg_norm"),
                                                         in1=self.tile2(T_HGATE, 4), op0=ALU.mult, op1=ALU.mult))
        self.phase_end(eng, who)

    def branches(self, who, eng):
        v = self.nsa_views()
        o = v["o"].rearrange("p (t d) -> p t d", t=2)
        oT = v["qr"].rearrange("p (k t) -> p k t", k=4)
        oh = v["o_hg"].rearrange("p (k t) -> p k t", k=4)
        self.flip(who, eng, lambda t, k: o[:, t, k * P:(k + 1) * P], lambda k: oT[:, k, :], 4, 2, "nsa")
        done, used = self.sem("branch_done"), self.sem("branch_used")
        bank = self.bank
        mixed = self.B[:, 0:KT * LAT].rearrange("p (k t) -> p k t", k=KT)
        tmp = self.X[:, 0:LAT]
        if who == "pe":
            g = FIRST["branch"]
            for s in range(2):
                eng.wait_ge(self.w_loaded[(g + s) % 2], 16 * ((g + s) // 2 + 1))
            for oc in range(KT):
                if oc >= 2:
                    eng.wait_ge(used, oc - 1)
                for s, r in enumerate((oT, oh)):
                    slot = self.ring[(g + s) % 2]
                    last = self.mm(eng, bank[2 * (oc % 2) + s][:, 0:LAT],
                                   [slot[:, (oc * 4 + k) * P:(oc * 4 + k + 1) * P] for k in range(4)],
                                   [r[:, k, :] for k in range(4)])
                last.then_inc(done, 1)
        if who == "dve":
            for oc in range(KT):
                eng.wait_ge(done, oc + 1)
                self.link(eng, who, eng.tensor_tensor(tmp, bank[2 * (oc % 2)][:, 0:LAT], self.tile2(T_MN + oc),
                                                      ALU.mult))
                eng.tensor_tensor(mixed[:, oc, :], bank[2 * (oc % 2) + 1][:, 0:LAT], self.tile2(T_MH + oc),
                                  ALU.mult).then_inc(used, 1)
                eng.wait_ge(used, oc + 1)
                self.link(eng, who, eng.tensor_tensor(mixed[:, oc, :], mixed[:, oc, :], tmp, ALU.add))
        self.phase_end(eng, who)
        self.project_residual(who, eng, "w_out", lambda k: mixed[:, k, :], KT, 4, None, 0, (1,))

    def router(self, who, eng):
        self.rms_to_input(who, eng, "ffn_norm")
        if who == "pe":
            for t in range(2):
                self.mm(eng, self.bank[0][:, t * 36:(t + 1) * 36],
                        [self.A[:, k, CTX + t * P:CTX + (t + 1) * P] for k in range(KT)],
                        [self.vec("w_route", k * 36, 36) for k in range(KT)])
        self.phase_end(eng, who)
        x = self.arena[:, FT * T - 512:FT * T]
        lg = x[:, 0:72].rearrange("p (t c) -> p t c", t=2)
        at = [72]

        def small(*shape):
            n = 2 * int(np.prod(shape)) if shape else 2
            r = x[:, at[0]:at[0] + n]
            at[0] += n
            return r.rearrange("p (t c) -> p t c", t=2)
        gm, ge, gs, gp = small(1), small(4), small(1), small(1)
        oneg, pref, pm = small(4), small(8), small(1)
        sel, ing = small(32), small(8)
        m1, o1, m2, o2, x2 = small(1), small(8), small(1), small(8), small(8)
        d, w1, w2 = small(1), small(1), small(1)
        comb = small(8)
        member, late, count = x[:, at[0]:at[0] + 64], x[:, at[0] + 64:at[0] + 128], x[:, at[0] + 128:at[0] + 129]
        C = self.S[:, 0:64].rearrange("p (t g c) -> p t g c", t=2, g=GROUPS)

        def L(ins):
            self.link(eng, who, ins)

        def one_hot(dst, src, m, first, n):
            pr = pref[:, :, 0:n]
            L(eng.tensor_tensor(dst, src, m.to_broadcast([P, 2, n]), ALU.is_equal))
            L(eng.tensor_tensor(pr, dst, self.con(first).unsqueeze(1).to_broadcast([P, 2, n]), ALU.mult))
            L(eng.tensor_reduce(pm, pr, AX.X, ALU.max))
            L(eng.tensor_tensor(dst, pr, pm.to_broadcast([P, 2, n]), ALU.is_equal))
        if who == "dve":
            br = self.vec("b_route").unsqueeze(1).to_broadcast([P, 2, 36])
            L(eng.tensor_tensor(lg, self.bank[0][:, 0:72].rearrange("p (t c) -> p t c", t=2), br, ALU.add))
            gl, el = lg[:, :, 0:4], lg[:, :, 4:36].rearrange("p t (g c) -> p t g c", g=GROUPS)
            L(eng.tensor_reduce(gm, gl, AX.X, ALU.max))
            L(eng.tensor_tensor(ge, gl, gm.to_broadcast([P, 2, 4]), ALU.subtract))
            one_hot(oneg, gl, gm, "first4", 4)
            s4 = sel.rearrange("p t (g c) -> p t g c", g=GROUPS)
            for t in range(2):
                L(eng.tensor_tensor(s4[:, t, :, :], el[:, t, :, :],
                                    oneg[:, t, :].unsqueeze(2).to_broadcast([P, 4, 8]), ALU.mult))
                L(eng.tensor_reduce(ing[:, t, :], s4[:, t, :, :].rearrange("p g c -> p c g"), AX.X, ALU.add))
            L(eng.tensor_reduce(m1, ing, AX.X, ALU.max))
            one_hot(o1, ing, m1, "first8", 8)
            L(eng.scalar_tensor_tensor(out=x2, in0=o1, scalar=-HUGE, in1=ing, op0=ALU.mult, op1=ALU.add))
            L(eng.tensor_reduce(m2, x2, AX.X, ALU.max))
            one_hot(o2, x2, m2, "first8", 8)
            L(eng.tensor_tensor(d, m2, m1, ALU.subtract))
        self.phase_end(eng, who)
        if who == "act":
            eng.activation(ge, ge, ACT.Exp)
            eng.activation(d, d, ACT.Exp)
        self.phase_end(eng, who)
        if who == "dve":
            L(eng.tensor_reduce(gs, ge, AX.X, ALU.add))
            L(eng.reciprocal(gp, gs))
            L(eng.tensor_scalar(w1, d, 1.0, None, ALU.add))
            L(eng.reciprocal(w1, w1))
            L(eng.tensor_tensor(w1, w1, gp, ALU.mult))
            L(eng.tensor_tensor(w2, w1, d, ALU.mult))
            L(eng.tensor_tensor(o1, o1, w1.to_broadcast([P, 2, 8]), ALU.mult))
            L(eng.tensor_tensor(o2, o2, w2.to_broadcast([P, 2, 8]), ALU.mult))
            L(eng.tensor_tensor(comb, o1, o2, ALU.add))
            for t in range(2):
                L(eng.tensor_tensor(C[:, t, :, :], comb[:, t, :].unsqueeze(1).to_broadcast([P, 4, 8]),
                                    oneg[:, t, :].unsqueeze(2).to_broadcast([P, 4, 8]), ALU.mult))
            eng.memset(self.rank(), -1.0)
            L(eng.tensor_scalar(member, self.S[:, 0:64], 0.0, None, ALU.not_equal))
        self.phase_end(eng, who)
        if who == "pe":
            eng.matmul(self.bank[0][:, 0:32], self.con("before"), member[:, 0:32], start=True, stop=True)
            self.mm(eng, self.bank[0][:, 32:64], [self.con("before"), self.con("ones")],
                    [member[:, 32:64], member[:, 0:32]])
        self.phase_end(eng, who)
        if who == "dve":
            r = self.rank()
            L(eng.scalar_tensor_tensor(out=late, in0=self.bank[0][:, 0:64], scalar=1.0, in1=member,
                                       op0=ALU.add, op1=ALU.mult))
            L(eng.tensor_scalar(r[:, :, 0:EXPERTS], late.rearrange("p (t c) -> p t c", t=2), -1.0, None, ALU.add))
            L(eng.tensor_scalar(late.rearrange("p (t c) -> p t c", t=2), r[:, :, 0:EXPERTS], float(SLOTS), None,
                                ALU.is_ge))
            eng.tensor_reduce(count, late, AX.X, ALU.add)
            eng.tensor_tensor(self.late_weights(), self.S[:, 0:64], late, ALU.mult)
        self.phase_end(eng, who)
        if who == "pe":
            eng.matmul(self.bank[0][0:1, 0:1], self.con("ones", 0, 1), count, start=True, stop=True)
            for t in range(2):
                for k in range(KT):
                    eng.transpose(self.bank[1 + 2 * t + k // 4][:, (k % 4) * P:(k % 4 + 1) * P],
                                  self.A[:, k, CTX + t * P:CTX + (t + 1) * P], self.con("ident"))
        self.phase_end(eng, who)
        m = self.moe_views()
        if who == "dve":
            eng.tensor_copy(self.overflow[:, :], self.bank[0][0:1, 0:1])
            for j in range(2):
                eng.tensor_copy(m["xt"][:, 512 * j:512 * j + 512], self.bank[1 + j][:, :])
            for n in ("zero", "gwt", "ya", "yb"):
                eng.memset(m[n], 0.0)
        if who == "act":
            for j in range(2, 4):
                eng.copy(m["xt"][:, 512 * j:512 * j + 512], self.bank[1 + j][:, :])
        self.phase_end(eng, who)

    def rank(self):
        return self.S[:, 64:64 + 2 * (EXPERTS + 2)].rearrange("p (t c) -> p t c", t=2)

    def late_weights(self):
        return self.S[:, 132:196]

    def moe_views(self):
        v, at = {}, 0
        for name, n in (("acc", 2 * D), ("xt", 2 * D), ("xe", KT * P), ("zero", 512), ("g", 2 * P),
                        ("gwa", 2 * P), ("gwb", 2 * P), ("gwt", 4 * P), ("sg", 256), ("hid", 256),
                        ("hidt", 256), ("ya", 512), ("yb", 512), ("late_sg", FET * LAT),
                        ("late_hid", FET * LAT)):
            v[name] = self.arena[:, at:at + n]
            at += n
        assert at <= FT * T - 512
        return v

    def moe(self, who, eng):
        v = self.moe_views()
        names = ("g_ready", "gw_ready", "gathered", "xe_act", "xe_dve", "gate_done", "up_done", "silu_done",
                 "hid_ready", "gwt_turned", "gwt_copied", "hid_turned", "hidt_copied", "down_done",
                 "y_copied")
        s = {n: self.sem("moe_" + n) for n in names}
        link = self.sem("moe_link")
        bank = self.bank
        slots, loaded = self.expert_slots(), self.expert_loaded()
        xt = v["xt"].rearrange("p (t d) -> p t d", t=2)
        xe = v["xe"].rearrange("p (k c) -> p k c", k=KT)
        gm, gwa, gwb = [v[n].rearrange("p (t e c) -> p t e c", t=2, e=2) for n in ("g", "gwa", "gwb")]
        gwt = v["gwt"].rearrange("p (n c) -> p n c", n=4)
        hidt = v["hidt"]
        C = self.S[:, 0:64].rearrange("p (t c) -> p t c", t=2)
        rank = self.rank()
        lo, hi = slice(0, 64), slice(64, 128)

        def gather(n):
            eng.wait_ge(s["g_ready"], n)
            for k in range(KT):
                last = self.mm(eng, bank[k // 4][:, (k % 4) * P:(k % 4 + 1) * P],
                               [xt[:, t, k * P:(k + 1) * P] for t in range(2)],
                               [gm[:, t, :, :].rearrange("p e c -> p (e c)") for t in range(2)])
            last.then_inc(s["gathered"], 1)

        def one_hots(pair):
            for t in range(2):
                ins = eng.tensor_tensor(gm[:, t, :, :], self.con("slot").unsqueeze(1).to_broadcast([P, 2, SLOTS]),
                                        rank[:, t, bass.ds(pair * 2, 2)].unsqueeze(2).to_broadcast([P, 2, SLOTS]),
                                        ALU.is_equal)
            ins.then_inc(s["g_ready"], 1)

        def project(x, e):
            for k in range(KT):
                for half in range(2):
                    o = (x * KT + k) * FE + half * 256
                    last = eng.matmul(bank[x][64 * half:64 * half + 64, 0:256], xe[:, k, 64 * e:64 * e + 64],
                                      slots[e][:, o:o + 256], start=(k == 0), stop=(k == KT - 1),
                                      skip_group_check=True)
            return last

        def turn_hidden():
            for c in range(2):
                last = eng.transpose(bank[3][:, c * P:(c + 1) * P], v["hid"][:, c * P:(c + 1) * P],
                                     self.con("ident"))
            last.then_inc(s["hid_turned"], 1)

        def down(e):
            for f in range(FET):
                for h in range(2):
                    grp = h if e == 0 else 1 - h
                    o = UPS + f * D + h * 512
                    at = (f % 2) * P + (f // 2) * 64
                    last = eng.matmul(bank[2][64 * grp:64 * grp + 64, :], hidt[:, at:at + 64],
                                      slots[e][:, o:o + 512], start=(f == 0), stop=(f == FET - 1),
                                      skip_group_check=True)
            last.then_inc(s["down_done"], 1)

        def scatter():
            for h, y in enumerate((v["ya"], v["yb"])):
                for t in range(2):
                    eng.matmul(bank[4 + 2 * t + h][:, :], gwt[:, 2 * h + t, :], y, start=False,
                               stop=False, skip_group_check=True)

        if who == "pe":
            for b in range(4, 8):
                eng.matmul(bank[b][:, :], v["zero"][:, 0:P], v["zero"], start=True, stop=False,
                           skip_group_check=True)
            eng.nop().then_inc(s["y_copied"], 1)
            gather(1)
            with eng.Fori(0, EXPERTS // 2) as i:
                x0 = i * 2
                eng.wait_ge(s["xe_act"], i + 1)
                eng.wait_ge(s["xe_dve"], i + 1)
                eng.wait_ge(loaded[0][0], i * 16 + 16)
                project(0, 0).then_inc(s["gate_done"], 1)
                eng.wait_ge(s["y_copied"], x0 + 1)
                scatter()
                eng.wait_ge(s["gw_ready"], i + 1)
                for n, w in enumerate((gwa, gwb)):
                    for t in range(2):
                        last = eng.transpose(bank[2][:, (2 * n + t) * P:(2 * n + t + 1) * P],
                                             w[:, t, :, :].rearrange("p e c -> p (e c)"), self.con("ident"))
                last.then_inc(s["gwt_turned"], 1)
                eng.wait_ge(loaded[0][1], i * 16 + 16)
                project(1, 0).then_inc(s["up_done"], 1)
                eng.wait_ge(s["silu_done"], x0 + 1)
                eng.wait_ge(loaded[1][0], i * 16 + 16)
                project(0, 1).then_inc(s["gate_done"], 1)
                eng.wait_ge(s["hid_ready"], x0 + 1)
                turn_hidden()
                eng.wait_ge(loaded[1][1], i * 16 + 16)
                project(1, 1).then_inc(s["up_done"], 1)
                eng.wait_ge(s["gwt_copied"], i + 1)
                eng.wait_ge(s["hidt_copied"], x0 + 1)
                eng.wait_ge(loaded[0][2], i * 16 + 16)
                down(0)
                eng.wait_ge(s["hid_ready"], x0 + 2)
                gather(i + 2)
                turn_hidden()
                eng.wait_ge(s["y_copied"], x0 + 2)
                eng.wait_ge(s["hidt_copied"], x0 + 2)
                eng.wait_ge(loaded[1][2], i * 16 + 16)
                down(1)
            eng.wait_ge(s["y_copied"], EXPERTS + 1)
            scatter()
            for b in range(4, 8):
                eng.matmul(bank[b][:, :], v["zero"][:, 0:P], v["zero"], start=False, stop=True,
                           skip_group_check=True)
        if who == "act":
            def copy_xe(n):
                eng.wait_ge(s["gathered"], n)
                eng.copy(v["xe"][:, 0:512], bank[0][:, :]).then_inc(s["xe_act"], 1)
            copy_xe(1)
            with eng.Fori(0, EXPERTS // 2) as i:
                for e in range(2):
                    eng.wait_ge(s["gate_done"], i * 2 + e + 1)
                    if e == 1:
                        eng.wait_ge(s["hid_ready"], i * 2 + 1)
                    eng.activation(v["sg"], bank[0][:, 0:256], ACT.Silu).then_inc(s["silu_done"], 1)
                copy_xe(i + 2)
        if who == "dve":
            def copy_xe(n):
                eng.wait_ge(s["gathered"], n)
                eng.tensor_copy(v["xe"][:, 512:1024], bank[1][:, :]).then_inc(s["xe_dve"], 1)

            def hidden(x):
                eng.wait_ge(s["silu_done"], x + 1)
                eng.wait_ge(s["up_done"], x + 1)
                eng.tensor_tensor(v["hid"], v["sg"], bank[1][:, 0:256], ALU.mult).then_inc(s["hid_ready"], 1)

            def copy_hidden(x):
                eng.wait_ge(s["hid_turned"], x + 1)
                eng.tensor_copy(v["hidt"], bank[3][:, 0:256]).then_inc(s["hidt_copied"], 1)

            def copy_rows(x, a, b):
                eng.wait_ge(s["down_done"], x + 1)
                eng.tensor_copy(v["ya"][a, :], bank[2][a, :])
                eng.tensor_copy(v["yb"][b, :], bank[2][b, :]).then_inc(s["y_copied"], 1)
            one_hots(0)
            copy_xe(1)
            with eng.Fori(0, EXPERTS // 2) as i:
                x0 = i * 2
                for t in range(2):
                    last = eng.tensor_tensor(gwa[:, t, :, :], gm[:, t, :, :],
                                             C[:, t, bass.ds(i * 2, 2)].unsqueeze(2)
                                             .to_broadcast([P, 2, SLOTS]), ALU.mult)
                last.then_inc(link, 1)
                eng.wait_ge(link, i + 1)
                eng.tensor_copy(gwb[:, :, 0, :], gwa[:, :, 1, :])
                eng.tensor_copy(gwb[:, :, 1, :], gwa[:, :, 0, :]).then_inc(s["gw_ready"], 1)
                one_hots(i + 1)
                eng.wait_ge(s["gwt_turned"], i + 1)
                eng.tensor_copy(v["gwt"], bank[2][:, :]).then_inc(s["gwt_copied"], 1)
                hidden(x0)
                copy_hidden(x0)
                hidden(x0 + 1)
                copy_rows(x0, lo, hi)
                copy_xe(i + 2)
                copy_hidden(x0 + 1)
                copy_rows(x0 + 1, hi, lo)
        self.phase_end(eng, who)
        if who == "dve":
            for t in range(2):
                for h in range(2):
                    eng.tensor_copy(v["acc"][:, t * D + h * 512:t * D + h * 512 + 512], bank[4 + 2 * t + h][:, :])
        self.phase_end(eng, who)
        self.flag_phase = 3 * self.phases[who]
        n = eng.value_load(self.overflow[0:1, 0:1])
        with eng.If(n != 0):
            self.late(who, eng)
        self.phase_end(eng, who)

    def late(self, who, eng):
        names = ("up_done", "silu_done", "hid_done", "down_done", "acc_used")
        up_done, silu_done, hid_done, down_done, acc_used = [self.sem("late_" + x) for x in names]
        loaded = self.sem("late_loaded")
        v = self.moe_views()
        bank = self.bank
        slot = self.expert_slots()[0]
        if who == "sp":
            with eng.Fori(0, EXPERTS) as e:
                eng.wait_ge(self.sem("late_free"), e + 1)
                eng.dma_start(slot, self.W["moe"][e]).then_inc(loaded, 16)
            return
        acc = v["acc"].rearrange("p (t h d) -> p t h d", t=2, h=2)
        sg = v["late_sg"].rearrange("p (f t) -> p f t", f=FET)
        hid = v["late_hid"].rearrange("p (f t) -> p f t", f=FET)
        C = self.late_weights().rearrange("p (t c) -> p t c", t=2)
        if who == "dve":
            eng.nop().then_inc(acc_used, 4)
        if who == "pe":
            eng.nop().then_inc(self.sem("late_free"), 1)
        with eng.Fori(0, EXPERTS) as e:
            if who == "pe":
                eng.wait_ge(loaded, e * 16 + 16)

                def up(x, f, k, w):
                    return eng.matmul(bank[f][:, x * LAT:(x + 1) * LAT], w[:, f * P:(f + 1) * P],
                                      self.A[:, k, CTX:T], start=(k == 0), stop=(k == KT - 1))
                for x in range(2):
                    for f in range(FET):
                        for k in range(KT):
                            c = x * KT + k
                            w = slot[:, c * FE:(c + 1) * FE]
                            last = up(x, f, k, w)
                        if x:
                            last.then_inc(up_done, 1)
                eng.wait_ge(acc_used, e * 4 + 4)
                for f in range(FET):
                    eng.wait_ge(hid_done, e * 4 + f + 1)
                for t in range(2):
                    for h in range(2):
                        for f in range(FET):
                            o = UPS + f * D + h * 512
                            last = eng.matmul(bank[4 + 2 * t + h][:, :], hid[:, f, t * P:(t + 1) * P],
                                              slot[:, o:o + 512], start=(f == 0), stop=(f == FET - 1))
                        last.then_inc(down_done, 1)
                eng.drain().then_inc(self.sem("late_free"), 1)
            if who == "act":
                for f in range(FET):
                    eng.wait_ge(up_done, e * 4 + f + 1)
                    eng.activation(sg[:, f, :], bank[f][:, 0:LAT], ACT.Silu).then_inc(silu_done, 1)
            if who == "dve":
                for f in range(FET):
                    eng.wait_ge(silu_done, e * 4 + f + 1)
                    eng.tensor_tensor(hid[:, f, :], sg[:, f, :], bank[f][:, LAT:2 * LAT], ALU.mult)\
                        .then_inc(hid_done, 1)
                for t in range(2):
                    c = C[:, t, bass.ds(e, 1)]
                    for h in range(2):
                        eng.wait_ge(down_done, e * 4 + 2 * t + h + 1)
                        eng.scalar_tensor_tensor(out=acc[:, t, h, :], in0=bank[4 + 2 * t + h][:, :], scalar=c,
                                                 in1=acc[:, t, h, :], op0=ALU.mult, op1=ALU.add)\
                            .then_inc(acc_used, 1)
        if who == "dve":
            eng.wait_ge(acc_used, 4 * EXPERTS + 4)

    def result(self):
        return self.moe_views()["acc"].rearrange("p (t d) -> p t d", t=2)

    def final(self, who, eng):
        acc = self.result()
        bank = self.bank
        if who == "pe":
            for t in range(2):
                for k in range(KT):
                    eng.transpose(bank[t * 2 + k // 4][:, (k % 4) * P:(k % 4 + 1) * P],
                                  self.H[:, k, CTX + t * P:CTX + (t + 1) * P], self.con("ident"))
        self.phase_end(eng, who)
        ss = self.S[:, 128:130]
        if who == "dve":
            for t in range(2):
                for h in range(2):
                    c = acc[:, t, 512 * h:512 * h + 512]
                    eng.tensor_tensor(c, c, bank[t * 2 + h][:, :], ALU.add)
        self.phase_end(eng, who)
        if who == "act":
            for t in range(2):
                eng.activation(self.X[:, t * D:(t + 1) * D], acc[:, t, :], ACT.Square,
                               accum_out=ss[:, t:t + 1])
        self.phase_end(eng, who)
        if who == "dve":
            eng.tensor_scalar(ss, ss, 1.0 / D, RMS_EPS, ALU.mult, ALU.add)
        self.phase_end(eng, who)
        if who == "act":
            eng.activation(ss, ss, ACT.Sqrt)
        self.phase_end(eng, who)
        if who == "dve":
            self.link(eng, who, eng.reciprocal(ss, ss))
            for t in range(2):
                last = eng.scalar_tensor_tensor(out=acc[:, t, :], in0=acc[:, t, :], scalar=ss[:, t:t + 1],
                                                in1=self.vec("final_norm"), op0=ALU.mult, op1=ALU.mult)
                self.link(eng, who, last)
            eng.nop().then_inc(self.sem("result_ready"), 1)


def constants():
    c = {}
    i = np.arange(P)
    c["ident"] = np.eye(P)
    c["ones"] = np.ones((P, P))
    c["mean"] = np.full((P, P), 1.0 / D)

    def rotation(base, half, n):
        r = np.zeros((P, n))
        for j in range(half):
            for at in base:
                r[at + half + j, at + j] = -1.0
                r[at + j, at + half + j] = 1.0
        return r
    tok = np.arange(LAT)
    nf = DR // 4
    inv = (10000.0 ** (-np.arange(nf, dtype=np.float32) / np.float32(nf))).astype(np.float32)
    row, col = (tok // GRID_W).astype(np.float32), (tok % GRID_W).astype(np.float32)
    ang = np.concatenate([row[:, None] * inv, col[:, None] * inv], -1).T.astype(np.float32)
    cos, sin = np.ones((P, LAT)), np.zeros((P, LAT))
    for h in range(2):
        cos[DN + 16 * h:DN + 16 * h + 16] = np.cos(ang)
        sin[DN + 16 * h:DN + 16 * h + 16] = np.sin(ang)
    c["rot_mla"], c["cos_mla"], c["sin_mla"] = rotation([DN], DR // 2, QK), cos, sin
    inv = (500000.0 ** (-np.arange(8, dtype=np.float32) / np.float32(8))).astype(np.float32)
    ang = (tok.astype(np.float32)[:, None] * inv).T.astype(np.float32)
    cos, sin = np.ones((P, LAT)), np.zeros((P, LAT))
    for at in (0, 8, 64, 72):
        cos[at:at + 8], sin[at:at + 8] = np.cos(ang), np.sin(ang)
    c["rot_nsa"], c["cos_nsa"], c["sin_nsa"] = rotation([0, 64], 8, P), cos, sin
    qc, kc = i % GRID_W, np.arange(LAT) % GRID_W
    start = np.clip(qc - 8, 0, GRID_W - 16)
    ok = (kc[None, :] >= start[:, None]) & (kc[None, :] < start[:, None] + 16)
    c["na_mask"] = np.where(ok, 0.0, NEG)
    m = np.full((P, 416), NEG)
    tri = np.where(i[None, :] <= i[:, None], 0.0, NEG)
    m[:, 0:128] = tri
    m[:, 128:256] = 0.0
    m[:, 256:384] = tri
    keep = np.zeros((P, 32))
    for t in range(2):
        n = np.arange(16)
        ok = (16 * n + 31)[None, :] <= (i + P * t)[:, None]
        ok &= (n < NCMP)[None, :]
        m[:, 384 + 16 * t:400 + 16 * t] = np.where(ok, 0.0, NEG)
        keep[:, 16 * t:16 * t + 16] = ok
    c["nsa_mask"], c["cmp_keep"] = m, keep
    s, t = i[:, None], i[None, :]
    masks = [(s // (2 * v) == t // (2 * v)) & (s // v % 2 == 0) & (t // v % 2 == 1) for v in LEVELS]
    c["level_mask"] = np.concatenate(masks + [s == t], 1)
    c["scan_keep"] = np.broadcast_to((tok % 64 != 0), (P, LAT))
    c["cmp_fold"] = (i[:, None] % 32 == np.arange(16)) & (np.arange(16) < NCMP)
    c["spread"] = np.repeat(i[:, None] == 32 * np.arange(4), P, 1)
    c["fold"] = i[:, None] % 32 == np.arange(2)
    c["before"] = i[:, None] < i[None, :]
    c["slot"] = np.broadcast_to(np.arange(SLOTS), (P, SLOTS))
    c["first4"] = np.broadcast_to(4.0 - np.arange(4), (P, 4))
    c["first8"] = np.broadcast_to(8.0 - np.arange(8), (P, 8))
    out = np.zeros((P, NCONST), np.float32)
    for n, w in CONSTS:
        out[:, COFF[n][0]:COFF[n][0] + w] = c[n]
    return out


def tiled(w, tiles_per_chunk):
    k, n = w.shape
    w = w.reshape(k // P, P, n // P // tiles_per_chunk, tiles_per_chunk, P)
    return np.ascontiguousarray(w.transpose(2, 1, 3, 0, 4)).reshape(w.shape[2], P, -1)


def columns(v):
    return np.asarray(v).reshape(-1, P).T


def lay_out(a):
    W = {}
    w = np.concatenate([a["ada_w"][i] for i in range(DEPTH)], 1).reshape(KT, P, -1)
    n = ADA_FIRST * P
    W["ada"] = w[:, :, :n].reshape(KT, P, 4, 512).transpose(2, 1, 0, 3).reshape(4, P, -1)
    ada = w[:, :, n:].reshape(KT, P, MLA_H, ADA_TILES * P).transpose(2, 1, 0, 3).reshape(MLA_H, P, -1)
    w = a["mla_w_in"][0]
    pe = np.zeros((D, QK), np.float32)
    pe[:, DN:] = w[:, QL + KVL:]
    W["mla_in"] = np.concatenate(
        [tiled(w[:, :QL + KVL], 5)[0], pe.reshape(KT, P, QK).transpose(1, 0, 2).reshape(P, -1)], 1)[None]
    q = a["mla_w_qb"][0].reshape(QLT, P, MLA_H, QK).transpose(2, 1, 0, 3).reshape(MLA_H, P, -1)
    kv = a["mla_w_kvb"][0].reshape(KVT, P, MLA_H, 2, DN)
    W["mla_v"] = kv[:, :, :, 1].transpose(1, 0, 2, 3).reshape(1, P, -1)
    kv = kv[:, :, :, 0].transpose(2, 1, 0, 3).reshape(MLA_H, P, -1)
    W["mla_head"] = np.concatenate([q, kv, ada], 2)
    W["mla_o"] = tiled(a["mla_w_o"][0], 4)
    for i in range(DEPTH):
        u = a["ffn_w_in"][i].reshape(KT, P, 2, FT // 2, 2, P)
        W[f"ffn_in{i}"] = u.transpose(3, 1, 2, 4, 0, 5).reshape(FT // 2, P, -1)
        W[f"ffn_out{i}"] = tiled(a["ffn_w_out"][i], 2)
    W["na_pair"] = a["na_w_qkv"][0].reshape(KT, P, 3, NA_PAIRS, P).transpose(3, 1, 2, 0, 4)\
        .reshape(NA_PAIRS, P, -1)
    W["na_o"] = tiled(a["na_w_o"][0], 4)
    w = a["w_in_2"][0]
    q = w[:, :512].reshape(D, 2, 4, 64).transpose(0, 2, 1, 3).reshape(D, 512)
    W["proj"] = tiled(np.concatenate([q, w[:, 512:1280], w[:, 1304:]], 1), 6)
    cmp = np.zeros((2, P, 32, P), np.float32)
    for x, n in enumerate(("w_cmp_k_2", "w_cmp_v_2")):
        c = a[n][0].reshape(32, 64, 64).transpose(1, 0, 2)
        cmp[x, 0:64, :, 0:64] = c
        cmp[x, 64:128, :, 64:128] = c
    W["cmp"] = cmp.reshape(2, P, -1)
    W["branch"] = np.concatenate([tiled(a["w_br_nsa_2"][0], 8), tiled(a["w_br_hg_2"][0], 8)])
    W["w_out"] = tiled(a["w_out_2"][0], 4)
    g, u = [a[n][0].reshape(EXPERTS, KT, P, FE).transpose(0, 2, 1, 3).reshape(EXPERTS, P, -1)
            for n in ("w_gate_2", "w_up_2")]
    dn = a["w_down_2"][0].reshape(EXPERTS, FET, P, D).transpose(0, 2, 1, 3).reshape(EXPERTS, P, -1)
    W["moe"] = np.concatenate([g, u, dn], 2)

    v = {}
    v["cvec"] = np.stack([columns(a["c_ctx"]), columns(a["c"][0])], 2).reshape(P, -1)
    for n in ("ada_b", "ln1_g", "ln1_b", "ln2_g", "ln2_b"):
        v[n] = columns(a[n])
    v["conv_w"], v["conv_b"] = columns(a["ffn_conv_w"]), columns(a["ffn_conv_b"])
    v["q_norm"], v["kv_norm"] = columns(a["mla_q_norm"]), columns(a["mla_kv_norm"])
    v["attn_norm"], v["ffn_norm"] = columns(a["attn_norm_2"]), columns(a["ffn_norm_2"])
    v["hg_lb"], v["hg_norm"] = columns(a["hg_lb_logits_2"]), columns(a["hg_norm_2"])
    v["cmp_pos"] = np.concatenate([a["cmp_pos_2"][0].T] * 2)
    w = a["w_in_2"][0][:, 1280:1304].reshape(KT, P, 2, 4, 3)[..., [1, 0, 2]]
    v["w_gate24"] = w.transpose(1, 0, 3, 2, 4).reshape(P, -1)
    w = np.concatenate([a["w_grp_2"][0], a["w_rtr_2"][0]], 1)
    v["w_route"] = w.reshape(KT, P, 36).transpose(1, 0, 2).reshape(P, -1)
    v["b_route"] = np.broadcast_to(np.concatenate([a["b_grp_2"][0], a["b_rtr_2"][0]]), (P, 36))
    v["final_norm"] = np.broadcast_to(a["final_norm_2"], (P, D))
    vec = np.zeros((P, NVEC), np.float32)
    for n, wd in VECS:
        vec[:, VOFF[n][0]:VOFF[n][0] + wd] = v[n]

    xT = np.concatenate([a["ctx"][0], a["x"][0]]).T.reshape(KT, P, T).transpose(1, 0, 2)
    r = a["na_rpb"][0]
    wide = np.zeros((16, 7, 2 * GRID_W - 1), np.float32)
    wide[:, :, 48:79] = r[:, 4:11, :]
    nab = np.empty((4, GRID_W, 16, 4, GRID_W), np.float32)
    for qr in range(4):
        for qc in range(GRID_W):
            nab[qr, qc] = wide[:, 3 - qr:7 - qr, 63 - qc:127 - qc]
    return W, vec, np.ascontiguousarray(xT), nab.reshape(4, GRID_W, 16, LAT)


def kernel(**inputs):
    import concourse.bacc as _bacc
    from concourse.bass_utils import run_bass_kernel_spmd as _run

    weights, vectors, x_t, na_bias = lay_out({k: np.asarray(v) for k, v in inputs.items()})
    nc = _bacc.Bacc("TRN2", target_bir_lowering=False, num_devices=1)
    arrays = {"in_vectors": vectors, "in_constants": constants(), "in_x_t": x_t, "in_na_bias": na_bias}
    arrays |= {"w_" + n: weights[n] for n, _, _ in STREAM}
    arrays = {n: np.ascontiguousarray(v) for n, v in arrays.items()}
    d = {n: nc.dram_tensor(n, v.shape, F32, kind="ExternalInput").ap() for n, v in arrays.items()}
    out = nc.dram_tensor("out", (1, LAT, D), F32, kind="ExternalOutput").ap()
    program = Kernel(nc, {n: d["w_" + n] for n, _, _ in STREAM}, d["in_vectors"], d["in_constants"],
                     d["in_x_t"], d["in_na_bias"], out)
    program.build()
    r = _run(nc, [arrays], core_ids=[0])
    return r.results[0]["out"]
```
